# Optimizing a Trainium2 kernel written in Bass

```python
import jax, jax.numpy as jnp
from jax import lax
import numpy as np

D_MODEL = 1024
BATCH = 1
SEQ = 1024
DEPTH = 1
DEC_BATCH = 8
DEC_SEQ = 16
PAST_LEN = 256

CHUNK = 64
BAND_CHUNKS = 8
WINDOW_A = BAND_CHUNKS * CHUNK
N_HEADS_A = 8
HEAD_DIM_A = 64
W_A = N_HEADS_A * HEAD_DIM_A
REL_CLIP = 128
N_HEADS_B = 4
DK_B = 128
DV_B = 256
QK_B = N_HEADS_B * DK_B
V_B = N_HEADS_B * DV_B
ROPE_BASE = 10000.0
N_GROUPS = 4
EXPERTS_PER_GROUP = 8
N_EXPERTS = N_GROUPS * EXPERTS_PER_GROUP
TOP_K = 2
D_EXPERT = 512
D_PLE = 256
EPS = 1e-6
_IN_SIZES = (W_A, W_A, W_A, QK_B, QK_B, V_B, V_B, D_MODEL, D_MODEL)
IN_WIDTH = sum(_IN_SIZES)
_IN_CUTS = [int(c) for c in np.cumsum(_IN_SIZES)[:-1]]

kernel_name = "hybrid_chunkband_retention_hmoe_stream_step"

F32 = jnp.float32

def rmsnorm(x, g):
    xf = x.astype(F32)
    y = xf * lax.rsqrt(jnp.mean(xf * xf, axis=-1, keepdims=True) + EPS)
    return (y * g.astype(F32)).astype(x.dtype)

def rope(x, pos):
    half = x.shape[-1] // 2
    freqs = ROPE_BASE ** (-jnp.arange(half, dtype=F32) / half)
    ang = pos.astype(F32)[:, None] * freqs[None, :]
    cos = jnp.cos(ang)[:, None, :]
    sin = jnp.sin(ang)[:, None, :]
    xf = x.astype(F32)
    x1, x2 = xf[..., :half], xf[..., half:]
    return jnp.concatenate([x1 * cos - x2 * sin, x2 * cos + x1 * sin], axis=-1).astype(x.dtype)

def rel_bias_block(table, n_q, n_k, offset):
    dist = jnp.arange(n_q)[:, None] + offset - jnp.arange(n_k)[None, :]
    idx = jnp.clip(dist, -REL_CLIP, REL_CLIP) + REL_CLIP
    return table[:, idx].astype(F32)

def attend(q, k, v, bias, valid=None):
    s = jnp.einsum('bqhd,bkhd->bhqk', q, k).astype(F32) * (HEAD_DIM_A ** -0.5) + bias[None]
    if valid is not None:
        s = jnp.where(valid[None, None, None, :], s, jnp.float32(-1e30))
    p = jax.nn.softmax(s, axis=-1)
    return jnp.einsum('bhqk,bkhd->bqhd', p.astype(v.dtype), v)

def band_attention_prompt(q, k, v, table):
    B, S, H, hd = q.shape
    nc = S // CHUNK
    band = WINDOW_A + CHUNK
    pad = ((0, 0), (WINDOW_A, 0), (0, 0), (0, 0))
    kp = jnp.pad(k, pad)
    vp = jnp.pad(v, pad)
    qc = q.reshape(B, nc, CHUNK, H, hd).transpose(1, 0, 2, 3, 4)
    bias = rel_bias_block(table, CHUNK, band, WINDOW_A)
    key_idx = jnp.arange(band)

    def one_chunk(args):
        c, qb = args
        kb = lax.dynamic_slice_in_dim(kp, c * CHUNK, band, axis=1)
        vb = lax.dynamic_slice_in_dim(vp, c * CHUNK, band, axis=1)
        valid = key_idx >= (BAND_CHUNKS - c) * CHUNK
        return attend(qb, kb, vb, bias, valid)

    out = lax.map(one_chunk, (jnp.arange(nc), qc))
    return out.transpose(1, 0, 2, 3, 4).reshape(B, S, H, hd)

def band_attention_sample(q, k, v, cache_k, cache_v, table):
    L = cache_k.shape[1]
    n = q.shape[1]
    k_all = jnp.concatenate([cache_k.astype(k.dtype), k], axis=1)
    v_all = jnp.concatenate([cache_v.astype(v.dtype), v], axis=1)
    bias = rel_bias_block(table, n, L + n, L)
    return attend(q, k_all, v_all, bias)

def retention_block(q, k, v, state, log_g):
    T = q.shape[1]
    idx = jnp.arange(T, dtype=F32)
    diff = idx[:, None] - idx[None, :]
    dmask = jnp.where(diff[None] >= 0, jnp.exp(log_g[:, None, None] * jnp.maximum(diff, 0.0)[None]), 0.0)
    scores = jnp.einsum('bihd,bjhd->bhij', q, k) * dmask[None]
    o = jnp.einsum('bhij,bjhe->bihe', scores, v)
    q_decay = jnp.exp(log_g[None, :] * (idx[:, None] + 1.0))
    o = o + jnp.einsum('bihd,bhde->bihe', q, state) * q_decay[None, :, :, None]
    k_decay = jnp.exp(log_g[None, :] * (T - 1.0 - idx[:, None]))
    new_state = state * jnp.exp(log_g * T)[None, :, None, None] + jnp.einsum(
        'bjhd,bjhe->bhde', k * k_decay[None, :, :, None], v)
    return o, new_state

def retention_prompt(q, k, v, log_g):
    B, S, H, dk = q.shape
    nc = S // CHUNK

    def to_chunks(t):
        return t.astype(F32).reshape(B, nc, CHUNK, H, t.shape[-1]).transpose(1, 0, 2, 3, 4)

    def step(s, qkv):
        o, s = retention_block(qkv[0], qkv[1], qkv[2], s, log_g)
        return s, o

    s0 = jnp.zeros((B, H, dk, DV_B), F32)
    s_final, o = lax.scan(step, s0, (to_chunks(q), to_chunks(k), to_chunks(v)))
    return o.transpose(1, 0, 2, 3, 4).reshape(B, S, H, DV_B), s_final

def project_in(x, g_norm, w_in, pos):
    B, S, _ = x.shape
    h = rmsnorm(x, g_norm)
    z = h @ w_in
    qa, ka, va, qb, kb, vb, gb, gate_a, gate_b = jnp.split(z, _IN_CUTS, axis=-1)
    qa = qa.reshape(B, S, N_HEADS_A, HEAD_DIM_A)
    ka = ka.reshape(B, S, N_HEADS_A, HEAD_DIM_A)
    va = va.reshape(B, S, N_HEADS_A, HEAD_DIM_A)
    qb = rope(qb.reshape(B, S, N_HEADS_B, DK_B), pos)
    kb = rope(kb.reshape(B, S, N_HEADS_B, DK_B), pos) * (DK_B ** -0.5)
    vb = vb.reshape(B, S, N_HEADS_B, DV_B)
    return qa, ka, va, qb, kb, vb, gb, gate_a, gate_b

def merge_out(att_a, ret_b, gb, gate_a, gate_b, ret_norm_g, w_proj_a, w_proj_b, w_out, dtype):
    B, S = att_a.shape[:2]
    a = att_a.reshape(B, S, W_A) @ w_proj_a
    mu = jnp.mean(ret_b, axis=-1, keepdims=True)
    var = jnp.mean(jnp.square(ret_b - mu), axis=-1, keepdims=True)
    rb = ((ret_b - mu) * lax.rsqrt(var + EPS)).reshape(B, S, V_B) * ret_norm_g.astype(F32)
    b = (jax.nn.silu(gb) * rb.astype(dtype)) @ w_proj_b
    m = jax.nn.sigmoid(gate_a) * a + jax.nn.sigmoid(gate_b) * b
    return m @ w_out

def hier_moe(h, w_rg, b_rg, w_re, b_re, w_gate, w_up, w_down):
    N = h.shape[0]
    rows = jnp.arange(N)
    lg = (h @ w_rg).astype(F32) + b_rg.astype(F32)
    grp = jnp.argmax(lg, axis=-1)
    p_grp = jax.nn.softmax(lg, axis=-1)[rows, grp]
    le = ((h @ w_re).astype(F32) + b_re.astype(F32)).reshape(N, N_GROUPS, EXPERTS_PER_GROUP)
    top_l, top_i = lax.top_k(le[rows, grp], TOP_K)
    wts = jax.nn.softmax(top_l, axis=-1) * p_grp[:, None]
    flat_e = (grp[:, None] * EXPERTS_PER_GROUP + top_i).reshape(-1)
    order = jnp.argsort(flat_e)
    tok = order // TOP_K
    xs = h[tok]
    sizes = jnp.bincount(flat_e, length=N_EXPERTS).astype(jnp.int32)
    g = lax.ragged_dot(xs, w_gate, sizes)
    u = lax.ragged_dot(xs, w_up, sizes)
    y = lax.ragged_dot(jax.nn.silu(g) * u, w_down, sizes)
    y = y * wts.reshape(-1)[order][:, None].astype(y.dtype)
    return jnp.zeros_like(h).at[tok].add(y)

def channel_and_ple(x, p, g_ffn, w_rg, b_rg, w_re, b_re, w_gate, w_up, w_down,
                    g_ple, w_ple_gate, w_ple_proj):
    B, S, D = x.shape
    h = rmsnorm(x, g_ffn).reshape(B * S, D)
    x = x + hier_moe(h, w_rg, b_rg, w_re, b_re, w_gate, w_up, w_down).reshape(B, S, D)
    e = (p.astype(x.dtype) @ w_ple_proj) * jax.nn.sigmoid(rmsnorm(x, g_ple) @ w_ple_gate)
    return x + e

def setup_inputs(seed: int = 0) -> dict:
    key = jax.random.key(seed)
    ks = jax.random.split(key, 32)
    n = lambda k, s, sc: jax.random.normal(k, s, F32) * sc
    L_A = min(WINDOW_A, PAST_LEN)
    return {
        "x_prompt": n(ks[0], (BATCH, SEQ, D_MODEL), 1.0),
        "x_sample": n(ks[1], (DEC_BATCH, DEC_SEQ, D_MODEL), 1.0),
        "cache_k_a": n(ks[2], (DEPTH, DEC_BATCH, L_A, N_HEADS_A, HEAD_DIM_A), 1.0),
        "cache_v_a": n(ks[3], (DEPTH, DEC_BATCH, L_A, N_HEADS_A, HEAD_DIM_A), 1.0),
        "state_ret": n(ks[4], (DEPTH, DEC_BATCH, N_HEADS_B, DK_B, DV_B), 0.3),
        "p_prompt": n(ks[5], (DEPTH, BATCH, SEQ, D_PLE), 1.0),
        "p_sample": n(ks[6], (DEPTH, DEC_BATCH, DEC_SEQ, D_PLE), 1.0),
        "norm_mix_g": 1.0 + n(ks[7], (DEPTH, D_MODEL), 0.01),
        "w_in": n(ks[8], (DEPTH, D_MODEL, IN_WIDTH), D_MODEL ** -0.5),
        "rel_bias": n(ks[9], (DEPTH, N_HEADS_A, 2 * REL_CLIP + 1), 0.1),
        "ret_norm_g": 1.0 + n(ks[10], (DEPTH, V_B), 0.01),
        "w_proj_a": n(ks[11], (DEPTH, W_A, D_MODEL), W_A ** -0.5),
        "w_proj_b": n(ks[12], (DEPTH, V_B, D_MODEL), V_B ** -0.5),
        "w_out": n(ks[13], (DEPTH, D_MODEL, D_MODEL), D_MODEL ** -0.5),
        "norm_ffn_g": 1.0 + n(ks[14], (DEPTH, D_MODEL), 0.01),
        "w_router_group": n(ks[15], (DEPTH, D_MODEL, N_GROUPS), D_MODEL ** -0.5),
        "b_router_group": n(ks[16], (DEPTH, N_GROUPS), 0.01),
        "w_router_expert": n(ks[17], (DEPTH, D_MODEL, N_EXPERTS), D_MODEL ** -0.5),
        "b_router_expert": n(ks[18], (DEPTH, N_EXPERTS), 0.01),
        "w_gate_e": n(ks[19], (DEPTH, N_EXPERTS, D_MODEL, D_EXPERT), D_MODEL ** -0.5),
        "w_up_e": n(ks[20], (DEPTH, N_EXPERTS, D_MODEL, D_EXPERT), D_MODEL ** -0.5),
        "w_down_e": n(ks[21], (DEPTH, N_EXPERTS, D_EXPERT, D_MODEL), D_EXPERT ** -0.5),
        "norm_ple_g": 1.0 + n(ks[22], (DEPTH, D_MODEL), 0.01),
        "w_ple_gate": n(ks[23], (DEPTH, D_MODEL, D_MODEL), D_MODEL ** -0.5),
        "w_ple_proj": n(ks[24], (DEPTH, D_PLE, D_MODEL), D_PLE ** -0.5),
        "final_norm_g": 1.0 + n(ks[25], (D_MODEL,), 0.01),
    }

def reference(x_prompt, x_sample, cache_k_a, cache_v_a, state_ret, p_prompt, p_sample,
              norm_mix_g, w_in, rel_bias, ret_norm_g, w_proj_a, w_proj_b, w_out,
              norm_ffn_g, w_router_group, b_router_group, w_router_expert, b_router_expert,
              w_gate_e, w_up_e, w_down_e, norm_ple_g, w_ple_gate, w_ple_proj, final_norm_g):
    S_p = x_prompt.shape[1]
    S_s = x_sample.shape[1]
    pos_p = jnp.arange(S_p)
    pos_s = PAST_LEN + jnp.arange(S_s)
    log_g = jnp.log(1.0 - 2.0 ** (-5.0 - jnp.arange(N_HEADS_B, dtype=F32)))
    keep = min(WINDOW_A, S_p)
    xp, xs = x_prompt, x_sample
    kp_l, vp_l, sp_l, ks_l, vs_l, ss_l = [], [], [], [], [], []
    for i in range(DEPTH):
        qa, ka, va, qb, kb, vb, gb, ga, gbt = project_in(xp, norm_mix_g[i], w_in[i], pos_p)
        att = band_attention_prompt(qa, ka, va, rel_bias[i])
        ret, s_new = retention_prompt(qb, kb, vb, log_g)
        xp = xp + merge_out(att, ret, gb, ga, gbt, ret_norm_g[i], w_proj_a[i], w_proj_b[i],
                            w_out[i], xp.dtype)
        xp = channel_and_ple(xp, p_prompt[i], norm_ffn_g[i], w_router_group[i], b_router_group[i],
                             w_router_expert[i], b_router_expert[i], w_gate_e[i], w_up_e[i],
                             w_down_e[i], norm_ple_g[i], w_ple_gate[i], w_ple_proj[i])
        kp_l.append(ka[:, S_p - keep:])
        vp_l.append(va[:, S_p - keep:])
        sp_l.append(s_new)
        qa, ka, va, qb, kb, vb, gb, ga, gbt = project_in(xs, norm_mix_g[i], w_in[i], pos_s)
        att = band_attention_sample(qa, ka, va, cache_k_a[i], cache_v_a[i], rel_bias[i])
        ret, s_upd = retention_block(qb.astype(F32), kb.astype(F32), vb.astype(F32),
                                     state_ret[i].astype(F32), log_g)
        xs = xs + merge_out(att, ret, gb, ga, gbt, ret_norm_g[i], w_proj_a[i], w_proj_b[i],
                            w_out[i], xs.dtype)
        xs = channel_and_ple(xs, p_sample[i], norm_ffn_g[i], w_router_group[i], b_router_group[i],
                             w_router_expert[i], b_router_expert[i], w_gate_e[i], w_up_e[i],
                             w_down_e[i], norm_ple_g[i], w_ple_gate[i], w_ple_proj[i])
        ks_l.append(ka)
        vs_l.append(va)
        ss_l.append(s_upd.astype(state_ret.dtype))
    y_prompt = rmsnorm(xp, final_norm_g)
    y_sample = rmsnorm(xs, final_norm_g)
    return (y_prompt, y_sample, jnp.stack(kp_l), jnp.stack(vp_l), jnp.stack(sp_l),
            jnp.stack(ks_l), jnp.stack(vs_l), jnp.stack(ss_l))


_drawn_inputs = setup_inputs


def setup_inputs(seed=0):
    import zlib

    import numpy as np

    out = dict(_drawn_inputs(seed))
    spreads = {}
    factors = {'norm_mix_g': 3.443,
     'rel_bias': 5.411,
     'ret_norm_g': 6.192,
     'norm_ffn_g': 3.424,
     'b_router_group': 6.04,
     'b_router_expert': 11.377,
     'norm_ple_g': 64.0,
     'final_norm_g': 31.285,
     'cache_k_a': 3.944,
     'cache_v_a': 5.158}
    for name, (base, spread) in spreads.items():
        noise = np.random.default_rng([zlib.crc32(name.encode()), seed]).standard_normal(out[name].shape)
        drawn = base * np.exp(spread * noise) if base else spread * noise
        out[name] = __import__('jax').numpy.asarray(drawn.astype(out[name].dtype))
    for name, factor in factors.items():
        out[name] = (out[name] * factor).astype(out[name].dtype)
    return out
```

```python
import numpy as np
import concourse.bass as bass
from concourse import mybir
from concourse.bass import ds

F32 = mybir.dt.float32
I32 = mybir.dt.int32
ALU = mybir.AluOpType
ACT = mybir.ActivationFunctionType
AX = mybir.AxisListType

P = 128
D = 1024
KD = D // P
SEQ, DEC_B, DEC_S = 1024, 8, 16
PT = SEQ // P
NT = PT + 1
HA, HDA = 8, 64
WA = HA * HDA
FA = WA // P
BAND = 512
NKB = BAND // P + 1
CLIP = 128
PAST = 256
HB, DK, DV = 4, 128, 256
VB = HB * DV
QKB = HB * DK
FB = VB // P
NG, EPG, NE = 4, 8, 32
DE = 512
KE = DE // P
DP = 256
KP = DP // P
EPS = 1e-6
BANK = 512
PAIRS = 2 * NT * P
OVER = 17
NBLK = NE + OVER
NEG = -1e30
SKEW = 768

CQA, CKA, CVA, CQB, CKB, CVB, CGB, CGA, CGT = 0, 512, 1024, 1536, 2048, 2560, 3584, 4608, 5632


class Counter:

    def __init__(self, nc, name, per=1):
        self.sem, self.per = nc.alloc_semaphore(name), per
        self.inc = (self.sem, 1)

    def __call__(self, t, m=None):
        return self.sem, t * self.per + 2 * self.per + (self.per if m is None else m)

    def credit(self, eng):
        eng.sem_inc(self.sem, 2 * self.per)


class DmaCounter:

    def __init__(self, nc, name, credits=1):
        self.sems = [nc.alloc_semaphore(f"{name}_{b}") for b in range(2)]
        self.credits = credits

    def inc(self, b):
        return self.sems[b], 16

    def __call__(self, t, b):
        return self.sems[b], t * 8 + (16 * (1 + self.credits) - 8 * b)

    def credit(self, eng):
        for sem in self.sems if self.credits else []:
            eng.sem_inc(sem, 16)


class Stage:

    def __init__(self, nc, name):
        self.nc, self.name, self.all = nc, name, []

    def counter(self, name, per=1):
        self.all.append(Counter(self.nc, f"{self.name}_{name}", per))
        return self.all[-1]

    def counters(self, *names, per=1):
        return [self.counter(n, per) for n in names]

    def dmas(self, *names, credits=1):
        new = [DmaCounter(self.nc, f"{self.name}_{n}", credits) for n in names]
        self.all += new
        return new

    def credit(self, eng):
        for s in self.all:
            s.credit(eng)

    def sems(self):
        return [sem for s in self.all for sem in (s.sems if isinstance(s, DmaCounter) else [s.sem])]


def reuse_semaphores(c):
    c.nc.clear_and_free_semaphores([sem for s in c.stages for sem in s.sems()])
    c.stages.clear()
    c.nc.all_engine_barrier()


class Steps:

    def __init__(self, eng, counter):
        self.eng, self.done, self.k = eng, counter, 0

    def start(self, t):
        assert self.k in (0, self.done.per), (self.k, self.done.per)
        self.t, self.k = t, 0

    def mark(self, ins):
        ins.then_inc(*self.done.inc)
        self.k += 1

    def link(self, ins):
        self.mark(ins)
        self.eng.wait_ge(*self.done(self.t, self.k))


def in_pairs(eng, n, body, peel=1):
    assert (n - peel) % 2 == 0
    with eng.Fori(0, (n - peel) // 2) as i:
        for b in range(2):
            body(i * 2 + b, b, True)
    for t in range(n - peel, n):
        body(t, t % 2, t + 2 < n)


def row(ap, t):
    return ap[ds(t, 1)].rearrange("a p n -> (a p) n")


def shape_constants():
    f = np.float32
    i = np.arange(P)
    log_g = np.log(f(1) - f(2) ** (f(-5) - np.arange(HB, dtype=f))).astype(np.float64)
    c = {}
    c["ident"] = np.eye(P)
    c["before"] = (i[:, None] < i[None, :])
    c["ones"] = np.ones((P, P))
    dist = i[None, :] - i[:, None]
    decay = np.exp(log_g[None, :, None] * np.maximum(dist, 0)[:, None, :]) * (dist >= 0)[:, None, :]
    same = (i[:, None] // DEC_S == i[None, :] // DEC_S)
    c["decay_p"] = decay
    c["decay_s"] = decay * same[:, None, :]
    c["qdec_p"] = np.broadcast_to(np.exp(log_g[:, None] * (i[None, :] + 1.0)), (P, HB, P))
    c["qdec_s"] = np.broadcast_to(np.exp(log_g[:, None] * (i[None, :] % DEC_S + 1.0)), (P, HB, P))
    c["kdec_p"] = np.exp(log_g[None, :] * (P - 1.0 - i[:, None]))
    ks = np.exp(log_g[None, :] * (DEC_S - 1.0 - i[:, None] % DEC_S))
    own = (i[:, None] // DEC_S == np.arange(DEC_B)[None, :])
    c["kdec_s"] = own[:, :, None] * ks[:, None, :]
    q, k = i[:, None], np.arange(NKB * P)[None, :]
    c["band"] = np.where((q < 64) & (k >= 576) | (q >= 64) & (k < 64), NEG, 0.0)
    c["halfneg"] = np.full((P, 16), -0.5)
    c["gidx"] = np.broadcast_to(np.arange(NG), (P, NG))
    c["eidx"] = np.broadcast_to(np.arange(NE), (P, NE))
    c["ebase"] = np.broadcast_to(np.arange(NE) * P, (P, NE))
    c["oidx"] = np.broadcast_to(np.arange(OVER), (P, OVER))
    c["ebase31"] = np.broadcast_to((NE - 1 - np.arange(NE)) * P, (P, NE))
    c["blocks"] = np.broadcast_to(np.arange(1, NBLK) * P, (P, NBLK - 1))
    c["block"] = np.broadcast_to(np.arange(NBLK), (P, NBLK))
    c["slot"] = np.broadcast_to(np.arange(P), (P, P))
    c["one"] = np.ones((P, NE))
    c["token"] = np.arange(NT)[None, :] * P + i[:, None]
    cols, at = [], {}
    n = 0
    for name, a in c.items():
        a = np.asarray(a, f).reshape(P, -1)
        at[name] = (n, a.shape[1])
        n += a.shape[1]
        cols.append(a)
    half = DK // 2
    freqs = (f(10000.0) ** (-np.arange(half, dtype=f) / f(half))).astype(f)
    pos = np.concatenate([np.arange(SEQ), PAST + i % DEC_S]).astype(f)
    ang = (pos[:, None] * freqs[None, :]).astype(f)
    rot = np.stack([np.cos(ang), np.sin(ang)], 1)
    rot = np.stack([rot, rot * f(DK ** -0.5)], 1)
    return np.concatenate(cols, 1), at, rot.reshape(NT, P, 4 * half).astype(f), [float(np.exp(x * P)) for x in log_g], [float(np.exp(x * DEC_S)) for x in log_g]


R1, R2, KV = 0, 24 * 1024, 36 * 1024
IDENT = KV + 9 * 1024
GAINS = IDENT + P
HALF = GAINS + 32
WORK = HALF + 16
ARENA = 52 * 1024 - 128


class Core:

    def __init__(self, nc, ins, outs, const_at, decay_tile, decay_sample):
        self.nc, self.i, self.o = nc, ins, outs
        self.const_at, self.decay_tile, self.decay_sample = const_at, decay_tile, decay_sample
        self.arena = nc.alloc_sbuf_tensor("arena", [P, ARENA], F32)
        self.psum = nc.alloc_psum_tensor("psum", [P, 8, BANK], F32)
        scratch = lambda name, shape, dt=F32: nc.dram_tensor(name, shape, dt, kind="Internal").ap()
        self.hT = scratch("hT_scratch", (NT, P, KD * P))
        self.qz = scratch("qz_scratch", (NT, P, HA * P))
        self.bT = scratch("bT_scratch", (NT, P, FB * P))
        self.aT = scratch("aT_scratch", (NT, P, FA * P))
        self.skew = scratch("bias_skew_scratch", (HA, P * SKEW))
        self.x1 = scratch("x1_scratch", (NT, P, D))
        self.xn = scratch("xn_scratch", (NT * P, D))
        self.ids = scratch("ids_scratch", (NBLK * P, 1), I32)
        self.y = scratch("y_scratch", (NBLK * P, D))
        self.kT = self.at(KV, FA, NT * P)
        self.vA = self.at(KV + FA * NT * P, NT, WA)
        self.ident = self.at(IDENT, P)
        self.half = self.at(HALF, 16)
        self.g_mix, self.g_ffn, self.g_ple, self.g_ret = (self.at(GAINS + 8 * n, KD) for n in range(4))
        self.stages = []
        self.holds = nc.alloc_semaphore("holds")
        self.consts_in = nc.alloc_semaphore("consts_in")

    def hold(self, eng):
        eng.sem_inc(self.holds, 1)

    def at(self, off, *dims, parts=P):
        n = int(np.prod(dims))
        assert off + n <= ARENA, (off, dims)
        ap = self.arena[0:parts, off:off + n]
        if len(dims) == 2:
            ap = ap.rearrange("p (a b) -> p a b", a=dims[0])
        if len(dims) == 3:
            ap = ap.rearrange("p (a b c) -> p a b c", a=dims[0], b=dims[1])
        if len(dims) == 4:
            ap = ap.rearrange("p (a b c d) -> p a b c d", a=dims[0], b=dims[1], c=dims[2])
        return ap

    def const(self, name, a=None):
        off, n = self.const_at[name]
        ap = self.i["consts"][:, off:off + n]
        return ap if a is None else ap.rearrange("p (a b) -> p a b", a=a)


class Room:

    def __init__(self, c, off, end=ARENA):
        self.c, self.off, self.end = c, off, end

    def take(self, *dims):
        ap = self.c.at(self.off, *dims)
        self.off += int(np.prod(dims))
        assert self.off <= self.end, (self.off, self.end)
        return ap


def slabs(w, c0, c1):
    return w.rearrange("(k p) n -> p k n", p=P)[:, :, c0:c1]


def gain(g, k0, k1):
    return g[:, k0:k1].unsqueeze(2).to_broadcast([P, k1 - k0, P])


def stage_a(c):
    nc, ps = c.nc, c.psum
    s = Stage(nc, "a")
    c.stages.append(s)
    x_in, hT_stored, k_stored, qz_stored = s.dmas("x_in", "hT_stored", "k_stored", "qz_stored")
    ssq_ready, ms_ready, rstd_ready, xn_ready = (s.counter(n) for n in ("ssq_ready", "ms_ready", "rstd_ready", "xn_ready"))
    xT_done, hT_ready, qz_ready = (s.counter(n, 2) for n in ("xT_done", "hT_ready", "qz_ready"))
    proj_done = s.counter("proj_done", 3)
    q_out, k_out, v_out, qT_done, kT_done, kT_out = (s.counter(n) for n in ("q_out", "k_out", "v_out", "qT_done", "kT_done", "kT_out"))
    v_stored, w_in, zeroed = (nc.alloc_semaphore(f"a_{n}") for n in ("v_stored", "w_in", "zeroed"))
    tmp = Room(c, R1 + 16 * 1024, R2)
    x, xn, hT, qz = tmp.take(2, D), tmp.take(2, D), tmp.take(2, KD, P), tmp.take(2, HA, P)
    w = c.at(R2, KD, 3 * WA)
    work = Room(c, WORK)
    q, k, junk = work.take(WA), work.take(2, WA), work.take(D)
    ssq, ms, rstd = work.take(2), work.take(2), work.take(2)
    zeros = work.take(D)
    zeros_ready, c.y_zeroed = nc.alloc_semaphore("a_zeros_ready"), nc.alloc_semaphore("y_zeroed")
    c.b_qkv_in = nc.alloc_semaphore("b_qkv_in")
    c.b_qkv = c.at(R1, KD, 2048)

    with nc.Block() as block:
        @block.sync
        def _(sp):
            s.credit(sp)
            sp.dma_start(c.ident, c.const("ident")).then_inc(c.consts_in, 16)
            sp.dma_start(c.half, c.const("halfneg")).then_inc(c.consts_in, 16)

            def load(t, b):
                sp.wait_ge(*xn_ready(t - 2))
                sp.dma_start(x[:, b, :], row(c.i["x_all"], t)).then_inc(*x_in.inc(b))

            load(0, 0)
            for g, name in ((c.g_mix, "norm_mix_g"), (c.g_ffn, "norm_ffn_g"), (c.g_ple, "norm_ple_g"),
                            (c.g_ret, "ret_norm_g")):
                sp.dma_start(g, c.i[name][0].rearrange("(k p) -> p k", p=P),
                             allow_slow_non_contiguous=True).then_inc(c.consts_in, 16)
            for kk in range(KD):
                sp.dma_start(w[:, kk, :], slabs(c.i["w_in"][0], CQA, CQA + 3 * WA)[:, kk, :]).then_inc(w_in, 16)
            load(1, 1)
            for kk in range(KD):
                sp.dma_start(c.b_qkv[:, kk, :], slabs(c.i["w_in"][0], CQB, CGB)[:, kk, :]).then_inc(c.b_qkv_in, 16)

            def tile(t, b, ahead):
                if ahead:
                    load(t + 2, b)
                sp.wait_ge(*hT_ready(t))
                sp.dma_start(row(c.hT, t), hT[:, b].rearrange("p k n -> p (k n)")).then_inc(*hT_stored.inc(b))
                sp.wait_ge(*k_out(t))
                sp.dma_start(row(c.o["k_all"], t), k[:, b, :]).then_inc(*k_stored.inc(b))
                sp.wait_ge(*qz_ready(t))
                sp.dma_start(row(c.qz, t), qz[:, b].rearrange("p h n -> p (h n)")).then_inc(*qz_stored.inc(b))
            in_pairs(sp, NT, tile, peel=3)
            sp.wait_ge(*v_out(NT - 1))
            sp.dma_start(c.o["v_all"].rearrange("t p n -> p t n"), c.vA).then_inc(v_stored, 16)
            sp.wait_ge(*hT_stored(NT - 1, 0))
            sp.wait_ge(*hT_stored(NT - 2, 1))
            sp.wait_ge(*k_stored(NT - 1, 0))
            sp.wait_ge(*k_stored(NT - 2, 1))
            sp.wait_ge(*qz_stored(NT - 1, 0))
            sp.wait_ge(*qz_stored(NT - 2, 1))
            sp.wait_ge(v_stored, 16)

        @block.scalar
        def _(act):
            def normalize(t, b):
                act.wait_ge(*x_in(t, b))
                act.wait_ge(*ssq_ready(t - 1))
                nc.scalar.activation(junk, x[:, b, :], ACT.Square, accum_out=ssq[:, b:b + 1]).then_inc(*ssq_ready.inc)
                act.wait_ge(*rstd_ready(t))
                act.wait_ge(*xT_done(t - 2))
                nc.scalar.activation(xn[:, b, :], x[:, b, :], ACT.Copy, scale=rstd[:, b:b + 1]).then_inc(*xn_ready.inc)

            def tile(t, b, ahead):
                if ahead or t == NT - 2:
                    normalize(t + 1, 1 - b)
                act.wait_ge(*proj_done(t, 1))
                act.wait_ge(*qT_done(t - 1))
                nc.scalar.activation(q, ps[:, 2, :], ACT.Copy).then_inc(*q_out.inc)
                act.wait_ge(*proj_done(t, 2))
                act.wait_ge(*k_stored(t - 2, b))
                nc.scalar.activation(k[:, b, :], ps[:, 3, :], ACT.Copy).then_inc(*k_out.inc)
            normalize(0, 0)
            act.wait_ge(zeros_ready, 1)
            for n in range(OVER):
                act.dma_start(c.y[(NE + n) * P:(NE + n + 1) * P, :], zeros).then_inc(c.y_zeroed, 16)
            in_pairs(act, NT, tile, peel=3)
            act.wait_ge(c.y_zeroed, 16 * OVER)

        @block.gpsimd
        def _(pool):
            nc.gpsimd.memset(zeros, 0.0).then_inc(zeros_ready, 1)
            pool.wait_ge(c.consts_in, 96)

            def tile(t, b, ahead):
                pool.wait_ge(*ms_ready(t))
                nc.gpsimd.tensor_tensor(rstd[:, b:b + 1], ms[:, b:b + 1], c.half[:, 0:1], ALU.pow).then_inc(*rstd_ready.inc)
            in_pairs(pool, NT, tile)

        @block.vector
        def _(dve):
            dve.wait_ge(c.consts_in, 96)
            qzp = qz.rearrange("p b (f two) n -> p (b f) two n", two=2)
            nc.vector.memset(qzp[64:128, :, 0, :], 0.0).then_inc(zeroed, 1)
            nc.vector.memset(qzp[0:64, :, 1, :], 0.0).then_inc(zeroed, 1)

            def h_transposed(t, b):
                dve.wait_ge(*ssq_ready(t))
                nc.vector.tensor_scalar(ms[:, b:b + 1], ssq[:, b:b + 1], 1.0 / D, EPS, ALU.mult, ALU.add).then_inc(*ms_ready.inc)
                for h in range(2):
                    dve.wait_ge(*xT_done(t, h + 1))
                    if h == 0:
                        dve.wait_ge(*hT_stored(t - 2, b))
                        dve.wait_ge(*proj_done(t - 2))
                    nc.vector.tensor_tensor(hT[:, b, 4 * h:4 * h + 4, :], ps[:, h, :].rearrange("p (k n) -> p k n", k=4),
                                            gain(c.g_mix, 4 * h, 4 * h + 4), ALU.mult).then_inc(*hT_ready.inc)

            def tile(t, b, ahead):
                if ahead or t == NT - 2:
                    h_transposed(t + 1, 1 - b)
                dve.wait_ge(*proj_done(t, 3))
                nc.vector.tensor_scalar(c.vA[:, ds(t, 1), :].rearrange("p a n -> p (a n)"), ps[:, 4, :], 1.0, None,
                                        ALU.mult).then_inc(*v_out.inc)
                dve.wait_ge(*qT_done(t))
                dve.wait_ge(*qz_stored(t - 2, b))
                q4 = qz[:, b].rearrange("p (f two) n -> p f two n", two=2)
                s4 = ps[:, 5, :].rearrange("p (f n) -> p f n", f=FA)
                nc.vector.tensor_copy(q4[0:64, :, 0, :], s4[0:64]).then_inc(*qz_ready.inc)
                nc.vector.tensor_copy(q4[64:128, :, 1, :], s4[64:128]).then_inc(*qz_ready.inc)
                dve.wait_ge(*kT_done(t))
                nc.vector.tensor_scalar(c.kT[:, :, ds(t * P, P)], ps[:, 6, :].rearrange("p (f n) -> p f n", f=FA),
                                        1.0, None, ALU.mult).then_inc(*kT_out.inc)
            h_transposed(0, 0)
            in_pairs(dve, NT, tile, peel=3)
            dve.wait_ge(zeroed, 2)

        @block.tensor
        def _(pe):
            pe.wait_ge(c.consts_in, 96)

            def transpose_x(t, b):
                pe.wait_ge(*xn_ready(t))
                for h in range(2):
                    pe.wait_ge(*hT_ready(t - 1, h + 1))
                    for kk in range(4 * h, 4 * h + 4):
                        last = nc.tensor.transpose(ps[:, h, (kk % 4) * P:(kk % 4 + 1) * P], xn[:, b, kk * P:(kk + 1) * P], c.ident)
                    last.then_inc(*xT_done.inc)

            def tile(t, b, ahead):
                pe.wait_ge(*hT_ready(t))
                for n, out in enumerate((q_out, k_out, v_out)):
                    pe.wait_ge(*out(t - 1))
                    for kk in range(KD):
                        last = nc.tensor.matmul(ps[:, 2 + n, :], hT[:, b, kk, :], w[:, kk, n * WA:(n + 1) * WA],
                                                start=kk == 0, stop=kk == KD - 1)
                    last.then_inc(*proj_done.inc)
                if ahead or t == NT - 2:
                    transpose_x(t + 1, 1 - b)
                for src, ready, out, done, bank in ((q, q_out, qz_ready, qT_done, 5), (k[:, b, :], k_out, kT_out, kT_done, 6)):
                    pe.wait_ge(*ready(t))
                    pe.wait_ge(*out(t - 1))
                    for f in range(FA):
                        last = nc.tensor.transpose(ps[:, bank, f * P:(f + 1) * P], src[:, f * P:(f + 1) * P], c.ident)
                    last.then_inc(*done.inc)
            transpose_x(0, 0)
            pe.wait_ge(w_in, 16 * KD)
            in_pairs(pe, NT, tile, peel=3)


def rows_normed(c, nc, dve, steps, o_done, ms_ready, rstd_ready, rb_ready, t, o, stats, mv, ms, rstd, rb, between=None):
    for h in range(HB):
        dve.wait_ge(*o_done(t, h // 2 + 1))
        ins = nc.vector.bn_stats(stats[:, h, :], o[:, h, :])
        steps.link(ins) if h == HB - 1 else steps.mark(ins)
    c.hold(dve)
    for h in range(HB):
        ins = nc.vector.bn_aggr(mv[:, h, :], stats[:, h, :])
        steps.link(ins) if h == HB - 1 else steps.mark(ins)
    nc.vector.tensor_scalar(ms, mv[:, :, 1], EPS, None, ALU.add).then_inc(*ms_ready.inc)
    if between:
        between()
    dve.wait_ge(*rstd_ready(t))
    for h in range(HB):
        nc.vector.tensor_scalar(rb[:, h, :], o[:, h, :], mv[:, h, 0:1], rstd[:, h:h + 1], ALU.subtract,
                                ALU.mult).then_inc(*rb_ready.inc)


def stage_b(c):
    nc, ps = c.nc, c.psum
    s = Stage(nc, "b")
    c.stages.append(s)
    hT_in, rot_in, bT_stored = s.dmas("hT_in", "rot_in", "bT_stored")
    proj_done = s.counter("proj_done", 6)
    qr_ready, kr_ready, q_read, k_read, v_out, silu_out, qT_out, o_done, st_done, bT_done, bT_out = s.counters(
        "qr_ready", "kr_ready", "q_read", "k_read", "v_out", "silu_out", "qT_out", "o_done", "st_done", "bT_done", "bT_out", per=2)
    qT_done, kT_done, kT_out, sT_done, sT_out, kd_ready, ms_ready, rstd_ready, b_ready = s.counters(
        "qT_done", "kT_done", "kT_out", "sT_done", "sT_out", "kd_ready", "ms_ready", "rstd_ready", "b_ready")
    state_out, rb_ready = s.counters("state_out", "rb_ready", per=4)
    norm_steps = s.counter("norm_steps", 8)
    g_in, tables_in, zeroed, state_stored = (nc.alloc_semaphore(f"b_{n}") for n in ("g_in", "tables_in", "zeroed", "state_stored"))
    c.b2_states_in = [nc.alloc_semaphore(f"b2_states_in{n}") for n in range(2)]
    wg = c.at(R1 + 16 * 1024, KD, 1024)
    room = Room(c, R2, KV)
    hT, v, sg = room.take(2, KD, P), room.take(2, VB), room.take(2, VB)
    tq, tk = room.take(2, QKB), room.take(2, QKB)
    rb, bg, state = room.take(HB, DV), room.take(VB), room.take(HB, DV)
    work = Room(c, WORK)
    qr, kr, kd, qT, qdT, kT, sT = (work.take(QKB) for _ in range(7))
    rot = work.take(2, 4, DK // 2)
    qdec = work.take(QKB)
    stats, mv, ms, rstd = work.take(HB, 6), work.take(HB, 2), work.take(HB), work.take(HB)
    kdec = work.take(HB)
    bT = room.take(FB, P)
    decay = work.take(QKB)
    c.tile8 = dict(qr=qr, kr=kr, v=v[:, 0, :], sg=sg[:, 0, :])
    bank_of = (0, 1, 2, 3, 0, 1)
    o = ps[:, 6:8, :].rearrange("p a (h n) -> p (a h) n", h=2)

    with nc.Block() as block:
        @block.sync
        def _(sp):
            s.credit(sp)

            def load(t, b):
                sp.wait_ge(*proj_done(t - 2))
                sp.dma_start(hT[:, b].rearrange("p k n -> p (k n)"), row(c.hT, t)).then_inc(*hT_in.inc(b))
                sp.wait_ge(*k_read(t - 2))
                sp.dma_start(rot[:, b].rearrange("p a n -> p (a n)"), row(c.i["rot"], t)).then_inc(*rot_in.inc(b))

            load(0, 0)
            for kk in range(KD):
                sp.dma_start(wg[:, kk, :], slabs(c.i["w_in"][0], CGB, CGA)[:, kk, :]).then_inc(g_in, 16)
            sp.dma_start(decay, c.const("decay_p")).then_inc(tables_in, 16)
            sp.dma_start(qdec, c.const("qdec_p")).then_inc(tables_in, 16)
            sp.dma_start(kdec, c.const("kdec_p")).then_inc(tables_in, 16)
            load(1, 1)

            def store(r, b):
                sp.wait_ge(*bT_out(r))
                sp.dma_start(row(c.bT, r), bT.rearrange("p k n -> p (k n)")).then_inc(*bT_stored.inc(b))

            with sp.Fori(0, 3) as i:
                for b in range(2):
                    t = i * 2 + (1 + b)
                    load(t + 1, b)
                    store(t - 1, b)
            load(8, 0)
            store(6, 0)
            sp.wait_ge(*proj_done(NT - 1, 4))
            for n in range(DEC_B):
                sp.dma_start(c.at(R1 + n * D, HB, DV), c.i["state_ret"][0, n].rearrange("h d e -> d h e")).then_inc(
                    c.b2_states_in[n // 4], 16)
            sp.wait_ge(*state_out(PT - 1))
            sp.dma_start(c.o["state_p"].rearrange("h d e -> d h e"), state).then_inc(state_stored, 16)
            store(7, 1)
            sp.wait_ge(*bT_stored(6, 0))
            sp.wait_ge(*bT_stored(7, 1))
            sp.wait_ge(state_stored, 16)

        @block.scalar
        def _(act):
            def tile(t, b):
                for h in range(2):
                    act.wait_ge(*proj_done(t, 3 + h))
                    act.wait_ge(*st_done(t - 2))
                    nc.scalar.activation(v[:, b, h * BANK:(h + 1) * BANK], ps[:, 2 + h, :], ACT.Copy).then_inc(*v_out.inc)
                for h in range(2):
                    act.wait_ge(*proj_done(t, 5 + h))
                    act.wait_ge(*b_ready(t - 2))
                    nc.scalar.activation(sg[:, b, h * BANK:(h + 1) * BANK], ps[:, h, :], ACT.Silu).then_inc(*silu_out.inc)
            in_pairs(act, NT, lambda t, b, ahead: tile(t, b))

        @block.gpsimd
        def _(pool):
            pool.wait_ge(tables_in, 48)

            def rotated(t, tmp, read, dst, last_use, ready):
                a, bb = (tmp[:, n, :].rearrange("p (h two d) -> p h two d", h=HB, two=2) for n in range(2))
                d = dst.rearrange("p (h two d) -> p h two d", h=HB, two=2)
                pool.wait_ge(*read(t))
                pool.wait_ge(*last_use(t - 1))
                nc.gpsimd.tensor_tensor(d[:, :, 0, :], a[:, :, 0, :], bb[:, :, 1, :], ALU.subtract).then_inc(*ready.inc)
                nc.gpsimd.tensor_tensor(d[:, :, 1, :], a[:, :, 1, :], bb[:, :, 0, :], ALU.add).then_inc(*ready.inc)

            def project_part(t):
                rotated(t, tq, q_read, qr, qT_done, qr_ready)
                pool.wait_ge(*kd_ready(t - 1))
                rotated(t, tk, k_read, kr, kT_done, kr_ready)

            def retain_part(r, b):
                pool.wait_ge(*ms_ready(r))
                nc.gpsimd.tensor_tensor(rstd, ms, c.half[:, 0:HB], ALU.pow).then_inc(*rstd_ready.inc)
                pool.wait_ge(*rb_ready(r))
                pool.wait_ge(*silu_out(r))
                pool.wait_ge(*bT_done(r - 1))
                nc.gpsimd.tensor_tensor(bg, rb.rearrange("p h n -> p (h n)"), sg[:, b, :], ALU.mult).then_inc(*b_ready.inc)

            def decayed(t):
                pool.wait_ge(*kr_ready(t))
                pool.wait_ge(*st_done(t - 1))
                nc.gpsimd.tensor_tensor(kd.rearrange("p (h n) -> p h n", h=HB), kr.rearrange("p (h n) -> p h n", h=HB),
                                        kdec.unsqueeze(2).to_broadcast([P, HB, DK]), ALU.mult).then_inc(*kd_ready.inc)

            project_part(0)
            decayed(0)
            with pool.Fori(0, PT // 2) as i:
                for b in range(2):
                    t = i * 2 + (1 + b)
                    project_part(t)
                    retain_part(t - 1, b)
                    decayed(t)

        @block.vector
        def _(dve):
            steps = Steps(dve, norm_steps)
            nc.vector.memset(state, 0.0).then_inc(zeroed, 1)
            dve.wait_ge(zeroed, 1)
            dve.wait_ge(tables_in, 48)

            def rotate(t, b, bank, tmp, part, read, ready):
                src = ps[:, bank, :].rearrange("p (h d) -> p h d", h=2 * HB)
                dve.wait_ge(*proj_done(t, bank + 1))
                dve.wait_ge(*rot_in(t, b))
                dve.wait_ge(*ready(t - 1))
                for n in range(2):
                    nc.vector.tensor_tensor(tmp[:, n, :].rearrange("p (h d) -> p h d", h=2 * HB), src,
                                            rot[:, b, 2 * part + n, :].unsqueeze(1).to_broadcast([P, 2 * HB, DK // 2]),
                                            ALU.mult).then_inc(*read.inc)

            def retain(r, b, between):
                dve.wait_ge(*qT_done(r))
                dve.wait_ge(*o_done(r - 1))
                nc.vector.tensor_copy(qT, ps[:, 4, :]).then_inc(*qT_out.inc)
                nc.vector.tensor_tensor(qdT, ps[:, 4, :], qdec, ALU.mult).then_inc(*qT_out.inc)
                between()
                dve.wait_ge(*kT_done(r))
                nc.vector.tensor_copy(kT, ps[:, 5, :]).then_inc(*kT_out.inc)
                dve.wait_ge(*sT_done(r))
                nc.vector.tensor_tensor(sT, ps[:, 4, :], decay, ALU.mult).then_inc(*sT_out.inc)

                def states():
                    for h in range(HB):
                        dve.wait_ge(*st_done(r, h // 2 + 1))
                        dve.wait_ge(*state_out(r - 1))
                        nc.vector.scalar_tensor_tensor(
                            state[:, h, :], state[:, h, :], c.decay_tile[h],
                            ps[:, 4 + h // 2, (h % 2) * DV:(h % 2 + 1) * DV], ALU.mult, ALU.add).then_inc(*state_out.inc)
                steps.start(r)
                dve.wait_ge(*b_ready(r - 1))
                rows_normed(c, nc, dve, steps, o_done, ms_ready, rstd_ready, rb_ready, r, o, stats, mv, ms, rstd, rb, states)
                for h in range(2):
                    dve.wait_ge(*bT_done(r, h + 1))
                    dve.wait_ge(*bT_stored(r - 1, 1 - b))
                    nc.vector.tensor_tensor(bT[:, 4 * h:4 * h + 4, :], ps[:, 4 + h, :].rearrange("p (k n) -> p k n", k=4),
                                            gain(c.g_ret, 4 * h, 4 * h + 4), ALU.mult).then_inc(*bT_out.inc)

            rotate(0, 0, 0, tq, 0, q_read, qr_ready)
            rotate(0, 0, 1, tk, 1, k_read, kr_ready)
            with dve.Fori(0, PT // 2) as i:
                for b in range(2):
                    t = i * 2 + (1 + b)
                    rotate(t, 1 - b, 0, tq, 0, q_read, qr_ready)
                    retain(t - 1, b, lambda: rotate(t, 1 - b, 1, tk, 1, k_read, kr_ready))

        @block.tensor
        def _(pe):
            def project(t, b, n):
                if n == 0:
                    pe.wait_ge(*hT_in(t, b))
                pe.wait_ge(*(silu_out(t - 1, 1), silu_out(t - 1, 2), v_out(t - 1, 1), v_out(t - 1, 2), q_read(t), k_read(t))[n])
                w = c.b_qkv[:, :, n * BANK:(n + 1) * BANK] if n < 4 else wg[:, :, (n - 4) * BANK:(n - 3) * BANK]
                for kk in range(KD):
                    last = nc.tensor.matmul(ps[:, bank_of[n], :], hT[:, b, kk, :], w[:, kk, :], start=kk == 0, stop=kk == KD - 1)
                last.then_inc(*proj_done.inc)

            def q_transposed(r, b):
                pe.wait_ge(*qr_ready(r))
                pe.wait_ge(*bT_out(r - 1, 1))
                for h in range(HB):
                    last = nc.tensor.transpose(ps[:, 4, h * P:(h + 1) * P], qr[:, h * P:(h + 1) * P], c.ident)
                last.then_inc(*qT_done.inc)

            def k_transposed(r, b):
                pe.wait_ge(*kr_ready(r))
                pe.wait_ge(*bT_out(r - 1, 2))
                for h in range(HB):
                    last = nc.tensor.transpose(ps[:, 5, h * P:(h + 1) * P], kr[:, h * P:(h + 1) * P], c.ident)
                last.then_inc(*kT_done.inc)

            def scores(r, b):
                pe.wait_ge(*qT_out(r))
                pe.wait_ge(*kT_out(r))
                for h in range(HB):
                    last = nc.tensor.matmul(ps[:, 4, h * P:(h + 1) * P], kT[:, h * P:(h + 1) * P], qT[:, h * P:(h + 1) * P],
                                            start=True, stop=True)
                last.then_inc(*sT_done.inc)

            def outputs(r, b):
                pe.wait_ge(*sT_out(r))
                pe.wait_ge(*v_out(r))
                pe.wait_ge(*state_out(r - 1))
                pe.wait_ge(*rb_ready(r - 1))
                for h in range(HB):
                    nc.tensor.matmul(o[:, h, :], sT[:, h * P:(h + 1) * P], v[:, b, h * DV:(h + 1) * DV], start=True, stop=False)
                    last = nc.tensor.matmul(o[:, h, :], qdT[:, h * P:(h + 1) * P], state[:, h, :], start=False, stop=True)
                    if h % 2:
                        last.then_inc(*o_done.inc)

            def states(r, b):
                pe.wait_ge(*kd_ready(r))
                for h in range(HB):
                    last = nc.tensor.matmul(ps[:, 4 + h // 2, (h % 2) * DV:(h % 2 + 1) * DV], kd[:, h * P:(h + 1) * P],
                                            v[:, b, h * DV:(h + 1) * DV], start=True, stop=True)
                    if h % 2:
                        last.then_inc(*st_done.inc)

            def gated_transposed(r, b):
                pe.wait_ge(*b_ready(r))
                for h in range(2):
                    pe.wait_ge(*state_out(r, 2 * h + 2))
                    for f in range(4 * h, 4 * h + 4):
                        last = nc.tensor.transpose(ps[:, 4 + h, (f % 4) * P:(f % 4 + 1) * P], bg[:, f * P:(f + 1) * P], c.ident)
                    last.then_inc(*bT_done.inc)

            pe.wait_ge(c.b_qkv_in, 16 * KD)
            for n in range(4):
                project(0, 0, n)
            pe.wait_ge(g_in, 16 * KD)
            for n in range(4, 6):
                project(0, 0, n)
            with pe.Fori(0, PT // 2) as i:
                for b in range(2):
                    t = i * 2 + (1 + b)
                    for n, retain in enumerate((q_transposed, k_transposed, scores, outputs, states, gated_transposed)):
                        project(t, 1 - b, n)
                        retain(t - 1, b)


def stage_b2(c):
    nc, ps = c.nc, c.psum
    s = Stage(nc, "b2")
    c.stages.append(s)
    qT_done, kT_done, sT_done, qT_out, sT_out, ms_ready, rstd_ready, b_ready = s.counters(
        "qT_done", "kT_done", "sT_done", "qT_out", "sT_out", "ms_ready", "rstd_ready", "b_ready")
    o_done, bT_done, bT_out = s.counters("o_done", "bT_done", "bT_out", per=2)
    km_ready = s.counter("km_ready", DEC_B)
    rb_ready, qm_out = s.counters("rb_ready", "qm_out", per=HB)
    st_done = s.counter("st_done", DEC_B)
    st_out = s.counter("st_out", DEC_B * HB)
    norm_steps = s.counter("norm_steps", 8)
    kT_out = s.counter("kT_out")
    tables_in, zeroed, stored = (nc.alloc_semaphore(f"b2_{n}") for n in ("tables_in", "zeroed", "stored"))
    room = Room(c, R1, R2)
    st = room.take(DEC_B, HB, DV)
    pitch = P + DEC_S
    qm = room.take(HB, DEC_B * pitch)
    km = room.take(DEC_B, HB, DK)
    qT, kT, sT, decay, qdec = (room.take(QKB) for _ in range(5))
    kdec = room.take(DEC_B, HB)
    rb, bg, bT = room.take(HB, DV), room.take(VB), room.take(FB, P)
    stats, mv, ms, rstd = room.take(HB, 6), room.take(HB, 2), room.take(HB), room.take(HB)
    qr, kr, v, sg = (c.tile8[n] for n in ("qr", "kr", "v", "sg"))
    o = ps[:, 3:5, :].rearrange("p a (h n) -> p (a h) n", h=2)

    table, skewed = c.at(WORK + 2 * QKB, HA, 2 * CLIP + 1), c.at(R2 + 6 * 1024, HA, SKEW)
    c.bias, band = c.at(WORK + 2 * QKB, HA, NKB * P), c.at(R2, NKB * P)
    table_in, skewed_done, skew_stored, bias_in = (nc.alloc_semaphore(f"b2_{n}") for n in ("table_in", "skewed_done", "skew_stored", "bias_in"))
    c.bias_ready = nc.alloc_semaphore("bias_ready")

    def state_banks(n):
        return (5, 6) if n % 2 == 0 else (7, 2)

    with nc.Block() as block:
        @block.sync
        def _(sp):
            s.credit(sp)
            for dst, name in ((decay, "decay_s"), (qdec, "qdec_s")):
                sp.dma_start(dst, c.const(name)).then_inc(tables_in, 16)
            sp.dma_start(kdec, c.const("kdec_s", DEC_B)).then_inc(tables_in, 16)
            for n in range(DEC_B):
                sp.wait_ge(*st_out(0, HB * (n + 1)))
                sp.dma_start(c.o["state_s"][n].rearrange("h d e -> d h e"), st[:, n]).then_inc(stored, 16)
            sp.wait_ge(*bT_out(0))
            sp.dma_start(row(c.bT, NT - 1), bT.rearrange("p k n -> p (k n)")).then_inc(stored, 16)
            sp.wait_ge(stored, 16 * (DEC_B + 1))

        @block.scalar
        def _(act):
            act.dma_start(table, c.i["rel_reversed"].unsqueeze(0).to_broadcast([P, HA, 2 * CLIP + 1])).then_inc(table_in, 16)
            act.dma_start(band, c.const("band")).then_inc(bias_in, 16)
            act.wait_ge(table_in, 16)
            far = BAND - 1
            nc.scalar.activation(skewed[:, :, 0:far], table[:, :, 0:1].to_broadcast([P, HA, far]), ACT.Copy).then_inc(skewed_done, 1)
            nc.scalar.activation(skewed[:, :, far:SKEW], table, ACT.Copy).then_inc(skewed_done, 1)
            act.wait_ge(skewed_done, 2)
            act.dma_start(c.skew.rearrange("h (p n) -> p h n", p=P), skewed).then_inc(skew_stored, 16)
            act.wait_ge(skew_stored, 16)
            act.dma_start(c.bias, bass.AP(tensor=c.skew.tensor, offset=P - 1, ap=[[SKEW - 1, P], [P * SKEW, HA], [1, NKB * P]])).then_inc(
                bias_in, 16)
            act.wait_ge(bias_in, 32)

        @block.gpsimd
        def _(pool):
            pool.wait_ge(tables_in, 48)
            for n in range(DEC_B):
                nc.gpsimd.tensor_tensor(km[:, n], kr.rearrange("p (h n) -> p h n", h=HB),
                                        kdec[:, n, :].unsqueeze(2).to_broadcast([P, HB, DK]), ALU.mult).then_inc(*km_ready.inc)
            pool.wait_ge(*ms_ready(0))
            nc.gpsimd.tensor_tensor(rstd, ms, c.half[:, 0:HB], ALU.pow).then_inc(*rstd_ready.inc)
            pool.wait_ge(*rb_ready(0))
            nc.gpsimd.tensor_tensor(bg, rb.rearrange("p h n -> p (h n)"), sg, ALU.mult).then_inc(*b_ready.inc)
            pool.wait_ge(bias_in, 32)
            nc.gpsimd.tensor_tensor(c.bias, c.bias, band.unsqueeze(1).to_broadcast([P, HA, NKB * P]), ALU.add).then_inc(c.bias_ready, 1)

        @block.vector
        def _(dve):
            steps = Steps(dve, norm_steps)
            nc.vector.memset(qm, 0.0).then_inc(zeroed, 1)
            dve.wait_ge(tables_in, 48)
            dve.wait_ge(*qT_done(0))
            nc.vector.tensor_copy(qT, ps[:, 0, :]).then_inc(*qT_out.inc)
            dve.wait_ge(*kT_done(0))
            nc.vector.tensor_copy(kT, ps[:, 1, :]).then_inc(*kT_out.inc)
            dve.wait_ge(zeroed, 1)
            for h in range(HB):
                nc.vector.tensor_tensor(qm[:, h].rearrange("p (b x) -> p b x", b=DEC_B)[:, :, 0:DEC_S],
                                        ps[:, 0, h * P:(h + 1) * P].rearrange("p (b x) -> p b x", b=DEC_B),
                                        qdec[:, h * P:(h + 1) * P].rearrange("p (b x) -> p b x", b=DEC_B),
                                        ALU.mult).then_inc(*qm_out.inc)
            dve.wait_ge(*sT_done(0))
            nc.vector.tensor_tensor(sT, ps[:, 2, :], decay, ALU.mult).then_inc(*sT_out.inc)

            def states():
                for n in range(DEC_B):
                    dve.wait_ge(*st_done(0, n + 1))
                    for h in range(HB):
                        new = ps[:, state_banks(n)[h // 2], (h % 2) * DV:(h % 2 + 1) * DV]
                        nc.vector.scalar_tensor_tensor(st[:, n, h, :], st[:, n, h, :], c.decay_sample[h], new,
                                                       ALU.mult, ALU.add).then_inc(*st_out.inc)
            steps.start(0)
            rows_normed(c, nc, dve, steps, o_done, ms_ready, rstd_ready, rb_ready, 0, o, stats, mv, ms, rstd, rb)
            states()
            for h in range(2):
                dve.wait_ge(*bT_done(0, h + 1))
                nc.vector.tensor_tensor(bT[:, 4 * h:4 * h + 4, :], ps[:, h, :].rearrange("p (k n) -> p k n", k=4),
                                        gain(c.g_ret, 4 * h, 4 * h + 4), ALU.mult).then_inc(*bT_out.inc)

        @block.tensor
        def _(pe):
            for src, done, bank in ((qr, qT_done, 0), (kr, kT_done, 1)):
                for h in range(HB):
                    last = nc.tensor.transpose(ps[:, bank, h * P:(h + 1) * P], src[:, h * P:(h + 1) * P], c.ident)
                last.then_inc(*done.inc)
            pe.wait_ge(*qT_out(0))
            pe.wait_ge(*kT_out(0))
            for h in range(HB):
                last = nc.tensor.matmul(ps[:, 2, h * P:(h + 1) * P], kT[:, h * P:(h + 1) * P], qT[:, h * P:(h + 1) * P],
                                        start=True, stop=True)
            last.then_inc(*sT_done.inc)
            pe.wait_ge(*sT_out(0))
            for n in range(2):
                pe.wait_ge(c.b2_states_in[n], 16 * 4)
            for h in range(HB):
                nc.tensor.matmul(o[:, h, :], sT[:, h * P:(h + 1) * P], v[:, h * DV:(h + 1) * DV], start=True, stop=False)
                pe.wait_ge(*qm_out(0, h + 1))
                for n in range(DEC_B):
                    last = nc.tensor.matmul(o[:, h, :], qm[:, h, n * P:(n + 1) * P], st[:, n, h, :], start=False,
                                            stop=n == DEC_B - 1)
                if h % 2:
                    last.then_inc(*o_done.inc)
            for n in range(DEC_B):
                pe.wait_ge(*km_ready(0, n + 1))
                if n >= 2:
                    pe.wait_ge(*st_out(0, HB * (n - 1)))
                for h in range(HB):
                    last = nc.tensor.matmul(ps[:, state_banks(n)[h // 2], (h % 2) * DV:(h % 2 + 1) * DV], km[:, n, h, :],
                                            v[:, h * DV:(h + 1) * DV], start=True, stop=True)
                last.then_inc(*st_done.inc)
            pe.wait_ge(*b_ready(0))
            for h in range(2):
                for f in range(4 * h, 4 * h + 4):
                    last = nc.tensor.transpose(ps[:, h, (f % 4) * P:(f % 4 + 1) * P], bg[:, f * P:(f + 1) * P], c.ident)
                last.then_inc(*bT_done.inc)


SCALE = HDA ** -0.5


def stage_c(c):
    nc, ps = c.nc, c.psum
    s = Stage(nc, "c")
    c.stages.append(s)
    qz_in, aT_stored = s.dmas("qz_in", "aT_stored")
    s_done, s_out, max_ready, p_ready, pT_done, pT_out, pv_done = s.counters(
        "s_done", "s_out", "max_ready", "p_ready", "pT_done", "pT_out", "pv_done", per=HA)
    inv_ready, a_out, aT_done, aT_out = s.counters("inv_ready", "a_out", "aT_done", "aT_out")
    c.merge_in = {n: nc.alloc_semaphore(f"merge_{n}_in") for n in ("ga", "pa", "gb", "pb", "wo")}
    room = Room(c, R2, KV)
    qz, S, Pr = room.take(2, HA, P), room.take(2, NKB * P), room.take(2, NKB * P)
    pT = room.take(2, NKB, P)
    a, aT = room.take(HA, HDA), room.take(2, FA, P)
    nmax, rsum, rinv = room.take(HA), room.take(2, HA), room.take(HA)
    c.w_ga, c.w_pa, c.w_gb = c.at(R1, KD, D), c.at(R1 + 8 * 1024, FA, D), c.at(R1 + 12 * 1024, KD, D)
    c.w_pb = c.at(R1 + 20 * 1024, FB, D)
    c.w_wo = c.at(R2 + 4 * 1024, KD, D)
    pT_banks = ps[:, 4:6, :].rearrange("p a n -> p (a n)")

    def s_banks(h):
        return ps[:, 2 * (h % 2):2 * (h % 2) + 2, :].rearrange("p a n -> p (a n)")

    def tiles(eng, body):
        full = NKB - 1
        for t in range(full):
            body(t, t % 2, t + 1)
        with eng.Fori(0, (PT - full) // 2) as i:
            for b in range(2):
                body(i * 2 + (full + b), b, NKB)

    with nc.Block() as block:
        @block.sync
        def _(sp):
            s.credit(sp)

            def load(t, b):
                sp.wait_ge(*s_done(t - 2))
                sp.dma_start(qz[:, b].rearrange("p h n -> p (h n)"), row(c.qz, t)).then_inc(*qz_in.inc(b))

            def tile(t, b, nb):
                load(t, b)
                if isinstance(t, int) and t == 0:
                    for dst, src, sem in ((c.w_ga, slabs(c.i["w_in"][0], CGA, CGT), "ga"), (c.w_pa, slabs(c.i["w_proj_a"][0], 0, D), "pa"),
                                          (c.w_gb, slabs(c.i["w_in"][0], CGT, CGT + D), "gb"), (c.w_pb[:, 0:4], slabs(c.i["w_proj_b"][0], 0, D)[:, 0:4], "pb")):
                        for k in range(dst.shape[1]):
                            sp.dma_start(dst[:, k, :], src[:, k, :]).then_inc(c.merge_in[sem], 16)
            tiles(sp, tile)
            sp.wait_ge(*aT_stored(PT - 2, 0))
            sp.wait_ge(*aT_stored(PT - 1, 1))

        @block.vector
        def _(dve):
            dve.wait_ge(c.bias_ready, 1)

            def tile(t, b, nb):
                for h in range(HA):
                    n = nb * P
                    dve.wait_ge(*s_done(t, h + 1))
                    dve.wait_ge(*p_ready(t, h - 1))
                    nc.vector.scalar_tensor_tensor(S[:, h % 2, 0:n], s_banks(h)[:, 0:n], SCALE, c.bias[:, h, NKB * P - n:], ALU.mult,
                                                   ALU.add).then_inc(*s_out.inc)
                    dve.wait_ge(*s_out(t, h + 1))
                    nc.vector.reduce_max(nmax[:, h:h + 1], S[:, h % 2, 0:n], AX.X, negate=True).then_inc(*max_ready.inc)
                dve.wait_ge(*p_ready(t))
                dve.wait_ge(*a_out(t - 1))
                nc.vector.reciprocal(rinv, rsum[:, b, :]).then_inc(*inv_ready.inc)
                dve.wait_ge(*inv_ready(t))
                dve.wait_ge(*pv_done(t))
                dve.wait_ge(*aT_done(t - 1))
                nc.vector.tensor_tensor(a, ps[:, 6, :].rearrange("p (h d) -> p h d", h=HA),
                                        rinv.unsqueeze(2).to_broadcast([P, HA, HDA]), ALU.mult).then_inc(*a_out.inc)
            tiles(dve, tile)

        @block.scalar
        def _(act):
            def transposed(t, h, b, nb):
                act.wait_ge(*pT_done(t, h + 1))
                act.wait_ge(*pv_done(t, h - 1))
                nc.scalar.activation(pT[:, h % 2, 0:nb, :].rearrange("p k n -> p (k n)"), pT_banks[:, 0:nb * P], ACT.Copy).then_inc(*pT_out.inc)

            def tile(t, b, nb):
                for h in range(HA):
                    act.wait_ge(*max_ready(t, h + 1))
                    act.wait_ge(*pT_done(t, h - 1))
                    nc.scalar.activation(Pr[:, h % 2, 0:nb * P], S[:, h % 2, 0:nb * P], ACT.Exp, bias=nmax[:, h:h + 1],
                                         accum_out=rsum[:, b, h:h + 1]).then_inc(*p_ready.inc)
                    if h:
                        transposed(t, h - 1, b, nb)
                transposed(t, HA - 1, b, nb)
                act.wait_ge(*aT_done(t))
                act.wait_ge(*aT_stored(t - 2, b))
                nc.scalar.activation(aT[:, b].rearrange("p f n -> p (f n)"), ps[:, 7, :], ACT.Copy).then_inc(*aT_out.inc)
                act.wait_ge(*aT_out(t))
                act.dma_start(row(c.aT, t), aT[:, b].rearrange("p f n -> p (f n)")).then_inc(*aT_stored.inc(b))
            tiles(act, tile)

        @block.tensor
        def _(pe):
            def scores(t, h, b, nb):
                if h == 0:
                    pe.wait_ge(*qz_in(t, b))
                pe.wait_ge(*s_out(t, h - 1))
                n = min(nb * P, BANK)
                k0 = t * P - (nb - 1) * P
                last = nc.tensor.matmul(s_banks(h)[:, 0:n], qz[:, b, h, :], c.kT[:, h // 2, ds(k0, n)], start=True, stop=True)
                if nb == NKB:
                    last = nc.tensor.matmul(s_banks(h)[:, n:n + P], qz[:, b, h, :], c.kT[:, h // 2, ds(k0 + n, P)], start=True, stop=True)
                last.then_inc(*s_done.inc)

            def transposed(t, h, b, nb):
                pe.wait_ge(*p_ready(t, h + 1))
                pe.wait_ge(*pT_out(t, h))
                for k in range(nb):
                    last = nc.tensor.transpose(pT_banks[:, k * P:(k + 1) * P], Pr[:, h % 2, k * P:(k + 1) * P], c.ident)
                last.then_inc(*pT_done.inc)

            def weighted(t, h, b, nb):
                if h == 0:
                    pe.wait_ge(*a_out(t - 1))
                pe.wait_ge(*pT_out(t, h + 1))
                for k in range(nb):
                    last = nc.tensor.matmul(ps[:, 6, h * HDA:(h + 1) * HDA], pT[:, h % 2, k, :],
                                            c.vA[:, ds(t - (nb - 1) + k, 1), h * HDA:(h + 1) * HDA].rearrange("p a n -> p (a n)"),
                                            start=k == 0, stop=k == nb - 1)
                last.then_inc(*pv_done.inc)

            def tile(t, b, nb):
                for h in range(HA + 2):
                    if h < HA:
                        scores(t, h, b, nb)
                    if 1 <= h <= HA:
                        transposed(t, h - 1, b, nb)
                    if h >= 2:
                        weighted(t, h - 2, b, nb)
                pe.wait_ge(*a_out(t))
                pe.wait_ge(*aT_out(t - 1))
                for f in range(FA):
                    last = nc.tensor.transpose(ps[:, 7, f * P:(f + 1) * P], a[:, 2 * f:2 * f + 2, :].rearrange("p h d -> p (h d)"), c.ident)
                last.then_inc(*aT_done.inc)
            tiles(pe, tile)


def stage_c2(c):
    nc, ps = c.nc, c.psum
    s = Stage(nc, "c2")
    c.stages.append(s)
    k_in, v_in = s.dmas("k_in", "v_in")
    vn_in = s.dmas("vn_in")[0]
    s_done, s_out, max_ready, p_ready, inv_ready, pn_ready, pT_done, pv_done = s.counters(
        "s_done", "s_out", "max_ready", "p_ready", "inv_ready", "pn_ready", "pT_done", "pv_done")
    kT_done, kT_out, pT_out, a_out = s.counters("kT_done", "kT_out", "pT_out", "a_out", per=2)
    q_in, qs_ready, bias_in, stored = (nc.alloc_semaphore(f"c2_{n}") for n in ("q_in", "qs_ready", "bias_in", "stored"))
    NK = PAST + DEC_S
    room = Room(c, R2, KV)
    ck, cv = room.take(2, 2, WA), room.take(2, 3, WA)
    kT, pT = room.take(2, FA, PAST), room.take(2, 3, P)
    S, Pr = room.take(2, NK), room.take(2, NK)
    qz = c.at(WORK, HA, P)
    work = Room(c, WORK + 1024)
    aT, bias = work.take(FA, P), work.take(NK)
    qs = work.take(DEC_B, HA, DEC_S)
    nmax, rsum, rinv = work.take(2), work.take(2), work.take(2)
    with nc.Block() as block:
        @block.sync
        def _(sp):
            s.credit(sp)
            sp.dma_start(qz.rearrange("p h n -> p (h n)"), row(c.qz, NT - 1)).then_inc(q_in, 16)
            for n in range(DEC_B):
                b = n % 2
                sp.wait_ge(*kT_done(n - 2))
                sp.dma_start(ck[:, b], c.i["cache_k_a"][0, n].rearrange("(k p) h d -> p k (h d)", p=P)).then_inc(*k_in.inc(b))
                sp.wait_ge(*pv_done(n - 2))
                sp.dma_start(cv[:, b, 0:2], c.i["cache_v_a"][0, n].rearrange("(k p) h d -> p k (h d)", p=P)).then_inc(*v_in.inc(b))
                sp.dma_start(cv[0:DEC_S, b, 2], c.o["v_all"][NT - 1, n * DEC_S:(n + 1) * DEC_S, :]).then_inc(*vn_in.inc(b))
                if n == 0:
                    for h in range(HA):
                        sp.dma_start(bias[h * DEC_S:(h + 1) * DEC_S, :], bass.AP(
                            tensor=c.skew.tensor, offset=h * P * SKEW + (NKB * P - 1) - PAST, ap=[[SKEW - 1, DEC_S], [1, NK]])).then_inc(bias_in, 16)
            sp.wait_ge(*a_out(DEC_B - 1))
            sp.dma_start(row(c.aT, NT - 1), aT.rearrange("p f n -> p (f n)")).then_inc(stored, 16)
            sp.wait_ge(stored, 16)

        @block.gpsimd
        def _(pool):
            pool.wait_ge(q_in, 16)
            nc.gpsimd.tensor_copy(qs.rearrange("p b h x -> p h b x"), qz.rearrange("p h (b x) -> p h b x", b=DEC_B)).then_inc(qs_ready, 1)

        @block.vector
        def _(dve):
            dve.wait_ge(bias_in, 16 * HA)

            def outputs(n):
                b = n % 2
                dve.wait_ge(*pv_done(n))
                src = ps[:, 6 + b, 0:FA * 2 * DEC_S].rearrange("p (f two x) -> p f two x", f=FA, two=2)
                for half in range(2):
                    rows = slice(64 * half, 64 * half + 64)
                    nc.vector.tensor_copy(aT[rows, :, n * DEC_S:(n + 1) * DEC_S], src[rows, :, half, :]).then_inc(*a_out.inc)

            for n in range(DEC_B):
                b = n % 2
                dve.wait_ge(*s_done(n))
                dve.wait_ge(*p_ready(n - 2))
                nc.vector.scalar_tensor_tensor(S[:, b, :], ps[:, 2 + b, 0:NK], SCALE, bias, ALU.mult, ALU.add).then_inc(*s_out.inc)
                dve.wait_ge(*s_out(n))
                nc.vector.reduce_max(nmax[:, b:b + 1], S[:, b, :], AX.X, negate=True).then_inc(*max_ready.inc)
                if n:
                    outputs(n - 1)
                dve.wait_ge(*p_ready(n))
                nc.vector.reciprocal(rinv[:, b:b + 1], rsum[:, b:b + 1]).then_inc(*inv_ready.inc)
                dve.wait_ge(*inv_ready(n))
                nc.vector.tensor_scalar(Pr[:, b, :], Pr[:, b, :], rinv[:, b:b + 1], None, ALU.mult).then_inc(*pn_ready.inc)
            outputs(DEC_B - 1)

        @block.scalar
        def _(act):
            def keys(n):
                b = n % 2
                for h in range(2):
                    act.wait_ge(*kT_done(n, h + 1))
                    act.wait_ge(*s_done(n - 2))
                    nc.scalar.activation(kT[:, b, 2 * h:2 * h + 2].rearrange("p f n -> p (f n)"), ps[:, h, :], ACT.Copy).then_inc(*kT_out.inc)

            keys(0)
            for n in range(DEC_B):
                b = n % 2
                if n + 1 < DEC_B:
                    keys(n + 1)
                act.wait_ge(*max_ready(n))
                act.wait_ge(*pT_done(n - 2))
                nc.scalar.activation(Pr[:, b, :], S[:, b, :], ACT.Exp, bias=nmax[:, b:b + 1], accum_out=rsum[:, b:b + 1]).then_inc(*p_ready.inc)
                act.wait_ge(*pT_done(n))
                act.wait_ge(*pv_done(n - 2))
                nc.scalar.activation(pT[:, b, 0:2].rearrange("p k n -> p (k n)"), ps[:, 4 + b, 0:2 * P], ACT.Copy).then_inc(*pT_out.inc)
                nc.scalar.activation(pT[0:DEC_S, b, 2], ps[0:DEC_S, 4 + b, 2 * P:3 * P], ACT.Copy).then_inc(*pT_out.inc)

        @block.tensor
        def _(pe):
            pe.wait_ge(qs_ready, 1)

            def keys(n):
                b = n % 2
                pe.wait_ge(*k_in(n, b))
                for h in range(2):
                    pe.wait_ge(*kT_out(n - 1, h + 1))
                    for f in range(2 * h, 2 * h + 2):
                        for k in range(2):
                            last = nc.tensor.transpose(ps[:, h, ((f % 2) * 2 + k) * P:((f % 2) * 2 + k + 1) * P],
                                                       ck[:, b, k, f * P:(f + 1) * P], c.ident)
                    last.then_inc(*kT_done.inc)

            def scores(n):
                b = n % 2
                pe.wait_ge(*kT_out(n))
                pe.wait_ge(*s_out(n - 2))
                for f in range(FA):
                    q = qs[:, n, 2 * f:2 * f + 2, :].rearrange("p h x -> p (h x)")
                    out = ps[32 * f:32 * f + 32, 2 + b, :]
                    nc.tensor.matmul(out[:, 0:PAST], q, kT[:, b, f, :], start=True, stop=True)
                    last = nc.tensor.matmul(out[:, PAST:NK], q, c.kT[:, f, SEQ + n * DEC_S:SEQ + (n + 1) * DEC_S], start=True, stop=True)
                last.then_inc(*s_done.inc)

            def outputs(n):
                b = n % 2
                pe.wait_ge(*pn_ready(n))
                pe.wait_ge(*pT_out(n - 2))
                for k in range(2):
                    nc.tensor.transpose(ps[:, 4 + b, k * P:(k + 1) * P], Pr[:, b, k * P:(k + 1) * P], c.ident)
                nc.tensor.transpose(ps[0:DEC_S, 4 + b, 2 * P:3 * P], Pr[:, b, PAST:NK], c.ident).then_inc(*pT_done.inc)
                pe.wait_ge(*pT_out(n))
                pe.wait_ge(*v_in(n, b))
                pe.wait_ge(*vn_in(n, b))
                pe.wait_ge(*a_out(n - 2))
                for f in range(FA):
                    for k in range(3):
                        rows = P if k < 2 else DEC_S
                        last = nc.tensor.matmul(ps[:, 6 + b, f * 32:(f + 1) * 32], cv[0:rows, b, k, f * P:(f + 1) * P],
                                                pT[0:rows, b, k, f * 32:(f + 1) * 32], start=k == 0, stop=k == 2)
                last.then_inc(*pv_done.inc)

            keys(0)
            scores(0)
            for n in range(DEC_B):
                if n + 1 < DEC_B:
                    keys(n + 1)
                    scores(n + 1)
                outputs(n)


NR = NG + NE
LOGITS = ARENA - NT * NR


def expert_slot(c, b):
    off = R1 + b * 12 * 1024
    return c.at(off, KD, DE), c.at(off + 4 * 1024, KD, DE), c.at(off + 8 * 1024, KE, D)


def stage_d(c):
    nc, ps = c.nc, c.psum
    reuse_semaphores(c)
    s = Stage(nc, "d")
    c.stages.append(s)
    hT_in, aT_in, bT_in, x_in, x1_stored, xn_stored = s.dmas("hT_in", "aT_in", "bT_in", "x_in", "x1_stored", "xn_stored")
    proj_done = s.counter("proj_done", 8)
    gate_out, prod_out = s.counters("gate_out", "prod_out", per=4)
    m_ready, mT_done, mT_out, wo_done, x1_ready, h2_done, h2_out = s.counters(
        "m_ready", "mT_done", "mT_out", "wo_done", "x1_ready", "h2_done", "h2_out", per=2)
    ssq_ready, ms_ready, rstd_ready, xn_ready, lg_done, lg_out = s.counters(
        "ssq_ready", "ms_ready", "rstd_ready", "xn_ready", "lg_done", "lg_out")
    router_in = nc.alloc_semaphore("d_router_in")
    kv = Room(c, KV, IDENT)
    hT, bT, aT, x = kv.take(2, KD, P), kv.take(2, FB, P), kv.take(2, FA, P), kv.take(2, D)
    g = kv.take(4, BANK)
    work = Room(c, WORK, LOGITS)
    m, mT, x1, xn, h2 = work.take(D), work.take(KD, P), work.take(D), work.take(D), work.take(KD, P)
    wr, br = work.take(KD, NR), work.take(NR)
    ssq, ms, rstd = work.take(1), work.take(1), work.take(1)
    c.logits = c.at(LOGITS, NT, NR)
    c.expert_in = [[nc.alloc_semaphore(f"expert_{n}_in{b}") for b in range(2)] for n in ("gate", "up", "down")]
    chunks = [(w, lhs, half) for half in range(2) for w, lhs in ((c.w_ga, hT), (c.w_pa, aT), (c.w_gb, hT), (c.w_pb, bT))]

    with nc.Block() as block:
        @block.sync
        def _(sp):
            s.credit(sp)

            def load(t, b):
                sp.wait_ge(*proj_done(t - 2))
                sp.dma_start(hT[:, b].rearrange("p k n -> p (k n)"), row(c.hT, t)).then_inc(*hT_in.inc(b))
                sp.dma_start(aT[:, b].rearrange("p k n -> p (k n)"), row(c.aT, t)).then_inc(*aT_in.inc(b))
                sp.dma_start(bT[:, b].rearrange("p k n -> p (k n)"), row(c.bT, t)).then_inc(*bT_in.inc(b))
                sp.wait_ge(*x1_ready(t - 2))
                sp.dma_start(x[:, b], row(c.i["x_all"], t)).then_inc(*x_in.inc(b))

            def store(r, b):
                sp.wait_ge(*x1_ready(r))
                sp.dma_start(row(c.x1, r), x1).then_inc(*x1_stored.inc(b))
                sp.wait_ge(*xn_ready(r))
                sp.dma_start(c.xn[ds(r * P, P), :], xn).then_inc(*xn_stored.inc(b))

            load(0, 0)
            for k in range(4, FB):
                sp.dma_start(c.w_pb[:, k, :], slabs(c.i["w_proj_b"][0], 0, D)[:, k, :]).then_inc(c.merge_in["pb"], 16)
            for k in range(KD):
                sp.dma_start(c.w_wo[:, k, :], slabs(c.i["w_out"][0], 0, D)[:, k, :]).then_inc(c.merge_in["wo"], 16)
            sp.dma_start(wr[:, :, 0:NG], slabs(c.i["w_router_group"][0], 0, NG), allow_slow_non_contiguous=True).then_inc(router_in, 16)
            sp.dma_start(wr[:, :, NG:NR], slabs(c.i["w_router_expert"][0], 0, NE)).then_inc(router_in, 16)
            sp.dma_start(br[:, 0:NG], c.i["b_router_group"].to_broadcast([P, NG])).then_inc(router_in, 16)
            sp.dma_start(br[:, NG:NR], c.i["b_router_expert"].to_broadcast([P, NE])).then_inc(router_in, 16)
            load(1, 1)
            with sp.Fori(0, 3) as i:
                for b in range(2):
                    t = i * 2 + (1 + b)
                    load(t + 1, b)
                    store(t - 1, b)
            load(8, 0)
            store(6, 0)
            store(7, 1)
            for b in range(2):
                for n, (dst, src, done) in enumerate(zip(expert_slot(c, b), (c.i["w_gate_e"][0, b], c.i["w_up_e"][0, b], c.i["w_down_e"][0, b]),
                                                         ((5, 5, 6), (7, 7, 8))[b])):
                    sp.wait_ge(*proj_done(NT - 1, done))
                    sp.dma_start(dst, src.rearrange("(k p) n -> p k n", p=P)).then_inc(c.expert_in[n][b], 16)
            store(8, 0)
            for sig in (x1_stored, xn_stored):
                sp.wait_ge(*sig(8, 0))
                sp.wait_ge(*sig(7, 1))

        @block.scalar
        def _(act):
            def gated(t, n):
                act.wait_ge(*proj_done(t, 2 * n + 1))
                act.wait_ge(*m_ready(t - 1, n // 2 + 1))
                nc.scalar.activation(g[:, n, :], ps[:, 2 * n % 4, :], ACT.Sigmoid).then_inc(*gate_out.inc)

            def turn(t, new, old):
                if new:
                    gated(t, 0)
                if old:
                    act.wait_ge(*x1_ready(t - 1))
                    act.wait_ge(*xn_stored(t - 2, old[1]))
                    act.wait_ge(*h2_done(t - 2))
                    nc.scalar.activation(xn, x1, ACT.Square, accum_out=ssq).then_inc(*ssq_ready.inc)
                if new:
                    gated(t, 1)
                if old:
                    act.wait_ge(*rstd_ready(t - 1))
                    nc.scalar.activation(xn, x1, ACT.Copy, scale=rstd).then_inc(*xn_ready.inc)
                if new:
                    gated(t, 2)
                    gated(t, 3)

            turn(0, True, None)
            with act.Fori(0, PT // 2) as i:
                for b in range(2):
                    turn(i * 2 + (1 + b), True, (b, 1 - b))
            turn(NT, False, (0, 1))

        @block.gpsimd
        def _(pool):
            def merged(t, half):
                pool.wait_ge(*prod_out(t, 2 * half + 2))
                pool.wait_ge(*mT_done(t - 1))
                nc.gpsimd.tensor_tensor(m[:, half * BANK:(half + 1) * BANK], g[:, 2 * half, :], g[:, 2 * half + 1, :], ALU.add).then_inc(*m_ready.inc)

            def turn(t, new, old):
                if old:
                    pool.wait_ge(*ms_ready(t - 1))
                    nc.gpsimd.tensor_tensor(rstd, ms, c.half[:, 0:1], ALU.pow).then_inc(*rstd_ready.inc)
                if new:
                    merged(t, 0)
                    merged(t, 1)

            turn(0, True, False)
            with pool.Fori(0, PT // 2) as i:
                for b in range(2):
                    turn(i * 2 + (1 + b), True, True)
            turn(NT, False, True)

        @block.vector
        def _(dve):
            dve.wait_ge(router_in, 64)

            def product(t, n):
                dve.wait_ge(*proj_done(t, 2 * n + 2))
                dve.wait_ge(*gate_out(t, n + 1))
                nc.vector.tensor_tensor(g[:, n, :], g[:, n, :], ps[:, (2 * n + 1) % 4, :], ALU.mult).then_inc(*prod_out.inc)

            def turn(t, b, new, old):
                r = t - 1
                if old:
                    for h in range(2):
                        dve.wait_ge(*mT_done(r, h + 1))
                        nc.vector.tensor_copy(mT[:, 4 * h:4 * h + 4].rearrange("p k n -> p (k n)"), ps[:, 4 + h, :]).then_inc(*mT_out.inc)
                if new:
                    product(t, 0)
                if old:
                    for h in range(2):
                        dve.wait_ge(*wo_done(r, h + 1))
                        dve.wait_ge(*x_in(r, 1 - b))
                        dve.wait_ge(*x1_stored(r - 1, b))
                        dve.wait_ge(*xn_ready(r - 1))
                        nc.vector.tensor_tensor(x1[:, h * BANK:(h + 1) * BANK], ps[:, 6 + h, :], x[:, 1 - b, h * BANK:(h + 1) * BANK],
                                                ALU.add).then_inc(*x1_ready.inc)
                    dve.wait_ge(*ssq_ready(r))
                    nc.vector.tensor_scalar(ms, ssq, 1.0 / D, EPS, ALU.mult, ALU.add).then_inc(*ms_ready.inc)
                if new:
                    product(t, 1)
                if old:
                    for h in range(2):
                        dve.wait_ge(*h2_done(r, h + 1))
                        dve.wait_ge(*lg_done(r - 1))
                        nc.vector.tensor_tensor(h2[:, 4 * h:4 * h + 4, :], ps[:, 4 + h, :].rearrange("p (k n) -> p k n", k=4),
                                                gain(c.g_ffn, 4 * h, 4 * h + 4), ALU.mult).then_inc(*h2_out.inc)
                    dve.wait_ge(*lg_done(r))
                    nc.vector.tensor_tensor(c.logits[:, ds(r, 1), :].rearrange("p a n -> p (a n)"), ps[:, 6, 0:NR], br, ALU.add).then_inc(*lg_out.inc)
                if new:
                    product(t, 2)
                    product(t, 3)

            turn(0, 0, True, False)
            with dve.Fori(0, PT // 2) as i:
                for b in range(2):
                    turn(i * 2 + (1 + b), 1 - b, True, True)
            turn(NT, 1, False, True)

        @block.tensor
        def _(pe):
            def project(t, b, n):
                w, lhs, half = chunks[n]
                if n == 0:
                    pe.wait_ge(*hT_in(t, b))
                if n == 1:
                    pe.wait_ge(*aT_in(t, b))
                if n == 3:
                    pe.wait_ge(*bT_in(t, b))
                out = gate_out if n % 2 == 0 else prod_out
                if n < 4:
                    pe.wait_ge(*out(t - 1, n // 2 + 3))
                else:
                    pe.wait_ge(*out(t, n // 2 - 1))
                slab_count = lhs.shape[2]
                for k in range(slab_count):
                    last = nc.tensor.matmul(ps[:, n % 4, :], lhs[:, b, k, :], w[:, k, half * BANK:(half + 1) * BANK],
                                            start=k == 0, stop=k == slab_count - 1)
                last.then_inc(*proj_done.inc)

            def merged_transposed(r):
                for h in range(2):
                    pe.wait_ge(*m_ready(r, h + 1))
                    pe.wait_ge(*h2_out(r - 1, h + 1))
                    for k in range(4 * h, 4 * h + 4):
                        last = nc.tensor.transpose(ps[:, 4 + h, (k % 4) * P:(k % 4 + 1) * P], m[:, k * P:(k + 1) * P], c.ident)
                    last.then_inc(*mT_done.inc)

            def projected_out(r):
                pe.wait_ge(*mT_out(r))
                pe.wait_ge(*lg_out(r - 1))
                for h in range(2):
                    for k in range(KD):
                        last = nc.tensor.matmul(ps[:, 6 + h, :], mT[:, k, :], c.w_wo[:, k, h * BANK:(h + 1) * BANK],
                                                start=k == 0, stop=k == KD - 1)
                    last.then_inc(*wo_done.inc)

            def normed_transposed(r):
                pe.wait_ge(*xn_ready(r))
                for h in range(2):
                    for k in range(4 * h, 4 * h + 4):
                        last = nc.tensor.transpose(ps[:, 4 + h, (k % 4) * P:(k % 4 + 1) * P], xn[:, k * P:(k + 1) * P], c.ident)
                    last.then_inc(*h2_done.inc)

            def routed(r):
                pe.wait_ge(*h2_out(r))
                for k in range(KD):
                    last = nc.tensor.matmul(ps[:, 6, 0:NR], h2[:, k, :], wr[:, k, :], start=k == 0, stop=k == KD - 1)
                last.then_inc(*lg_done.inc)

            waits = {0: ("ga", KD), 1: ("pa", FA), 2: ("gb", KD), 3: ("pb", FB)}
            for n in range(8):
                if n in waits:
                    pe.wait_ge(c.merge_in[waits[n][0]], 16 * waits[n][1])
                project(0, 0, n)
            pe.wait_ge(c.merge_in["wo"], 16 * KD)
            pe.wait_ge(router_in, 64)

            def turn(t, b, new):
                r = t - 1
                for n in range(8):
                    if new:
                        project(t, b, n)
                    if n == 0:
                        merged_transposed(r)
                    if n == 1:
                        projected_out(r)
                    if n == 3:
                        normed_transposed(r)
                    if n == 4:
                        routed(r)
            with pe.Fori(0, PT // 2) as i:
                for b in range(2):
                    turn(i * 2 + (1 + b), 1 - b, True)
            turn(NT, 1, False)


TOP = 2
FAR = -100.0
ROUTE_TABLES = (("before", P), ("ones", P), ("gidx", NG), ("eidx", NE), ("ebase", NE), ("ebase31", NE), ("oidx", OVER),
                ("blocks", NBLK - 1), ("block", NBLK), ("slot", P), ("one", NE), ("token", NT))


def stage_e(c):
    nc, ps = c.nc, c.psum
    s = Stage(nc, "e")
    c.stages.append(s)
    step, placed = s.counters("step", "placed")
    (exp_in, chosen, counted, gap_ready, gap_exp, sel_ready, ids_done) = s.counters(
        "exp_in", "chosen", "counted", "gap_ready", "gap_exp", "sel_ready", "ids_done")
    tables_in = nc.alloc_semaphore("e_tables_in")
    keep = Room(c, WORK, LOGITS)
    c.weights = keep.take(TOP, NT)
    c.places = keep.take(TOP, NT).bitcast(I32)
    c.block_ids = keep.take(NBLK).bitcast(I32)
    c.over_expert, c.over_count = keep.take(OVER).bitcast(I32), keep.take(1).bitcast(I32)
    c.after_routing = keep.off
    room = Room(c, KV, IDENT)
    T = {n: room.take(w) for n, w in ROUTE_TABLES}
    lg, le = c.logits[:, :, 0:NG], c.logits[:, :, NG:NR]
    gmax, gmin = room.take(NT), room.take(NT)
    g4, gsel, gexp = room.take(NT, NG), room.take(NT, NG), room.take(NT, NG)
    v, t32 = room.take(NT, NE), room.take(NT, NE)
    pick = [room.take(NT, NE) for _ in range(TOP)]
    top, first = [room.take(NT) for _ in range(TOP)], room.take(NT)
    both, rank, base = room.take(NT, NE), room.take(NT, NE), room.take(NT, NE)
    pg, gap = room.take(NT), room.take(NT)
    count, extra, total, diff = room.take(NE), room.take(NE), room.take(NE), room.take(NE)
    over = Room(c, R2, KV)
    grid, place = over.take(NE, 8), over.take(TOP, NT)
    grid2 = over.take(OVER, NE)
    grid3, hi, lo = over.take(TOP * NT, NBLK - 1), over.take(TOP, NT), over.take(TOP, NT)
    at_slot, at_block = over.take(TOP * NT, P), over.take(TOP * NT, NBLK)
    over_f = over.take(OVER)

    def wide(ap, *shape):
        return ap.to_broadcast([P, *shape])

    with nc.Block() as block:
        @block.sync
        def _(sp):
            s.credit(sp)
            for n, _ in ROUTE_TABLES:
                sp.dma_start(T[n], c.const(n)).then_inc(tables_in, 16)

        @block.scalar
        def _(act):
            act.wait_ge(*exp_in(0))
            nc.scalar.activation(gexp, g4, ACT.Exp).then_inc(*gap_exp.inc)
            act.wait_ge(*gap_ready(0))
            nc.scalar.activation(gap, gap, ACT.Exp).then_inc(*gap_exp.inc)

        @block.tensor
        def _(pe):
            pe.wait_ge(*chosen(0))
            rows = both.rearrange("p t e -> p (t e)")
            nc.tensor.matmul(ps[:, 0, 0:NT * NE], T["before"], rows, start=True, stop=True)
            nc.tensor.matmul(ps[:, 1, 0:NT * NE], T["ones"], rows, start=True, stop=True).then_inc(*counted.inc)
            pe.wait_ge(*sel_ready(0))
            for n in range(TOP * NT):
                last = nc.tensor.matmul(ps[:, 2, 0:NBLK], at_slot[:, n, :], at_block[:, n, :], start=n == 0, stop=n == TOP * NT - 1)
            last.then_inc(*ids_done.inc)

        @block.vector
        def _(dve):
            st = Steps(dve, step)
            st.start(0)
            link, V = st.link, nc.vector
            dve.wait_ge(tables_in, 16 * len(ROUTE_TABLES))
            link(V.tensor_reduce(gmax, lg, AX.X, ALU.max))
            link(V.tensor_tensor(g4, lg, wide(gmax.unsqueeze(2), NT, NG), ALU.is_equal))
            link(V.scalar_tensor_tensor(g4, g4, FAR, wide(T["gidx"].unsqueeze(1), NT, NG), ALU.mult, ALU.add))
            link(V.tensor_reduce(gmin, g4, AX.X, ALU.min))
            link(V.tensor_tensor(gsel, g4, wide(gmin.unsqueeze(2), NT, NG), ALU.is_equal))
            V.tensor_tensor(g4, lg, wide(gmax.unsqueeze(2), NT, NG), ALU.subtract).then_inc(*exp_in.inc)
            link(V.tensor_scalar(gsel, gsel, -NEG, NEG, ALU.mult, ALU.add))
            link(V.tensor_tensor(v.rearrange("p t (g e) -> p t g e", g=NG), le.rearrange("p t (g e) -> p t g e", g=NG),
                                 wide(gsel.unsqueeze(3), NT, NG, EPG), ALU.add))
            for k in range(TOP):
                link(V.tensor_reduce(top[k], v, AX.X, ALU.max))
                link(V.tensor_tensor(t32, v, wide(top[k].unsqueeze(2), NT, NE), ALU.is_equal))
                link(V.scalar_tensor_tensor(t32, t32, FAR, wide(T["eidx"].unsqueeze(1), NT, NE), ALU.mult, ALU.add))
                link(V.tensor_reduce(first, t32, AX.X, ALU.min))
                link(V.tensor_tensor(pick[k], t32, wide(first.unsqueeze(2), NT, NE), ALU.is_equal))
                if k == 0:
                    link(V.scalar_tensor_tensor(v, pick[0], 2 * NEG, v, ALU.mult, ALU.add))
            V.tensor_tensor(both, pick[0], pick[1], ALU.add).then_inc(*chosen.inc)
            V.tensor_tensor(gap, top[1], top[0], ALU.subtract).then_inc(*gap_ready.inc)
            dve.wait_ge(*gap_exp(0))
            link(V.tensor_reduce(pg, gexp, AX.X, ALU.add))
            dve.wait_ge(*gap_exp(1))
            link(V.tensor_scalar(first, gap, 1.0, None, ALU.add))
            link(V.tensor_tensor(pg, pg, first, ALU.mult))
            link(V.reciprocal(c.weights[:, 0, :], pg))
            link(V.tensor_tensor(c.weights[:, 1, :], c.weights[:, 0, :], gap, ALU.mult))
            dve.wait_ge(*counted(0))
            seen = ps[:, 1, 0:NT * NE].rearrange("p (t e) -> p t e", t=NT)
            link(V.memset(base[:, 0, :], 0.0))
            for t in range(1, NT):
                link(V.tensor_tensor(base[:, t, :], base[:, t - 1, :], seen[:, t - 1, :], ALU.add))
            link(V.tensor_tensor(count, base[:, NT - 1, :], seen[:, NT - 1, :], ALU.add))
            link(V.tensor_tensor(rank, base, ps[:, 0, 0:NT * NE].rearrange("p (t e) -> p t e", t=NT), ALU.add))
            link(V.tensor_tensor(grid, wide(count.unsqueeze(2), NE, 8), wide(T["blocks"][:, 0:8].unsqueeze(1), NE, 8), ALU.is_gt))
            link(V.tensor_reduce(extra, grid, AX.X, ALU.add))
            link(V.tensor_tensor_scan(total, T["one"], extra, 0.0, ALU.mult, ALU.add))
            link(V.tensor_tensor(diff, total, extra, ALU.subtract))
            link(V.scalar_tensor_tensor(diff, diff, float(P), T["ebase31"], ALU.mult, ALU.add))
            link(V.scalar_tensor_tensor(t32, rank, float(P), wide(diff.unsqueeze(1), NT, NE), ALU.is_ge, ALU.mult))
            link(V.tensor_tensor(rank, rank, wide(T["ebase"].unsqueeze(1), NT, NE), ALU.add))
            link(V.tensor_tensor(rank, rank, t32, ALU.add))
            for k in range(TOP):
                link(V.tensor_tensor(t32, pick[k], rank, ALU.mult))
                link(V.tensor_reduce(place[:, k, :], t32, AX.X, ALU.add))
            flat = place.rearrange("p k t -> p (k t)")
            link(V.tensor_copy(c.places, place))
            link(V.tensor_tensor(grid3, wide(flat.unsqueeze(2), TOP * NT, NBLK - 1), wide(T["blocks"].unsqueeze(1), TOP * NT, NBLK - 1), ALU.is_ge))
            link(V.tensor_reduce(hi.rearrange("p k t -> p (k t)"), grid3, AX.X, ALU.add))
            link(V.scalar_tensor_tensor(lo, hi, -float(P), place, ALU.mult, ALU.add))
            link(V.tensor_tensor(at_slot, wide(lo.rearrange("p k t -> p (k t)").unsqueeze(2), TOP * NT, P),
                                 wide(T["slot"].unsqueeze(1), TOP * NT, P), ALU.is_equal))
            link(V.tensor_tensor(at_block, wide(hi.rearrange("p k t -> p (k t)").unsqueeze(2), TOP * NT, NBLK),
                                 wide(T["block"].unsqueeze(1), TOP * NT, NBLK), ALU.is_equal))
            V.tensor_tensor(at_block.rearrange("p (k t) b -> p k t b", k=TOP), at_block.rearrange("p (k t) b -> p k t b", k=TOP),
                            wide(T["token"].unsqueeze(1).unsqueeze(3), TOP, NT, NBLK), ALU.mult).then_inc(*sel_ready.inc)
            link(V.tensor_tensor(grid2, wide(total.unsqueeze(1), OVER, NE), wide(T["oidx"].unsqueeze(2), OVER, NE), ALU.is_le))
            link(V.tensor_reduce(over_f, grid2, AX.X, ALU.add))
            link(V.tensor_scalar(over_f, over_f, float(NE - 1), None, ALU.min))
            link(V.tensor_copy(c.over_expert, over_f))
            link(V.tensor_copy(c.over_count, total[:, NE - 1:NE]))
            dve.wait_ge(*ids_done(0))
            link(V.tensor_copy(c.block_ids, ps[:, 2, 0:NBLK]))


def stage_f(c):
    nc, ps = c.nc, c.psum
    s = Stage(nc, "f")
    c.stages.append(s)
    (g_in,), (y_stored,) = s.dmas("g_in", credits=0), s.dmas("y_stored")
    gate_done, up_done, idx_ready, silu_out, hh_ready, hhT_done, hhT_out = s.counters(
        "gate_done", "up_done", "idx_ready", "silu_out", "hh_ready", "hhT_done", "hhT_out")
    xT_done, xT_out, down_done, y_out = s.counters("xT_done", "xT_out", "down_done", "y_out", per=2)
    c.ple_in = nc.alloc_semaphore("ple_in")
    room = Room(c, R2, R2 + 8 * 1024)
    xg, hg, y = room.take(2, D), room.take(2, KD, P), room.take(2, D)
    sil, hh, hhT = room.take(DE), room.take(DE), room.take(KE, P)
    c.idx = c.at(c.after_routing, 2 * TOP).bitcast(I32)
    c.w_pp = c.at(R2 + 8 * 1024, KP, D)
    c.w_ple = c.at(KV, KD, D)
    c.g_final = c.at(KV + 8 * 1024, D)
    slots = [expert_slot(c, b) for b in range(2)]

    def w_arrived(eng, n, e, b):
        eng.wait_ge(c.expert_in[n][b], e * 8 + (16 - 8 * b))

    with nc.Block() as block:
        @block.sync
        def _(sp):
            s.credit(sp)
            names = ("w_gate_e", "w_up_e", "w_down_e")

            def store(e, b):
                sp.wait_ge(*y_out(e))
                sp.dma_start(c.y[ds(e * P, P), :], y[:, b, :]).then_inc(*y_stored.inc(b))

            with sp.Fori(0, NE // 2 - 1) as i:
                for b in range(2):
                    e = i * 2 + b
                    for n, done in enumerate((gate_done, up_done, down_done)):
                        sp.wait_ge(*done(e))
                        sp.dma_start(slots[b][n], c.i[names[n]][0, ds(e + 2, 1)].rearrange("a (k p) n -> p (a k) n", p=P)).then_inc(
                            c.expert_in[n][b], 16)
                    store(e, b)
            for k in range(KD):
                sp.dma_start(c.w_ple[:, k, :], slabs(c.i["w_ple_gate"][0], 0, D)[:, k, :]).then_inc(c.ple_in, 16)
            sp.dma_start(c.w_pp, slabs(c.i["w_ple_proj"][0], 0, D)).then_inc(c.ple_in, 16)
            sp.dma_start(c.g_final, c.i["final_norm_g"].unsqueeze(0).to_broadcast([P, D])).then_inc(c.ple_in, 16)
            store(NE - 2, 0)
            store(NE - 1, 1)
            sp.wait_ge(*y_stored(NE - 2, 0))
            sp.wait_ge(*y_stored(NE - 1, 1))

        @block.gpsimd
        def _(pool):
            def gather(e, b, ahead):
                pool.wait_ge(*xT_done(e - 2))
                c.hold(pool)
                nc.gpsimd.tensor_copy(c.idx[:, b:b + 1], c.block_ids[:, ds(e, 1)]).then_inc(*idx_ready.inc)
                pool.wait_ge(*idx_ready(e))
                c.hold(pool)
                nc.gpsimd.indirect_dma_start(xg[:, b, :], None, c.xn, bass.IndirectOffsetOnAxis(ap=c.idx[:, b:b + 1], axis=0)).then_inc(
                    *g_in.inc(b))
            in_pairs(pool, NE, gather, peel=2)

        @block.scalar
        def _(act):
            def expert(e, b, ahead):
                act.wait_ge(*gate_done(e))
                act.wait_ge(*hh_ready(e - 1))
                nc.scalar.activation(sil, ps[:, 0, :], ACT.Silu).then_inc(*silu_out.inc)
                for h in range(2):
                    act.wait_ge(*down_done(e, h + 1))
                    act.wait_ge(*y_stored(e - 2, b))
                    nc.scalar.activation(y[:, b, h * BANK:(h + 1) * BANK], ps[:, 5 + h, :], ACT.Copy).then_inc(*y_out.inc)
            in_pairs(act, NE, expert, peel=2)

        @block.vector
        def _(dve):
            def rows(e, b):
                for h in range(2):
                    dve.wait_ge(*xT_done(e, h + 1))
                    dve.wait_ge(*up_done(e - 2))
                    nc.vector.tensor_tensor(hg[:, b, 4 * h:4 * h + 4, :], ps[:, 2 + h, :].rearrange("p (k n) -> p k n", k=4),
                                            gain(c.g_ffn, 4 * h, 4 * h + 4), ALU.mult).then_inc(*xT_out.inc)

            def expert(e, b, ahead):
                dve.wait_ge(*silu_out(e))
                dve.wait_ge(*up_done(e))
                dve.wait_ge(*hhT_done(e - 1))
                nc.vector.tensor_tensor(hh, sil, ps[:, 1, :], ALU.mult).then_inc(*hh_ready.inc)
                if ahead or e == NE - 2:
                    rows(e + 1, 1 - b)
                dve.wait_ge(*hhT_done(e))
                dve.wait_ge(*down_done(e - 1))
                nc.vector.tensor_copy(hhT.rearrange("p k n -> p (k n)"), ps[:, 4, :]).then_inc(*hhT_out.inc)
            rows(0, 0)
            in_pairs(dve, NE, expert, peel=2)

        @block.tensor
        def _(pe):
            def rows(e, b):
                pe.wait_ge(*g_in(e, b))
                for h in range(2):
                    pe.wait_ge(*xT_out(e - 1, h + 1))
                    for k in range(4 * h, 4 * h + 4):
                        last = nc.tensor.transpose(ps[:, 2 + h, (k % 4) * P:(k % 4 + 1) * P], xg[:, b, k * P:(k + 1) * P], c.ident)
                    last.then_inc(*xT_done.inc)

            def expert(e, b, ahead):
                pe.wait_ge(*xT_out(e))
                for n, out, done in ((0, silu_out, gate_done), (1, hh_ready, up_done)):
                    w_arrived(pe, n, e, b)
                    pe.wait_ge(*out(e - 1))
                    for k in range(KD):
                        last = nc.tensor.matmul(ps[:, n, :], hg[:, b, k, :], slots[b][n][:, k, :], start=k == 0, stop=k == KD - 1)
                    last.then_inc(*done.inc)
                if ahead or e == NE - 2:
                    rows(e + 1, 1 - b)
                pe.wait_ge(*hh_ready(e))
                pe.wait_ge(*hhT_out(e - 1))
                for k in range(KE):
                    last = nc.tensor.transpose(ps[:, 4, k * P:(k + 1) * P], hh[:, k * P:(k + 1) * P], c.ident)
                last.then_inc(*hhT_done.inc)
                pe.wait_ge(*hhT_out(e))
                w_arrived(pe, 2, e, b)
                for h in range(2):
                    pe.wait_ge(*y_out(e - 1, h + 1))
                    for k in range(KE):
                        last = nc.tensor.matmul(ps[:, 5 + h, :], hhT[:, k, :], slots[b][2][:, k, h * BANK:(h + 1) * BANK],
                                                start=k == 0, stop=k == KE - 1)
                    last.then_inc(*down_done.inc)
            rows(0, 0)
            in_pairs(pe, NE, expert, peel=2)


def stage_g(c):
    nc, ps = c.nc, c.psum
    names = ("idx_ready", "g_in", "w_in", "xT_done", "xT_out", "gate_done", "up_done", "silu_out", "hh_ready", "hhT_done",
             "hhT_out", "down_done", "y_out", "y_stored")
    idx_ready, g_in, w_in, xT_done, xT_out, gate_done, up_done, silu_out, hh_ready, hhT_done, hhT_out, down_done, y_out, y_stored = (
        nc.alloc_semaphore(f"g_{n}") for n in names)
    room = Room(c, R2, R2 + 8 * 1024)
    xg, hg, y = room.take(D), room.take(KD, P), room.take(D)
    sil, hh, hhT = room.take(DE), room.take(DE), room.take(KE, P)
    w = expert_slot(c, 0)

    def blocks(eng, body):
        count = eng.value_load(c.over_count[0:1, 0:1], min_val=0, max_val=OVER)
        with eng.Fori(0, OVER) as j:
            with eng.If(count > j):
                body(j)

    with nc.Block() as block:
        @block.sync
        def _(sp):
            def body(j):
                e = sp.value_load(c.over_expert[0:1, ds(j, 1)], min_val=0, max_val=NE - 1)
                for n, name in enumerate(("w_gate_e", "w_up_e", "w_down_e")):
                    sp.dma_start(w[n], c.i[name][0, ds(e, 1)].rearrange("a (k p) n -> p (a k) n", p=P)).then_inc(w_in, 16)
                sp.wait_ge(y_out, j * 2 + 2)
                sp.dma_start(c.y[ds((j + NE) * P, P), :], y).then_inc(y_stored, 16)
                sp.wait_ge(y_stored, j * 16 + 16)
                c.hold(sp)
            blocks(sp, body)

        @block.gpsimd
        def _(pool):
            def body(j):
                nc.gpsimd.tensor_copy(c.idx[:, 0:1], c.block_ids[:, ds(j + NE, 1)]).then_inc(idx_ready, 1)
                pool.wait_ge(idx_ready, j + 1)
                c.hold(pool)
                nc.gpsimd.indirect_dma_start(xg, None, c.xn, bass.IndirectOffsetOnAxis(ap=c.idx[:, 0:1], axis=0)).then_inc(g_in, 16)
                pool.wait_ge(y_stored, j * 16 + 16)
                c.hold(pool)
            blocks(pool, body)

        @block.scalar
        def _(act):
            def body(j):
                act.wait_ge(gate_done, j + 1)
                nc.scalar.activation(sil, ps[:, 0, :], ACT.Silu).then_inc(silu_out, 1)
                for h in range(2):
                    act.wait_ge(down_done, j * 2 + (h + 1))
                    nc.scalar.activation(y[:, h * BANK:(h + 1) * BANK], ps[:, 5 + h, :], ACT.Copy).then_inc(y_out, 1)
                act.wait_ge(y_stored, j * 16 + 16)
                c.hold(act)
            blocks(act, body)

        @block.vector
        def _(dve):
            def body(j):
                for h in range(2):
                    dve.wait_ge(xT_done, j * 2 + (h + 1))
                    nc.vector.tensor_tensor(hg[:, 4 * h:4 * h + 4, :], ps[:, 2 + h, :].rearrange("p (k n) -> p k n", k=4),
                                            gain(c.g_ffn, 4 * h, 4 * h + 4), ALU.mult).then_inc(xT_out, 1)
                dve.wait_ge(silu_out, j + 1)
                dve.wait_ge(up_done, j + 1)
                nc.vector.tensor_tensor(hh, sil, ps[:, 1, :], ALU.mult).then_inc(hh_ready, 1)
                dve.wait_ge(hhT_done, j + 1)
                nc.vector.tensor_copy(hhT.rearrange("p k n -> p (k n)"), ps[:, 4, :]).then_inc(hhT_out, 1)
                dve.wait_ge(y_stored, j * 16 + 16)
                c.hold(dve)
            blocks(dve, body)

        @block.tensor
        def _(pe):
            def body(j):
                pe.wait_ge(g_in, j * 16 + 16)
                for h in range(2):
                    for k in range(4 * h, 4 * h + 4):
                        last = nc.tensor.transpose(ps[:, 2 + h, (k % 4) * P:(k % 4 + 1) * P], xg[:, k * P:(k + 1) * P], c.ident)
                    last.then_inc(xT_done, 1)
                pe.wait_ge(xT_out, j * 2 + 2)
                pe.wait_ge(w_in, j * 48 + 48)
                for n, done in ((0, gate_done), (1, up_done)):
                    for k in range(KD):
                        last = nc.tensor.matmul(ps[:, n, :], hg[:, k, :], w[n][:, k, :], start=k == 0, stop=k == KD - 1)
                    last.then_inc(done, 1)
                pe.wait_ge(hh_ready, j + 1)
                for k in range(KE):
                    last = nc.tensor.transpose(ps[:, 4, k * P:(k + 1) * P], hh[:, k * P:(k + 1) * P], c.ident)
                last.then_inc(hhT_done, 1)
                pe.wait_ge(hhT_out, j + 1)
                for h in range(2):
                    for k in range(KE):
                        last = nc.tensor.matmul(ps[:, 5 + h, :], hhT[:, k, :], w[2][:, k, h * BANK:(h + 1) * BANK],
                                                start=k == 0, stop=k == KE - 1)
                    last.then_inc(down_done, 1)
                pe.wait_ge(y_stored, j * 16 + 16)
            blocks(pe, body)


def stage_h(c):
    nc, ps = c.nc, c.psum
    s = Stage(nc, "h")
    x_in, p_in, out_stored = s.dmas("x_in", "p_in", "out_stored")
    y1_in, y2_in = s.dmas("y1_in", "y2_in", credits=0)
    idx_ready, pT_done, pT_out, f_ready = s.counters("idx_ready", "pT_done", "pT_out", "f_ready")
    ssq_ready, ms_ready, rstd_ready, xn_ready, x2_ready, x2a_ready = s.counters(
        "ssq_ready", "ms_ready", "rstd_ready", "xn_ready", "x2_ready", "x2a_ready")
    ssq3_ready, ms3_ready, rstd3_ready, n3_ready = s.counters("ssq3_ready", "ms3_ready", "rstd3_ready", "n3_ready")
    xT_done, xT_out, gate_done, gate_out, emb_done, e_ready, x3_ready = s.counters(
        "xT_done", "xT_out", "gate_done", "gate_out", "emb_done", "e_ready", "x3_ready", per=2)
    room = Room(c, R1, R2)
    x, p, y1, y2 = room.take(2, D), room.take(2, DP), room.take(2, D), room.take(2, D)
    xn, hT, pT = room.take(D), room.take(2, KD, P), room.take(2, KP, P)
    g, e, x3, out = room.take(D), room.take(D), room.take(D), room.take(2, D)
    x2 = room.take(2, D)
    x2a = room.take(D)
    ssq, ms, rstd, ssq3, ms3, rstd3 = (room.take(1) for _ in range(6))

    with nc.Block() as block:
        @block.sync
        def _(sp):
            s.credit(sp)

            def load(t, b):
                sp.wait_ge(*x2a_ready(t - 2))
                sp.dma_start(x[:, b], row(c.x1, t)).then_inc(*x_in.inc(b))
                sp.wait_ge(*pT_done(t - 2))
                sp.dma_start(p[:, b], row(c.i["p_all"], t)).then_inc(*p_in.inc(b))

            load(0, 0)
            load(1, 1)

            def tile(t, b, ahead):
                if ahead:
                    load(t + 2, b)
                sp.wait_ge(*f_ready(t))
                sp.dma_start(row(c.o["y_all"], t), out[:, b]).then_inc(*out_stored.inc(b))
            in_pairs(sp, NT, tile, peel=3)
            sp.wait_ge(*out_stored(NT - 1, 0))
            sp.wait_ge(*out_stored(NT - 2, 1))

        @block.gpsimd
        def _(pool):
            def gather(t, b):
                pool.wait_ge(*x2_ready(t - 2))
                c.hold(pool)
                nc.gpsimd.tensor_copy(c.idx[:, 2 * b:2 * b + 2], c.places[:, :, ds(t, 1)].rearrange("p k a -> p (k a)")).then_inc(*idx_ready.inc)
                pool.wait_ge(*idx_ready(t))
                c.hold(pool)
                for k, (dst, sig) in enumerate(((y1, y1_in), (y2, y2_in))):
                    nc.gpsimd.indirect_dma_start(dst[:, b, :], None, c.y, bass.IndirectOffsetOnAxis(
                        ap=c.idx[:, 2 * b + k:2 * b + k + 1], axis=0)).then_inc(*sig.inc(b))

            def root(m, ms_, rstd_, ready, t):
                pool.wait_ge(*m(t))
                nc.gpsimd.tensor_tensor(rstd_, ms_, c.half[:, 0:1], ALU.pow).then_inc(*ready.inc)

            def tile(t, b, ahead):
                if ahead or t == NT - 2:
                    gather(t + 1, 1 - b)
                root(ms_ready, ms, rstd, rstd_ready, t)
                root(ms3_ready, ms3, rstd3, rstd3_ready, t)
                pool.wait_ge(*n3_ready(t))
                pool.wait_ge(*out_stored(t - 2, b))
                nc.gpsimd.tensor_tensor(out[:, b], x3, c.g_final, ALU.mult).then_inc(*f_ready.inc)
            gather(0, 0)
            pool.wait_ge(c.ple_in, 16 * (KD + 2))
            in_pairs(pool, NT, tile, peel=3)

        @block.vector
        def _(dve):
            def tile(t, b, ahead):
                w = c.weights
                dve.wait_ge(*x_in(t, b))
                dve.wait_ge(*y1_in(t, b))
                nc.vector.scalar_tensor_tensor(x2a, y1[:, b], w[:, 0, ds(t, 1)], x[:, b], ALU.mult, ALU.add).then_inc(*x2a_ready.inc)
                dve.wait_ge(*x2a_ready(t))
                dve.wait_ge(*y2_in(t, b))
                dve.wait_ge(*x3_ready(t - 2))
                nc.vector.scalar_tensor_tensor(x2[:, b], y2[:, b], w[:, 1, ds(t, 1)], x2a, ALU.mult, ALU.add).then_inc(*x2_ready.inc)
                dve.wait_ge(*ssq_ready(t))
                nc.vector.tensor_scalar(ms, ssq, 1.0 / D, EPS, ALU.mult, ALU.add).then_inc(*ms_ready.inc)
                dve.wait_ge(*pT_done(t))
                dve.wait_ge(*emb_done(t - 2))
                nc.vector.tensor_copy(pT[:, b].rearrange("p k n -> p (k n)"), ps[:, 2, 0:KP * P]).then_inc(*pT_out.inc)
                for h in range(2):
                    dve.wait_ge(*xT_done(t, h + 1))
                    dve.wait_ge(*gate_done(t - 2))
                    nc.vector.tensor_tensor(hT[:, b, 4 * h:4 * h + 4, :], ps[:, h, :].rearrange("p (k n) -> p k n", k=4),
                                            gain(c.g_ple, 4 * h, 4 * h + 4), ALU.mult).then_inc(*xT_out.inc)
                for h in range(2):
                    cols = slice(h * BANK, (h + 1) * BANK)
                    dve.wait_ge(*emb_done(t, h + 1))
                    dve.wait_ge(*gate_out(t, h + 1))
                    nc.vector.tensor_tensor(e[:, cols], g[:, cols], ps[:, 5 + h, :], ALU.mult).then_inc(*e_ready.inc)
                    dve.wait_ge(*e_ready(t, h + 1))
                    dve.wait_ge(*f_ready(t - 1))
                    nc.vector.tensor_tensor(x3[:, cols], e[:, cols], x2[:, b, cols], ALU.add).then_inc(*x3_ready.inc)
                dve.wait_ge(*ssq3_ready(t))
                nc.vector.tensor_scalar(ms3, ssq3, 1.0 / D, EPS, ALU.mult, ALU.add).then_inc(*ms3_ready.inc)
            in_pairs(dve, NT, tile)

        @block.scalar
        def _(act):
            def tile(t, b, ahead):
                act.wait_ge(*x2_ready(t))
                act.wait_ge(*xT_done(t - 1))
                nc.scalar.activation(xn, x2[:, b], ACT.Square, accum_out=ssq).then_inc(*ssq_ready.inc)
                act.wait_ge(*rstd_ready(t))
                nc.scalar.activation(xn, x2[:, b], ACT.Copy, scale=rstd).then_inc(*xn_ready.inc)
                for h in range(2):
                    cols = slice(h * BANK, (h + 1) * BANK)
                    act.wait_ge(*gate_done(t, h + 1))
                    act.wait_ge(*e_ready(t - 1))
                    nc.scalar.activation(g[:, cols], ps[:, 3 + h, :], ACT.Sigmoid).then_inc(*gate_out.inc)
                act.wait_ge(*x3_ready(t))
                nc.scalar.activation(g, x3, ACT.Square, accum_out=ssq3).then_inc(*ssq3_ready.inc)
                act.wait_ge(*rstd3_ready(t))
                nc.scalar.activation(x3, x3, ACT.Copy, scale=rstd3).then_inc(*n3_ready.inc)
            in_pairs(act, NT, tile)

        @block.tensor
        def _(pe):
            def tile(t, b, ahead):
                pe.wait_ge(*p_in(t, b))
                pe.wait_ge(*pT_out(t - 1))
                for k in range(KP):
                    last = nc.tensor.transpose(ps[:, 2, k * P:(k + 1) * P], p[:, b, k * P:(k + 1) * P], c.ident)
                last.then_inc(*pT_done.inc)
                pe.wait_ge(*xn_ready(t))
                for h in range(2):
                    pe.wait_ge(*xT_out(t - 1, h + 1))
                    for k in range(4 * h, 4 * h + 4):
                        last = nc.tensor.transpose(ps[:, h, (k % 4) * P:(k % 4 + 1) * P], xn[:, k * P:(k + 1) * P], c.ident)
                    last.then_inc(*xT_done.inc)
                pe.wait_ge(*pT_out(t))
                for h in range(2):
                    pe.wait_ge(*e_ready(t - 1, h + 1))
                    for k in range(KP):
                        last = nc.tensor.matmul(ps[:, 5 + h, :], pT[:, b, k, :], c.w_pp[:, k, h * BANK:(h + 1) * BANK],
                                                start=k == 0, stop=k == KP - 1)
                    last.then_inc(*emb_done.inc)
                pe.wait_ge(*xT_out(t))
                for h in range(2):
                    pe.wait_ge(*gate_out(t - 1, h + 1))
                    for k in range(KD):
                        last = nc.tensor.matmul(ps[:, 3 + h, :], hT[:, b, k, :], c.w_ple[:, k, h * BANK:(h + 1) * BANK],
                                                start=k == 0, stop=k == KD - 1)
                    last.then_inc(*gate_done.inc)
            pe.wait_ge(c.ple_in, 16 * (KD + 2))
            in_pairs(pe, NT, tile)


def build(nc, ins, outs, const_at, decay_tile, decay_sample):
    c = Core(nc, ins, outs, const_at, decay_tile, decay_sample)
    stage_a(c)
    stage_b(c)
    stage_b2(c)
    stage_c(c)
    stage_c2(c)
    stage_d(c)
    stage_e(c)
    stage_f(c)
    stage_g(c)
    stage_h(c)


INPUTS = ("cache_k_a", "cache_v_a", "state_ret", "norm_mix_g", "w_in", "rel_bias", "ret_norm_g", "w_proj_a",
          "w_proj_b", "w_out", "norm_ffn_g", "w_router_group", "b_router_group", "w_router_expert",
          "b_router_expert", "w_gate_e", "w_up_e", "w_down_e", "norm_ple_g", "w_ple_gate", "w_ple_proj",
          "final_norm_g")
OUTPUTS = {"y_all": (NT, P, D), "k_all": (NT, P, WA), "v_all": (NT, P, WA), "state_p": (HB, DK, DV),
           "state_s": (DEC_B, HB, DK, DV)}


def kernel(**inputs):
    import numpy as np
    import concourse.bacc as bacc
    from concourse.bass_utils import run_bass_kernel_spmd

    nc = bacc.Bacc("TRN2", target_bir_lowering=False, num_devices=1)
    consts, const_at, rot, decay_tile, decay_sample = shape_constants()
    arrays = {name: np.ascontiguousarray(inputs[name]) for name in INPUTS}
    tiles = lambda p, s: np.concatenate([np.asarray(p).reshape(PT, P, -1), np.asarray(s).reshape(1, P, -1)])
    arrays["x_all"] = tiles(inputs["x_prompt"], inputs["x_sample"])
    arrays["p_all"] = tiles(inputs["p_prompt"], inputs["p_sample"])
    arrays["rel_reversed"] = np.ascontiguousarray(np.asarray(inputs["rel_bias"])[0, :, ::-1])
    arrays["consts"], arrays["rot"] = consts, rot
    ins = {n: nc.dram_tensor(n, a.shape, mybir.dt.from_np(a.dtype), kind="ExternalInput").ap() for n, a in arrays.items()}
    outs = {n: nc.dram_tensor(n, shape, F32, kind="ExternalOutput").ap() for n, shape in OUTPUTS.items()}
    build(nc, ins, outs, const_at, decay_tile, decay_sample)
    r = run_bass_kernel_spmd(nc, [arrays], core_ids=[0])
    y, k, v, sp, ss = (np.asarray(r.results[0][n]) for n in OUTPUTS)
    band = PT - BAND // P
    return (y[:PT].reshape(1, SEQ, D), y[PT].reshape(DEC_B, DEC_S, D),
            k[band:PT].reshape(1, 1, BAND, HA, HDA), v[band:PT].reshape(1, 1, BAND, HA, HDA),
            sp.reshape(1, 1, HB, DK, DV),
            k[PT].reshape(1, DEC_B, DEC_S, HA, HDA), v[PT].reshape(1, DEC_B, DEC_S, HA, HDA),
            ss.reshape(1, DEC_B, HB, DK, DV))
```

```python
import numpy as np
import concourse.bass as bass
from concourse import mybir
from concourse.bass import ds

F32 = mybir.dt.float32
F32R = mybir.dt.float32r
I32 = mybir.dt.int32
ALU = mybir.AluOpType
ACT = mybir.ActivationFunctionType
AX = mybir.AxisListType

P = 128
D = 1024
KD = D // P
SEQ, DEC_B, DEC_S = 1024, 8, 16
PT = SEQ // P
NT = PT + 1
HA, HDA = 8, 64
WA = HA * HDA
FA = WA // P
BAND = 512
NKB = BAND // P + 1
CLIP = 128
PAST = 256
HB, DK, DV = 4, 128, 256
VB = HB * DV
QKB = HB * DK
FB = VB // P
NG, EPG, NE = 4, 8, 32
DE = 512
KE = DE // P
DP = 256
KP = DP // P
EPS = 1e-6
BANK = 512
OVER = 17
NBLK = NE + OVER
NEG = -1e30
SKEW = 768

CQA, CKA, CVA, CQB, CKB, CVB, CGB, CGA, CGT = 0, 512, 1024, 1536, 2048, 2560, 3584, 4608, 5632


class Counter:

    def __init__(self, nc, name, per=1):
        self.sem, self.per = nc.alloc_semaphore(name), per
        self.inc = (self.sem, 1)

    def __call__(self, t, m=None):
        return self.sem, t * self.per + 2 * self.per + (self.per if m is None else m)

    def credit(self, eng):
        eng.sem_inc(self.sem, 2 * self.per)


class DmaCounter:

    def __init__(self, nc, name, credits=1):
        self.sems = [nc.alloc_semaphore(f"{name}_{b}") for b in range(2)]
        self.credits = credits

    def inc(self, b):
        return self.sems[b], 16

    def __call__(self, t, b):
        return self.sems[b], t * 8 + (16 * (1 + self.credits) - 8 * b)

    def credit(self, eng):
        for sem in self.sems if self.credits else []:
            eng.sem_inc(sem, 16)


class Stage:

    def __init__(self, nc, name):
        self.nc, self.name, self.all = nc, name, []

    def counter(self, name, per=1):
        self.all.append(Counter(self.nc, f"{self.name}_{name}", per))
        return self.all[-1]

    def counters(self, *names, per=1):
        return [self.counter(n, per) for n in names]

    def dmas(self, *names, credits=1):
        new = [DmaCounter(self.nc, f"{self.name}_{n}", credits) for n in names]
        self.all += new
        return new

    def credit(self, eng):
        for s in self.all:
            s.credit(eng)

    def sems(self):
        return [sem for s in self.all for sem in (s.sems if isinstance(s, DmaCounter) else [s.sem])]


def reuse_semaphores(c):
    c.nc.clear_and_free_semaphores([sem for s in c.stages for sem in s.sems()])
    c.stages.clear()
    c.nc.all_engine_barrier()


class Steps:

    def __init__(self, eng, counter):
        self.eng, self.done, self.k = eng, counter, 0

    def start(self, t):
        assert self.k in (0, self.done.per), (self.k, self.done.per)
        self.t, self.k = t, 0

    def mark(self, ins):
        ins.then_inc(*self.done.inc)
        self.k += 1

    def link(self, ins):
        self.mark(ins)
        self.eng.wait_ge(*self.done(self.t, self.k))


def in_pairs(eng, n, body, peel=1):
    assert (n - peel) % 2 == 0
    with eng.Fori(0, (n - peel) // 2) as i:
        for b in range(2):
            body(i * 2 + b, b, True)
    for t in range(n - peel, n):
        body(t, t % 2, t + 2 < n)


def row(ap, t):
    return ap[ds(t, 1)].rearrange("a p n -> (a p) n")


def split_product(nc, out, x_hi, x_lo, w_hi, w_lo, first, last):
    nc.tensor.matmul(out, x_hi, w_hi, start=first, stop=False)
    nc.tensor.matmul(out, x_hi, w_lo, start=False, stop=False)
    return nc.tensor.matmul(out, x_lo, w_hi, start=False, stop=last)




def shape_constants():
    f = np.float32
    i = np.arange(P)
    log_g = np.log(f(1) - f(2) ** (f(-5) - np.arange(HB, dtype=f))).astype(np.float64)
    c = {}
    c["ident"] = np.eye(P)
    dist = i[None, :] - i[:, None]
    decay = np.exp(log_g[None, :, None] * np.maximum(dist, 0)[:, None, :]) * (dist >= 0)[:, None, :]
    same = (i[:, None] // DEC_S == i[None, :] // DEC_S)
    c["decay_p"] = decay
    c["decay_s"] = decay * same[:, None, :]
    c["qdec_p"] = np.broadcast_to(np.exp(log_g[:, None] * (i[None, :] + 1.0)), (P, HB, P))
    c["qdec_s"] = np.broadcast_to(np.exp(log_g[:, None] * (i[None, :] % DEC_S + 1.0)), (P, HB, P))
    c["kdec_p"] = np.exp(log_g[None, :] * (P - 1.0 - i[:, None]))
    ks = np.exp(log_g[None, :] * (DEC_S - 1.0 - i[:, None] % DEC_S))
    own = (i[:, None] // DEC_S == np.arange(DEC_B)[None, :])
    c["kdec_s"] = own[:, :, None] * ks[:, None, :]
    q, k = i[:, None], np.arange(NKB * P)[None, :]
    c["band"] = np.where((q < 64) & (k >= 576) | (q >= 64) & (k < 64), NEG, 0.0)
    c["halfneg"] = np.full((P, 16), -0.5)
    c["before"] = (i[:, None] < i[None, :])
    c["ones"] = np.ones((P, P))
    c["gidx"] = np.broadcast_to(np.arange(NG), (P, NG))
    c["eidx"] = np.broadcast_to(np.arange(NE), (P, NE))
    c["ebase"] = np.broadcast_to(np.arange(NE) * P, (P, NE))
    c["ebase31"] = np.broadcast_to((NE - 1 - np.arange(NE)) * P, (P, NE))
    c["oidx"] = np.broadcast_to(np.arange(OVER), (P, OVER))
    c["blocks"] = np.broadcast_to(np.arange(1, NBLK) * P, (P, NBLK - 1))
    c["block"] = np.broadcast_to(np.arange(IDS), (P, IDS))
    c["slot"] = np.broadcast_to(np.arange(P), (P, P))
    c["one"] = np.ones((P, NE))
    c["token"] = np.arange(NT)[None, :] * P + i[:, None]
    cols, at = [], {}
    n = 0
    for name, a in c.items():
        a = np.asarray(a, f).reshape(P, -1)
        at[name] = (n, a.shape[1])
        n += a.shape[1]
        cols.append(a)
    half = DK // 2
    freqs = (f(10000.0) ** (-np.arange(half, dtype=f) / f(half))).astype(f)
    pos = np.concatenate([np.arange(SEQ), PAST + i % DEC_S]).astype(f)
    ang = (pos[:, None] * freqs[None, :]).astype(f)
    rot = np.stack([np.cos(ang), np.sin(ang)], 1)
    rot = np.stack([rot, rot * f(DK ** -0.5)], 1)
    return np.concatenate(cols, 1), at, rot.reshape(NT, P, 4 * half).astype(f), [float(np.exp(x * P)) for x in log_g], [float(np.exp(x * DEC_S)) for x in log_g]


R1, R2, KV = 0, 24 * 1024, 36 * 1024
IDENT = KV + 9 * 1024
GAINS = IDENT + P
HALF = GAINS + 32
WORK = HALF + 16
ARENA = 52 * 1024 - 128


class Core:

    def __init__(self, nc, ins, outs, const_at, decay_tile, decay_sample):
        self.nc, self.i, self.o = nc, ins, outs
        self.const_at, self.decay_tile, self.decay_sample = const_at, decay_tile, decay_sample
        self.arena = nc.alloc_sbuf_tensor("arena", [P, ARENA], F32)
        self.arena_bytes = nc.sbuf_base - 4 * ARENA
        self.blocks = []
        self.psum = nc.alloc_psum_tensor("psum", [P, 8, BANK], F32)
        scratch = lambda name, shape, dt=F32: nc.dram_tensor(name, shape, dt, kind="Internal").ap()
        self.hT = scratch("hT_scratch", (NT, P, KD * P))
        self.qz = scratch("qz_scratch", (NT, P, HA * P))
        self.bT = scratch("bT_scratch", (NT, P, FB * P))
        self.aT = scratch("aT_scratch", (NT, P, FA * P))
        self.kT_kept = scratch("kT_scratch", (NT, P, FA * P))
        self.skew = scratch("bias_skew_scratch", (HA, P * SKEW))
        self.x1 = scratch("x1_scratch", (NT, P, D))
        self.xn = scratch("xn_scratch", (NT * P, D))
        self.y = scratch("y_scratch", (NBLK * P, D))
        self.kT = self.at(KV, FA, NT * P)
        self.vA = self.at(KV + FA * NT * P, NT, WA)
        self.ident = self.at(IDENT, P)
        self.half = self.at(HALF, 16)
        self.g_mix, self.g_ffn, self.g_ple, self.g_ret = (self.at(GAINS + 8 * n, KD) for n in range(4))
        self.stages = []
        self.holds = nc.alloc_semaphore("holds")
        self.consts_in = nc.alloc_semaphore("consts_in")

    def hold(self, eng):
        eng.sem_inc(self.holds, 1)

    def at(self, off, *dims, parts=P):
        n = int(np.prod(dims))
        assert off + n <= ARENA, (off, dims)
        ap = self.arena[0:parts, off:off + n]
        if len(dims) == 2:
            ap = ap.rearrange("p (a b) -> p a b", a=dims[0])
        if len(dims) == 3:
            ap = ap.rearrange("p (a b c) -> p a b c", a=dims[0], b=dims[1])
        if len(dims) == 4:
            ap = ap.rearrange("p (a b c d) -> p a b c d", a=dims[0], b=dims[1], c=dims[2])
        return ap

    def rounded(self, name, *aps):
        for n, ap in enumerate(aps):
            words = ap.free_size()
            self.blocks = [x for x in self.blocks if x[0] + x[1] <= ap.offset or ap.offset + words <= x[0]]
            self.blocks.append((ap.offset, words, self.nc.alloc_sbuf_tensor_at(
                f"{name}_{n}_rounded", [P, words], F32R, offset=self.arena_bytes + 4 * ap.offset)))

    def exact(self, ap):
        off, words, tensor = next(x for x in self.blocks if x[0] <= ap.offset < x[0] + x[1])
        return bass.AP(tensor=tensor, offset=ap.offset - off, ap=[(words, P)] + list(ap.ap)[1:])

    def high(self, ap):
        return self.exact(ap).bitcast(F32)

    def const(self, name, a=None):
        off, n = self.const_at[name]
        ap = self.i["consts"][:, off:off + n]
        return ap if a is None else ap.rearrange("p (a b) -> p a b", a=a)


class Room:

    def __init__(self, c, off, end=ARENA):
        self.c, self.off, self.end = c, off, end

    def take(self, *dims):
        ap = self.c.at(self.off, *dims)
        self.off += int(np.prod(dims))
        assert self.off <= self.end, (self.off, self.end)
        return ap


def slabs(w, c0, c1):
    return w.rearrange("(k p) n -> p k n", p=P)[:, :, c0:c1]


def gain(g, k0, k1):
    return g[:, k0:k1].unsqueeze(2).to_broadcast([P, k1 - k0, P])


def stage_a(c):
    nc, ps = c.nc, c.psum
    s = Stage(nc, "a")
    c.stages.append(s)
    x_in, hT_stored, k_stored, qz_stored = s.dmas("x_in", "hT_stored", "k_stored", "qz_stored")
    kT_stored, = s.dmas("kT_stored")
    v_stored, = s.dmas("v_stored")
    ssq_ready, ms_ready, rstd_ready, xn_ready = (s.counter(n) for n in ("ssq_ready", "ms_ready", "rstd_ready", "xn_ready"))
    xT_done, hT_ready, qz_ready = (s.counter(n, 2) for n in ("xT_done", "hT_ready", "qz_ready"))
    proj_done = s.counter("proj_done", 3)
    q_out, k_out, v_out, qT_done, kT_done, kT_out = (s.counter(n) for n in ("q_out", "k_out", "v_out", "qT_done", "kT_done", "kT_out"))
    hi_ready, lo_ready = s.counters("hi_ready", "lo_ready", per=2)
    w_hi_ready, w_lo_ready, zeroed, half_in = (nc.alloc_semaphore(f"a_{n}") for n in ("w_hi_ready", "w_lo_ready", "zeroed", "half_in"))
    w_in = [nc.alloc_semaphore(f"a_w{n}_in") for n in range(6)]
    tmp = Room(c, R1 + 16 * 1024, R2)
    x, xn, hT, qz = tmp.take(2, D), tmp.take(2, D), tmp.take(2, KD, P), tmp.take(2, HA, P)
    w, w_hi = c.at(R2, 6, 4 * WA), c.at(R1 + 4 * 1024, 6, 4 * WA)
    work = Room(c, WORK)
    hT_hi, hT_lo = work.take(2, KD, P), work.take(2, KD, P)
    q, k = work.take(WA), work.take(2, WA)
    ssq, ms, rstd = work.take(2), work.take(2), work.take(2)
    zeros = work.take(D)
    zeros_ready, c.y_zeroed = nc.alloc_semaphore("a_zeros_ready"), nc.alloc_semaphore("y_zeroed")
    c.b_qkv_in = [nc.alloc_semaphore(f"b_qkv_in{n}") for n in range(4)]
    c.b_qkv = [c.at(R1 + n * 4 * 1024, KD, BANK) for n in range(4)]
    c.rounded("a_w", *(x[:, n] for x in (w, w_hi) for n in range(6)))
    c.rounded("a_x", hT_hi, hT_lo)

    def load_qkv(eng, n):
        eng.dma_start(c.b_qkv[n], slabs(c.i["w_in"][0], CQB + n * BANK, CQB + (n + 1) * BANK)).then_inc(c.b_qkv_in[n], 16)
    c.load_qkv = load_qkv

    with nc.Block() as block:
        @block.sync
        def _(sp):
            def load(t, b):
                if not (isinstance(t, int) and t == 0):
                    sp.wait_ge(*xn_ready(t - 2))
                sp.dma_start(x[:, b, :], row(c.i["x_all"], t)).then_inc(*x_in.inc(b))

            load(0, 0)
            s.credit(sp)
            sp.dma_start(c.half, c.const("halfneg")).then_inc(half_in, 16)
            sp.dma_start(c.ident, c.const("ident")).then_inc(c.consts_in, 16)
            for g, name in ((c.g_mix, "norm_mix_g"), (c.g_ffn, "norm_ffn_g"), (c.g_ple, "norm_ple_g"),
                            (c.g_ret, "ret_norm_g")):
                sp.dma_start(g, c.i[name][0].rearrange("(k p) -> p k", p=P),
                             allow_slow_non_contiguous=True).then_inc(c.consts_in, 16)
            for n in range(6):
                sp.dma_start(w[:, n, :].rearrange("p (k m) -> p k m", k=4),
                             slabs(c.i["w_in"][0], CQA + n // 2 * WA, CQA + (n // 2 + 1) * WA)[:, 4 * (n % 2):4 * (n % 2) + 4, :]).then_inc(w_in[n], 16)
            load(1, 1)
            c.load_qkv(sp, 0)

            def tile(t, b, ahead):
                if ahead:
                    load(t + 2, b)
                sp.wait_ge(*hT_ready(t))
                sp.dma_start(row(c.hT, t), hT[:, b].rearrange("p k n -> p (k n)")).then_inc(*hT_stored.inc(b))
                if isinstance(t, int) and t == NT - 1:
                    sp.wait_ge(*proj_done(t, 1))
                    c.load_qkv(sp, 1)
                sp.wait_ge(*k_out(t))
                sp.dma_start(row(c.o["k_all"], t), k[:, b, :]).then_inc(*k_stored.inc(b))
                sp.wait_ge(*v_out(t))
                sp.dma_start(row(c.o["v_all"], t), c.vA[:, ds(t, 1), :].rearrange("p a n -> p (a n)")).then_inc(*v_stored.inc(b))
                sp.wait_ge(*qz_ready(t))
                sp.dma_start(row(c.qz, t), qz[:, b].rearrange("p h n -> p (h n)")).then_inc(*qz_stored.inc(b))
                sp.wait_ge(*kT_out(t))
                sp.dma_start(row(c.kT_kept, t).rearrange("p (f n) -> p f n", f=FA), c.kT[:, :, ds(t * P, P)]).then_inc(*kT_stored.inc(b))
            in_pairs(sp, NT, tile, peel=3)
            sp.wait_ge(*hT_stored(NT - 1, 0))
            sp.wait_ge(*hT_stored(NT - 2, 1))
            sp.wait_ge(*k_stored(NT - 1, 0))
            sp.wait_ge(*k_stored(NT - 2, 1))
            sp.wait_ge(*qz_stored(NT - 1, 0))
            sp.wait_ge(*qz_stored(NT - 2, 1))
            sp.wait_ge(*kT_stored(NT - 1, 0))
            sp.wait_ge(*kT_stored(NT - 2, 1))
            sp.wait_ge(*v_stored(NT - 1, 0))
            sp.wait_ge(*v_stored(NT - 2, 1))

        @block.scalar
        def _(act):
            def normalize(t, b):
                act.wait_ge(*x_in(t, b))
                act.wait_ge(*xT_done(t - 2))
                nc.scalar.activation(xn[:, b, :], x[:, b, :], ACT.Square, accum_out=ssq[:, b:b + 1]).then_inc(*ssq_ready.inc)
                act.wait_ge(*rstd_ready(t))
                nc.scalar.activation(xn[:, b, :], x[:, b, :], ACT.Copy, scale=rstd[:, b:b + 1]).then_inc(*xn_ready.inc)

            def hi(t, b):
                act.wait_ge(*proj_done(t - 2))
                for h in range(2):
                    act.wait_ge(*hT_ready(t, h + 1))
                    nc.scalar.activation(c.exact(hT_hi[:, b, 4 * h:4 * h + 4]), hT[:, b, 4 * h:4 * h + 4], ACT.Copy).then_inc(*hi_ready.inc)

            def weights_hi(ns):
                for n in ns:
                    act.wait_ge(w_in[n], 16)
                    nc.scalar.activation(c.exact(w_hi[:, n]), w[:, n], ACT.Copy).then_inc(w_hi_ready, 1)

            def tile(t, b, ahead):
                if ahead or t == NT - 2:
                    normalize(t + 1, 1 - b)
                    hi(t + 1, 1 - b)
                act.wait_ge(*proj_done(t, 1))
                act.wait_ge(*qT_done(t - 1))
                nc.scalar.activation(q, ps[:, 2, :], ACT.Copy).then_inc(*q_out.inc)
                act.wait_ge(*proj_done(t, 2))
                act.wait_ge(*k_stored(t - 2, b))
                nc.scalar.activation(k[:, b, :], ps[:, 3, :], ACT.Copy).then_inc(*k_out.inc)
            normalize(0, 0)
            weights_hi([0])
            hi(0, 0)
            weights_hi(range(1, 6))
            act.wait_ge(zeros_ready, 1)
            for n in range(OVER):
                act.dma_start(c.y[(NE + n) * P:(NE + n + 1) * P, :], zeros).then_inc(c.y_zeroed, 16)
            in_pairs(act, NT, tile, peel=3)
            act.wait_ge(c.y_zeroed, 16 * OVER)

        @block.gpsimd
        def _(pool):
            nc.gpsimd.memset(zeros, 0.0).then_inc(zeros_ready, 1)
            pool.wait_ge(half_in, 16)

            def tile(t, b, ahead):
                pool.wait_ge(*ms_ready(t))
                nc.gpsimd.tensor_tensor(rstd[:, b:b + 1], ms[:, b:b + 1], c.half[:, 0:1], ALU.pow).then_inc(*rstd_ready.inc)
            in_pairs(pool, NT, tile)

        @block.vector
        def _(dve):
            def h_transposed(t, b):
                dve.wait_ge(*ssq_ready(t))
                nc.vector.tensor_scalar(ms[:, b:b + 1], ssq[:, b:b + 1], 1.0 / D, EPS, ALU.mult, ALU.add).then_inc(*ms_ready.inc)
                if isinstance(t, int) and t == 0:
                    dve.wait_ge(c.consts_in, 80)
                for h in range(2):
                    dve.wait_ge(*xT_done(t, h + 1))
                    if h == 0:
                        dve.wait_ge(*hT_stored(t - 2, b))
                    nc.vector.tensor_tensor(hT[:, b, 4 * h:4 * h + 4, :], ps[:, h, :].rearrange("p (k n) -> p k n", k=4),
                                            gain(c.g_mix, 4 * h, 4 * h + 4), ALU.mult).then_inc(*hT_ready.inc)

            def lo(t, b):
                dve.wait_ge(*proj_done(t - 2))
                for h in range(2):
                    part = slice(4 * h, 4 * h + 4)
                    dve.wait_ge(*hi_ready(t, h + 1))
                    nc.vector.tensor_tensor(c.exact(hT_lo[:, b, part]), hT[:, b, part], c.high(hT_hi[:, b, part]), ALU.subtract).then_inc(*lo_ready.inc)

            def weights_lo(ns):
                for n in ns:
                    dve.wait_ge(w_hi_ready, n + 1)
                    nc.vector.tensor_tensor(c.exact(w[:, n]), w[:, n], c.high(w_hi[:, n]), ALU.subtract).then_inc(w_lo_ready, 1)

            def tile(t, b, ahead):
                if ahead or t == NT - 2:
                    h_transposed(t + 1, 1 - b)
                    lo(t + 1, 1 - b)
                dve.wait_ge(*proj_done(t, 3))
                nc.vector.tensor_scalar(c.vA[:, ds(t, 1), :].rearrange("p a n -> p (a n)"), ps[:, 4, :], 1.0, None,
                                        ALU.mult).then_inc(*v_out.inc)
                dve.wait_ge(*qT_done(t))
                dve.wait_ge(*qz_stored(t - 2, b))
                q4 = qz[:, b].rearrange("p (f two) n -> p f two n", two=2)
                s4 = ps[:, 5, :].rearrange("p (f n) -> p f n", f=FA)
                nc.vector.tensor_copy(q4[0:64, :, 0, :], s4[0:64]).then_inc(*qz_ready.inc)
                nc.vector.tensor_copy(q4[64:128, :, 1, :], s4[64:128]).then_inc(*qz_ready.inc)
                dve.wait_ge(*kT_done(t))
                nc.vector.tensor_scalar(c.kT[:, :, ds(t * P, P)], ps[:, 6, :].rearrange("p (f n) -> p f n", f=FA),
                                        1.0, None, ALU.mult).then_inc(*kT_out.inc)
            h_transposed(0, 0)
            weights_lo([0])
            lo(0, 0)
            weights_lo(range(1, 6))
            qzp = qz.rearrange("p b (f two) n -> p (b f) two n", two=2)
            nc.vector.memset(qzp[64:128, :, 0, :], 0.0).then_inc(zeroed, 1)
            nc.vector.memset(qzp[0:64, :, 1, :], 0.0).then_inc(zeroed, 1)
            dve.wait_ge(zeroed, 2)
            in_pairs(dve, NT, tile, peel=3)

        @block.tensor
        def _(pe):
            pe.wait_ge(c.consts_in, 80)

            def transpose_x(t, b):
                pe.wait_ge(*xn_ready(t))
                for h in range(2):
                    pe.wait_ge(*hT_ready(t - 1, h + 1))
                    for kk in range(4 * h, 4 * h + 4):
                        last = nc.tensor.transpose(ps[:, h, (kk % 4) * P:(kk % 4 + 1) * P], xn[:, b, kk * P:(kk + 1) * P], c.ident)
                    last.then_inc(*xT_done.inc)

            def project(t, b, first=False):
                pe.wait_ge(*lo_ready(t))
                for n, out in enumerate((q_out, k_out, v_out)):
                    pe.wait_ge(*out(t - 1))
                    for kk in range(KD):
                        piece, cols = 2 * n + kk // 4, slice(kk % 4 * WA, (kk % 4 + 1) * WA)
                        if first and kk % 4 == 0:
                            pe.wait_ge(w_lo_ready, piece + 1)
                        last = split_product(nc, ps[:, 2 + n, :], c.exact(hT_hi[:, b, kk]), c.exact(hT_lo[:, b, kk]),
                                             c.exact(w_hi[:, piece, cols]), c.exact(w[:, piece, cols]), kk == 0, kk == KD - 1)
                    last.then_inc(*proj_done.inc)

            def tile(t, b, ahead):
                if not (isinstance(t, int) and t == 0):
                    project(t, b)
                if ahead or t == NT - 2:
                    transpose_x(t + 1, 1 - b)
                for src, ready, out, done, bank in ((q, q_out, qz_ready, qT_done, 5), (k[:, b, :], k_out, kT_out, kT_done, 6)):
                    pe.wait_ge(*ready(t))
                    pe.wait_ge(*out(t - 1))
                    for f in range(FA):
                        last = nc.tensor.transpose(ps[:, bank, f * P:(f + 1) * P], src[:, f * P:(f + 1) * P], c.ident)
                    last.then_inc(*done.inc)
            transpose_x(0, 0)
            project(0, 0, first=True)
            tile(0, 0, True)
            with pe.Fori(0, PT // 2 - 1) as i:
                for b in range(2):
                    tile(i * 2 + (1 + b), 1 - b, True)
            for t in range(NT - 2, NT):
                tile(t, t % 2, False)


def rows_normed(c, nc, dve, steps, o_done, ms_ready, rstd_ready, rb_ready, t, o, stats, mv, ms, rstd, rb, between=None):
    for h in range(HB):
        dve.wait_ge(*o_done(t, h // 2 + 1))
        ins = nc.vector.bn_stats(stats[:, h, :], o[:, h, :])
        steps.link(ins) if h == HB - 1 else steps.mark(ins)
    c.hold(dve)
    for h in range(HB):
        ins = nc.vector.bn_aggr(mv[:, h, :], stats[:, h, :])
        steps.link(ins) if h == HB - 1 else steps.mark(ins)
    nc.vector.tensor_scalar(ms, mv[:, :, 1], EPS, None, ALU.add).then_inc(*ms_ready.inc)
    if between:
        between()
    dve.wait_ge(*rstd_ready(t))
    for h in range(HB):
        nc.vector.tensor_scalar(rb[:, h, :], o[:, h, :], mv[:, h, 0:1], rstd[:, h:h + 1], ALU.subtract,
                                ALU.mult).then_inc(*rb_ready.inc)


def stage_b(c):
    nc, ps = c.nc, c.psum
    s = Stage(nc, "b")
    c.stages.append(s)
    hT_in, rot_in, bT_stored = s.dmas("hT_in", "rot_in", "bT_stored")
    proj_done = s.counter("proj_done", 6)
    qr_ready, kr_ready, q_read, k_read, v_out, silu_out, qT_out, o_done, st_done, bT_done, bT_out = s.counters(
        "qr_ready", "kr_ready", "q_read", "k_read", "v_out", "silu_out", "qT_out", "o_done", "st_done", "bT_done", "bT_out", per=2)
    qT_done, kT_done, kT_out, sT_done, sT_out, kd_ready, ms_ready, rstd_ready, b_ready = s.counters(
        "qT_done", "kT_done", "kT_out", "sT_done", "sT_out", "kd_ready", "ms_ready", "rstd_ready", "b_ready")
    state_out, rb_ready = s.counters("state_out", "rb_ready", per=4)
    norm_steps = s.counter("norm_steps", 8)
    g_in, tables_in, zeroed, state_stored = (nc.alloc_semaphore(f"b_{n}") for n in ("g_in", "tables_in", "zeroed", "state_stored"))
    c.b2_states_in = [nc.alloc_semaphore(f"b2_states_in{n}") for n in range(2)]
    wg = c.at(R1 + 16 * 1024, KD, 1024)
    room = Room(c, R2, KV)
    hT, v, sg = room.take(2, KD, P), room.take(2, VB), room.take(2, VB)
    tq, tk = room.take(2, QKB), room.take(2, QKB)
    rb, bg, state = room.take(HB, DV), room.take(VB), room.take(HB, DV)
    work = Room(c, WORK)
    qr, kr, kd, qT, qdT, kT, sT = (work.take(QKB) for _ in range(7))
    rot = work.take(2, 4, DK // 2)
    qdec = work.take(QKB)
    stats, mv, ms, rstd = work.take(HB, 6), work.take(HB, 2), work.take(HB), work.take(HB)
    kdec = work.take(HB)
    bT = room.take(FB, P)
    decay = work.take(QKB)
    work.off = -(-work.off // 8) * 8
    v_hi, hT_hi, hT_lo = c.at(KV, 4, 4 * BANK), c.at(KV + 8 * 1024, KD, P), work.take(KD, P)
    v_raw = c.at(R1 + 8 * 1024, 4, 4 * BANK)
    c.rounded("b_w", *(x[:, n] for x in (v_raw, v_hi) for n in range(4)))
    c.rounded("b_x", hT_hi, hT_lo)
    hi_ready, lo_ready = s.counters("hi_ready", "lo_ready")
    w_hi_ready, w_lo_ready, c.kv_in = (nc.alloc_semaphore(f"b_{n}") for n in ("w_hi_ready", "w_lo_ready", "kv_in"))
    c.tile8 = dict(qr=qr, kr=kr, v=v[:, 0, :], sg=sg[:, 0, :])
    bank_of = (0, 1, 2, 3, 0, 1)
    o = ps[:, 6:8, :].rearrange("p a (h n) -> p (a h) n", h=2)

    with nc.Block() as block:
        @block.sync
        def _(sp):
            def load(t, b):
                if isinstance(t, int) and t == 0:
                    sp.dma_start(hT[:, b].rearrange("p k n -> p (k n)"), row(c.hT, t)).then_inc(*hT_in.inc(b))
                    sp.dma_start(rot[:, b].rearrange("p a n -> p (a n)"), row(c.i["rot"], t)).then_inc(*rot_in.inc(b))
                    return
                sp.wait_ge(*proj_done(t - 2))
                sp.dma_start(hT[:, b].rearrange("p k n -> p (k n)"), row(c.hT, t)).then_inc(*hT_in.inc(b))
                sp.wait_ge(*k_read(t - 2))
                sp.dma_start(rot[:, b].rearrange("p a n -> p (a n)"), row(c.i["rot"], t)).then_inc(*rot_in.inc(b))

            load(0, 0)
            s.credit(sp)
            c.load_qkv(sp, 2)
            c.load_qkv(sp, 3)
            for kk in range(KD):
                sp.dma_start(wg[:, kk, :], slabs(c.i["w_in"][0], CGB, CGA)[:, kk, :]).then_inc(g_in, 16)
            sp.dma_start(decay, c.const("decay_p")).then_inc(tables_in, 16)
            sp.dma_start(qdec, c.const("qdec_p")).then_inc(tables_in, 16)
            sp.dma_start(kdec, c.const("kdec_p")).then_inc(tables_in, 16)
            load(1, 1)

            def store(r, b):
                sp.wait_ge(*bT_out(r))
                sp.dma_start(row(c.bT, r), bT.rearrange("p k n -> p (k n)")).then_inc(*bT_stored.inc(b))

            with sp.Fori(0, 3) as i:
                for b in range(2):
                    t = i * 2 + (1 + b)
                    load(t + 1, b)
                    store(t - 1, b)
            load(8, 0)
            store(6, 0)
            sp.wait_ge(*proj_done(NT - 1, 4))
            for n in range(DEC_B):
                sp.dma_start(c.at(R1 + n * D, HB, DV), c.i["state_ret"][0, n].rearrange("h d e -> d h e")).then_inc(
                    c.b2_states_in[n // 4], 16)
            sp.wait_ge(*state_out(PT - 1))
            sp.dma_start(c.o["state_p"].rearrange("h d e -> d h e"), state).then_inc(state_stored, 16)
            store(7, 1)
            sp.wait_ge(*bT_stored(6, 0))
            sp.wait_ge(*bT_stored(7, 1))
            sp.wait_ge(state_stored, 16)

        @block.scalar
        def _(act):
            def hi(t, b):
                act.wait_ge(*hT_in(t, b))
                act.wait_ge(*proj_done(t - 1, 4))
                nc.scalar.activation(c.exact(hT_hi), hT[:, b], ACT.Copy).then_inc(*hi_ready.inc)

            hi(0, 0)
            for n in range(4):
                act.wait_ge(c.b_qkv_in[2 + n // 2], 16)
                nc.scalar.activation(c.exact(v_hi[:, n]), v_raw[:, n], ACT.Copy).then_inc(w_hi_ready, 1)

            def tile(t, b):
                if not (isinstance(t, int) and t == 0):
                    hi(t, b)
                for h in range(2):
                    act.wait_ge(*proj_done(t, 3 + h))
                    act.wait_ge(*st_done(t - 2))
                    nc.scalar.activation(v[:, b, h * BANK:(h + 1) * BANK], ps[:, 2 + h, :], ACT.Copy).then_inc(*v_out.inc)
                for h in range(2):
                    act.wait_ge(*proj_done(t, 5 + h))
                    act.wait_ge(*b_ready(t - 2))
                    nc.scalar.activation(sg[:, b, h * BANK:(h + 1) * BANK], ps[:, h, :], ACT.Silu).then_inc(*silu_out.inc)
            tile(0, 0)
            with act.Fori(0, PT // 2) as i:
                for b in range(2):
                    tile(i * 2 + (1 + b), 1 - b)

        @block.gpsimd
        def _(pool):
            pool.wait_ge(tables_in, 48)

            def rotated(t, tmp, read, dst, last_use, ready):
                a, bb = (tmp[:, n, :].rearrange("p (h two d) -> p h two d", h=HB, two=2) for n in range(2))
                d = dst.rearrange("p (h two d) -> p h two d", h=HB, two=2)
                pool.wait_ge(*read(t))
                pool.wait_ge(*last_use(t - 1))
                nc.gpsimd.tensor_tensor(d[:, :, 0, :], a[:, :, 0, :], bb[:, :, 1, :], ALU.subtract).then_inc(*ready.inc)
                nc.gpsimd.tensor_tensor(d[:, :, 1, :], a[:, :, 1, :], bb[:, :, 0, :], ALU.add).then_inc(*ready.inc)

            def project_part(t):
                rotated(t, tq, q_read, qr, qT_done, qr_ready)
                pool.wait_ge(*kd_ready(t - 1))
                rotated(t, tk, k_read, kr, kT_done, kr_ready)

            def retain_part(r, b):
                pool.wait_ge(*ms_ready(r))
                nc.gpsimd.tensor_tensor(rstd, ms, c.half[:, 0:HB], ALU.pow).then_inc(*rstd_ready.inc)
                pool.wait_ge(*rb_ready(r))
                pool.wait_ge(*silu_out(r))
                pool.wait_ge(*bT_done(r - 1))
                nc.gpsimd.tensor_tensor(bg, rb.rearrange("p h n -> p (h n)"), sg[:, b, :], ALU.mult).then_inc(*b_ready.inc)

            def decayed(t):
                pool.wait_ge(*kr_ready(t))
                pool.wait_ge(*st_done(t - 1))
                nc.gpsimd.tensor_tensor(kd.rearrange("p (h n) -> p h n", h=HB), kr.rearrange("p (h n) -> p h n", h=HB),
                                        kdec.unsqueeze(2).to_broadcast([P, HB, DK]), ALU.mult).then_inc(*kd_ready.inc)

            project_part(0)
            decayed(0)
            with pool.Fori(0, PT // 2) as i:
                for b in range(2):
                    t = i * 2 + (1 + b)
                    project_part(t)
                    retain_part(t - 1, b)
                    decayed(t)

        @block.vector
        def _(dve):
            steps = Steps(dve, norm_steps)
            nc.vector.memset(state, 0.0).then_inc(zeroed, 1)
            dve.wait_ge(zeroed, 1)

            def rotate(t, b, bank, tmp, part, read, ready):
                src = ps[:, bank, :].rearrange("p (h d) -> p h d", h=2 * HB)
                dve.wait_ge(*proj_done(t, bank + 1))
                dve.wait_ge(*rot_in(t, b))
                dve.wait_ge(*ready(t - 1))
                for n in range(2):
                    nc.vector.tensor_tensor(tmp[:, n, :].rearrange("p (h d) -> p h d", h=2 * HB), src,
                                            rot[:, b, 2 * part + n, :].unsqueeze(1).to_broadcast([P, 2 * HB, DK // 2]),
                                            ALU.mult).then_inc(*read.inc)

            def retain(r, b, between):
                dve.wait_ge(*qT_done(r))
                dve.wait_ge(*o_done(r - 1))
                nc.vector.tensor_copy(qT, ps[:, 4, :]).then_inc(*qT_out.inc)
                nc.vector.tensor_tensor(qdT, ps[:, 4, :], qdec, ALU.mult).then_inc(*qT_out.inc)
                between()
                dve.wait_ge(*kT_done(r))
                nc.vector.tensor_copy(kT, ps[:, 5, :]).then_inc(*kT_out.inc)
                dve.wait_ge(*sT_done(r))
                nc.vector.tensor_tensor(sT, ps[:, 4, :], decay, ALU.mult).then_inc(*sT_out.inc)

                def states():
                    for h in range(HB):
                        dve.wait_ge(*st_done(r, h // 2 + 1))
                        dve.wait_ge(*state_out(r - 1))
                        nc.vector.scalar_tensor_tensor(
                            state[:, h, :], state[:, h, :], c.decay_tile[h],
                            ps[:, 4 + h // 2, (h % 2) * DV:(h % 2 + 1) * DV], ALU.mult, ALU.add).then_inc(*state_out.inc)
                steps.start(r)
                dve.wait_ge(*b_ready(r - 1))
                rows_normed(c, nc, dve, steps, o_done, ms_ready, rstd_ready, rb_ready, r, o, stats, mv, ms, rstd, rb, states)
                for h in range(2):
                    dve.wait_ge(*bT_done(r, h + 1))
                    dve.wait_ge(*bT_stored(r - 1, 1 - b))
                    nc.vector.tensor_tensor(bT[:, 4 * h:4 * h + 4, :], ps[:, 4 + h, :].rearrange("p (k n) -> p k n", k=4),
                                            gain(c.g_ret, 4 * h, 4 * h + 4), ALU.mult).then_inc(*bT_out.inc)

            def lo(t, b):
                dve.wait_ge(*hi_ready(t))
                nc.vector.tensor_tensor(c.exact(hT_lo), hT[:, b], c.high(hT_hi), ALU.subtract).then_inc(*lo_ready.inc)

            def weights_lo(ns):
                for n in ns:
                    dve.wait_ge(w_hi_ready, n + 1)
                    nc.vector.tensor_tensor(c.exact(v_raw[:, n]), v_raw[:, n], c.high(v_hi[:, n]), ALU.subtract).then_inc(w_lo_ready, 1)

            lo(0, 0)
            rotate(0, 0, 0, tq, 0, q_read, qr_ready)
            weights_lo(range(2))
            rotate(0, 0, 1, tk, 1, k_read, kr_ready)
            weights_lo(range(2, 4))
            dve.wait_ge(tables_in, 48)
            with dve.Fori(0, PT // 2) as i:
                for b in range(2):
                    t = i * 2 + (1 + b)
                    lo(t, 1 - b)
                    rotate(t, 1 - b, 0, tq, 0, q_read, qr_ready)
                    retain(t - 1, b, lambda: rotate(t, 1 - b, 1, tk, 1, k_read, kr_ready))

        @block.tensor
        def _(pe):
            def project(t, b, n):
                if n == 0:
                    pe.wait_ge(*hT_in(t, b))
                pe.wait_ge(*(silu_out(t - 1, 1), silu_out(t - 1, 2), v_out(t - 1, 1), v_out(t - 1, 2), q_read(t), k_read(t))[n])
                if n in (2, 3):
                    pe.wait_ge(*lo_ready(t))
                    for kk in range(KD):
                        piece, cols = 2 * (n - 2) + kk // 4, slice(kk % 4 * BANK, (kk % 4 + 1) * BANK)
                        last = split_product(nc, ps[:, bank_of[n], :], c.exact(hT_hi[:, kk]), c.exact(hT_lo[:, kk]),
                                             c.exact(v_hi[:, piece, cols]), c.exact(v_raw[:, piece, cols]), kk == 0, kk == KD - 1)
                    last.then_inc(*proj_done.inc)
                    return
                w = c.b_qkv[n] if n < 4 else wg[:, :, (n - 4) * BANK:(n - 3) * BANK]
                for kk in range(KD):
                    last = nc.tensor.matmul(ps[:, bank_of[n], :], hT[:, b, kk, :], w[:, kk, :], start=kk == 0, stop=kk == KD - 1)
                last.then_inc(*proj_done.inc)

            def q_transposed(r, b):
                pe.wait_ge(*qr_ready(r))
                pe.wait_ge(*bT_out(r - 1, 1))
                for h in range(HB):
                    last = nc.tensor.transpose(ps[:, 4, h * P:(h + 1) * P], qr[:, h * P:(h + 1) * P], c.ident)
                last.then_inc(*qT_done.inc)

            def k_transposed(r, b):
                pe.wait_ge(*kr_ready(r))
                pe.wait_ge(*bT_out(r - 1, 2))
                for h in range(HB):
                    last = nc.tensor.transpose(ps[:, 5, h * P:(h + 1) * P], kr[:, h * P:(h + 1) * P], c.ident)
                last.then_inc(*kT_done.inc)

            def scores(r, b):
                pe.wait_ge(*qT_out(r))
                pe.wait_ge(*kT_out(r))
                for h in range(HB):
                    last = nc.tensor.matmul(ps[:, 4, h * P:(h + 1) * P], kT[:, h * P:(h + 1) * P], qT[:, h * P:(h + 1) * P],
                                            start=True, stop=True)
                last.then_inc(*sT_done.inc)

            def outputs(r, b):
                pe.wait_ge(*sT_out(r))
                pe.wait_ge(*v_out(r))
                pe.wait_ge(*state_out(r - 1))
                pe.wait_ge(*rb_ready(r - 1))
                for h in range(HB):
                    nc.tensor.matmul(o[:, h, :], sT[:, h * P:(h + 1) * P], v[:, b, h * DV:(h + 1) * DV], start=True, stop=False)
                    last = nc.tensor.matmul(o[:, h, :], qdT[:, h * P:(h + 1) * P], state[:, h, :], start=False, stop=True)
                    if h % 2:
                        last.then_inc(*o_done.inc)

            def states(r, b):
                pe.wait_ge(*kd_ready(r))
                for h in range(HB):
                    last = nc.tensor.matmul(ps[:, 4 + h // 2, (h % 2) * DV:(h % 2 + 1) * DV], kd[:, h * P:(h + 1) * P],
                                            v[:, b, h * DV:(h + 1) * DV], start=True, stop=True)
                    if h % 2:
                        last.then_inc(*st_done.inc)

            def gated_transposed(r, b):
                pe.wait_ge(*b_ready(r))
                for h in range(2):
                    pe.wait_ge(*state_out(r, 2 * h + 2))
                    for f in range(4 * h, 4 * h + 4):
                        last = nc.tensor.transpose(ps[:, 4 + h, (f % 4) * P:(f % 4 + 1) * P], bg[:, f * P:(f + 1) * P], c.ident)
                    last.then_inc(*bT_done.inc)

            for n in range(4):
                pe.wait_ge(*((c.b_qkv_in[n], 16) if n < 2 else (w_lo_ready, 2 * n - 2)))
                project(0, 0, n)
            pe.wait_ge(g_in, 16 * KD)
            for n in range(4, 6):
                project(0, 0, n)
            with pe.Fori(0, PT // 2) as i:
                for b in range(2):
                    t = i * 2 + (1 + b)
                    for n, retain in enumerate((q_transposed, k_transposed, scores, outputs, states, gated_transposed)):
                        project(t, 1 - b, n)
                        retain(t - 1, b)


def stage_b2(c):
    nc, ps = c.nc, c.psum
    s = Stage(nc, "b2")
    c.stages.append(s)
    qT_done, kT_done, sT_done, qT_out, sT_out, ms_ready, rstd_ready, b_ready = s.counters(
        "qT_done", "kT_done", "sT_done", "qT_out", "sT_out", "ms_ready", "rstd_ready", "b_ready")
    o_done, bT_done, bT_out = s.counters("o_done", "bT_done", "bT_out", per=2)
    km_ready = s.counter("km_ready", DEC_B)
    rb_ready, qm_out = s.counters("rb_ready", "qm_out", per=HB)
    st_done = s.counter("st_done", DEC_B)
    st_out = s.counter("st_out", DEC_B * HB)
    norm_steps = s.counter("norm_steps", 8)
    kT_out = s.counter("kT_out")
    tables_in, zeroed, stored = (nc.alloc_semaphore(f"b2_{n}") for n in ("tables_in", "zeroed", "stored"))
    room = Room(c, R1, R2)
    st = room.take(DEC_B, HB, DV)
    pitch = P + DEC_S
    qm = room.take(HB, DEC_B * pitch)
    km = room.take(DEC_B, HB, DK)
    qT, kT, sT, decay, qdec = (room.take(QKB) for _ in range(5))
    kdec = room.take(DEC_B, HB)
    rb, bg, bT = room.take(HB, DV), room.take(VB), room.take(FB, P)
    stats, mv, ms, rstd = room.take(HB, 6), room.take(HB, 2), room.take(HB), room.take(HB)
    qr, kr, v, sg = (c.tile8[n] for n in ("qr", "kr", "v", "sg"))
    o = ps[:, 3:5, :].rearrange("p a (h n) -> p (a h) n", h=2)

    table, skewed = c.at(WORK + 2 * QKB, HA, 2 * CLIP + 1), c.at(R2 + 6 * 1024, HA, SKEW)
    c.bias, band = c.at(WORK + 2 * QKB, HA, NKB * P), c.at(R2, NKB * P)
    table_in, skewed_done, skew_stored, bias_in = (nc.alloc_semaphore(f"b2_{n}") for n in ("table_in", "skewed_done", "skew_stored", "bias_in"))
    c.bias_ready = nc.alloc_semaphore("bias_ready")

    def state_banks(n):
        return (5, 6) if n % 2 == 0 else (7, 2)

    with nc.Block() as block:
        @block.sync
        def _(sp):
            s.credit(sp)
            for dst, name in ((decay, "decay_s"), (qdec, "qdec_s")):
                sp.dma_start(dst, c.const(name)).then_inc(tables_in, 16)
            sp.dma_start(kdec, c.const("kdec_s", DEC_B)).then_inc(tables_in, 16)
            for t in range(NT):
                sp.dma_start(c.kT[:, :, t * P:(t + 1) * P], c.kT_kept[t].rearrange("p (f n) -> p f n", f=FA)).then_inc(c.kv_in, 16)
            sp.dma_start(c.vA, c.o["v_all"].rearrange("t p n -> p t n")).then_inc(c.kv_in, 16)
            for n in range(DEC_B):
                sp.wait_ge(*st_out(0, HB * (n + 1)))
                sp.dma_start(c.o["state_s"][n].rearrange("h d e -> d h e"), st[:, n]).then_inc(stored, 16)
            sp.wait_ge(*bT_out(0))
            sp.dma_start(row(c.bT, NT - 1), bT.rearrange("p k n -> p (k n)")).then_inc(stored, 16)
            c.b2_stored = (stored, 16 * (DEC_B + 1))

        @block.scalar
        def _(act):
            act.dma_start(table, c.i["rel_reversed"].unsqueeze(0).to_broadcast([P, HA, 2 * CLIP + 1])).then_inc(table_in, 16)
            act.dma_start(band, c.const("band")).then_inc(bias_in, 16)
            act.wait_ge(table_in, 16)
            far = BAND - 1
            nc.scalar.activation(skewed[:, :, 0:far], table[:, :, 0:1].to_broadcast([P, HA, far]), ACT.Copy).then_inc(skewed_done, 1)
            nc.scalar.activation(skewed[:, :, far:SKEW], table, ACT.Copy).then_inc(skewed_done, 1)
            act.wait_ge(skewed_done, 2)
            act.dma_start(c.skew.rearrange("h (p n) -> p h n", p=P), skewed).then_inc(skew_stored, 16)
            act.wait_ge(skew_stored, 16)
            act.dma_start(c.bias, bass.AP(tensor=c.skew.tensor, offset=P - 1, ap=[[SKEW - 1, P], [P * SKEW, HA], [1, NKB * P]])).then_inc(
                bias_in, 16)
            act.wait_ge(bias_in, 32)

        @block.gpsimd
        def _(pool):
            nc.gpsimd.memset(qm, 0.0).then_inc(zeroed, 1)
            pool.wait_ge(tables_in, 48)
            for n in range(DEC_B):
                nc.gpsimd.tensor_tensor(km[:, n], kr.rearrange("p (h n) -> p h n", h=HB),
                                        kdec[:, n, :].unsqueeze(2).to_broadcast([P, HB, DK]), ALU.mult).then_inc(*km_ready.inc)
            pool.wait_ge(*ms_ready(0))
            nc.gpsimd.tensor_tensor(rstd, ms, c.half[:, 0:HB], ALU.pow).then_inc(*rstd_ready.inc)
            pool.wait_ge(*rb_ready(0))
            nc.gpsimd.tensor_tensor(bg, rb.rearrange("p h n -> p (h n)"), sg, ALU.mult).then_inc(*b_ready.inc)
            pool.wait_ge(bias_in, 32)
            nc.gpsimd.tensor_tensor(c.bias, c.bias, band.unsqueeze(1).to_broadcast([P, HA, NKB * P]), ALU.add).then_inc(c.bias_ready, 1)

        @block.vector
        def _(dve):
            steps = Steps(dve, norm_steps)
            dve.wait_ge(*qT_done(0))
            nc.vector.tensor_copy(qT, ps[:, 0, :]).then_inc(*qT_out.inc)
            dve.wait_ge(*kT_done(0))
            nc.vector.tensor_copy(kT, ps[:, 1, :]).then_inc(*kT_out.inc)
            dve.wait_ge(zeroed, 1)
            dve.wait_ge(tables_in, 48)
            for h in range(HB):
                nc.vector.tensor_tensor(qm[:, h].rearrange("p (b x) -> p b x", b=DEC_B)[:, :, 0:DEC_S],
                                        ps[:, 0, h * P:(h + 1) * P].rearrange("p (b x) -> p b x", b=DEC_B),
                                        qdec[:, h * P:(h + 1) * P].rearrange("p (b x) -> p b x", b=DEC_B),
                                        ALU.mult).then_inc(*qm_out.inc)
            dve.wait_ge(*sT_done(0))
            nc.vector.tensor_tensor(sT, ps[:, 2, :], decay, ALU.mult).then_inc(*sT_out.inc)

            def states():
                for n in range(DEC_B):
                    dve.wait_ge(*st_done(0, n + 1))
                    for h in range(HB):
                        new = ps[:, state_banks(n)[h // 2], (h % 2) * DV:(h % 2 + 1) * DV]
                        nc.vector.scalar_tensor_tensor(st[:, n, h, :], st[:, n, h, :], c.decay_sample[h], new,
                                                       ALU.mult, ALU.add).then_inc(*st_out.inc)
            steps.start(0)
            rows_normed(c, nc, dve, steps, o_done, ms_ready, rstd_ready, rb_ready, 0, o, stats, mv, ms, rstd, rb)
            states()
            for h in range(2):
                dve.wait_ge(*bT_done(0, h + 1))
                nc.vector.tensor_tensor(bT[:, 4 * h:4 * h + 4, :], ps[:, h, :].rearrange("p (k n) -> p k n", k=4),
                                        gain(c.g_ret, 4 * h, 4 * h + 4), ALU.mult).then_inc(*bT_out.inc)

        @block.tensor
        def _(pe):
            for src, done, bank in ((qr, qT_done, 0), (kr, kT_done, 1)):
                for h in range(HB):
                    last = nc.tensor.transpose(ps[:, bank, h * P:(h + 1) * P], src[:, h * P:(h + 1) * P], c.ident)
                last.then_inc(*done.inc)
            pe.wait_ge(*qT_out(0))
            pe.wait_ge(*kT_out(0))
            for h in range(HB):
                last = nc.tensor.matmul(ps[:, 2, h * P:(h + 1) * P], kT[:, h * P:(h + 1) * P], qT[:, h * P:(h + 1) * P],
                                        start=True, stop=True)
            last.then_inc(*sT_done.inc)
            pe.wait_ge(*sT_out(0))
            for n in range(2):
                pe.wait_ge(c.b2_states_in[n], 16 * 4)
            for h in range(HB):
                nc.tensor.matmul(o[:, h, :], sT[:, h * P:(h + 1) * P], v[:, h * DV:(h + 1) * DV], start=True, stop=False)
                pe.wait_ge(*qm_out(0, h + 1))
                for n in range(DEC_B):
                    last = nc.tensor.matmul(o[:, h, :], qm[:, h, n * P:(n + 1) * P], st[:, n, h, :], start=False,
                                            stop=n == DEC_B - 1)
                if h % 2:
                    last.then_inc(*o_done.inc)
            for n in range(DEC_B):
                pe.wait_ge(*km_ready(0, n + 1))
                if n >= 2:
                    pe.wait_ge(*st_out(0, HB * (n - 1)))
                for h in range(HB):
                    last = nc.tensor.matmul(ps[:, state_banks(n)[h // 2], (h % 2) * DV:(h % 2 + 1) * DV], km[:, n, h, :],
                                            v[:, h * DV:(h + 1) * DV], start=True, stop=True)
                last.then_inc(*st_done.inc)
            pe.wait_ge(*b_ready(0))
            for h in range(2):
                for f in range(4 * h, 4 * h + 4):
                    last = nc.tensor.transpose(ps[:, h, (f % 4) * P:(f % 4 + 1) * P], bg[:, f * P:(f + 1) * P], c.ident)
                last.then_inc(*bT_done.inc)


SCALE = HDA ** -0.5


def stage_c(c):
    nc, ps = c.nc, c.psum
    s = Stage(nc, "c")
    c.stages.append(s)
    qz_in, aT_stored = s.dmas("qz_in", "aT_stored")
    s_done, s_out, max_ready, p_ready, pT_done, pT_out, pv_done = s.counters(
        "s_done", "s_out", "max_ready", "p_ready", "pT_done", "pT_out", "pv_done", per=HA)
    inv_ready, a_out, aT_done, aT_out = s.counters("inv_ready", "a_out", "aT_done", "aT_out")
    W = c.merge_weights = MergeWeights(c)
    room = Room(c, R2, KV)
    qz, S, Pr = room.take(2, HA, P), room.take(2, NKB * P), room.take(2, NKB * P)
    pT = room.take(2, NKB, P)
    a, aT = room.take(HA, HDA), room.take(2, FA, P)
    nmax, rsum, rinv = room.take(HA), room.take(2, HA), room.take(HA)
    pT_banks = ps[:, 4:6, :].rearrange("p a n -> p (a n)")

    def s_banks(h):
        return ps[:, 2 * (h % 2):2 * (h % 2) + 2, :].rearrange("p a n -> p (a n)")

    def runs(eng, run):
        full = NKB - 1
        run([(t, t % 2, t + 1) for t in range(full)])
        with eng.Fori(0, (PT - full) // 2) as i:
            run([(i * 2 + (full + b), b, NKB) for b in range(2)])

    def steps_of(run):
        return [(t, h, b, nb) for t, b, nb in run for h in range(HA)]

    with nc.Block() as block:
        @block.sync
        def _(sp):
            s.credit(sp)

            def load(t, b):
                sp.wait_ge(*s_done(t - 2))
                sp.dma_start(qz[:, b].rearrange("p h n -> p (h n)"), row(c.qz, t)).then_inc(*qz_in.inc(b))

            load(0, 0)
            def tile(t, b, nb):
                if isinstance(t, int):
                    if t < NKB - 2:
                        load(t + 1, 1 - b)
                    if t == 0:
                        sp.wait_ge(*c.b2_stored)
                    for n in range(2 * t, min(2 * t + 2, W.pieces)):
                        W.load(sp, n, 0)
                else:
                    load(t, b)
            runs(sp, lambda run: [tile(*x) for x in run])
            sp.wait_ge(*aT_stored(PT - 2, 0))
            sp.wait_ge(*aT_stored(PT - 1, 1))

        @block.vector
        def _(dve):
            dve.wait_ge(c.bias_ready, 1)

            def head(t, h, b, nb):
                n = nb * P
                dve.wait_ge(*s_done(t, h + 1))
                dve.wait_ge(*p_ready(t, h - 1))
                nc.vector.scalar_tensor_tensor(S[:, h % 2, 0:n], s_banks(h)[:, 0:n], SCALE, c.bias[:, h, NKB * P - n:], ALU.mult,
                                               ALU.add).then_inc(*s_out.inc)
                dve.wait_ge(*s_out(t, h + 1))
                nc.vector.reduce_max(nmax[:, h:h + 1], S[:, h % 2, 0:n], AX.X, negate=True).then_inc(*max_ready.inc)

            def output(t, b):
                dve.wait_ge(*p_ready(t))
                dve.wait_ge(*a_out(t - 1))
                nc.vector.reciprocal(rinv, rsum[:, b, :]).then_inc(*inv_ready.inc)
                dve.wait_ge(*inv_ready(t))
                dve.wait_ge(*pv_done(t))
                dve.wait_ge(*aT_done(t - 1))
                nc.vector.tensor_tensor(a, ps[:, 6, :].rearrange("p (h d) -> p h d", h=HA),
                                        rinv.unsqueeze(2).to_broadcast([P, HA, HDA]), ALU.mult).then_inc(*a_out.inc)

            def run(tiles):
                for n, (t, b, nb) in enumerate(tiles):
                    for h in range(HA):
                        head(t, h, b, nb)
                        if n and h == 1:
                            output(*tiles[n - 1][:2])
                output(*tiles[-1][:2])
            runs(dve, run)

        @block.scalar
        def _(act):
            def transposed(t, h, b, nb):
                act.wait_ge(*pT_done(t, h + 1))
                act.wait_ge(*pv_done(t, h - 1))
                nc.scalar.activation(pT[:, h % 2, 0:nb, :].rearrange("p k n -> p (k n)"), pT_banks[:, 0:nb * P], ACT.Copy).then_inc(*pT_out.inc)

            def weights(t, h, b, nb):
                act.wait_ge(*max_ready(t, h + 1))
                act.wait_ge(*pT_done(t, h - 1))
                nc.scalar.activation(Pr[:, h % 2, 0:nb * P], S[:, h % 2, 0:nb * P], ACT.Exp, bias=nmax[:, h:h + 1],
                                     accum_out=rsum[:, b, h:h + 1]).then_inc(*p_ready.inc)

            def output(t, b):
                act.wait_ge(*aT_done(t))
                act.wait_ge(*aT_stored(t - 2, b))
                nc.scalar.activation(aT[:, b].rearrange("p f n -> p (f n)"), ps[:, 7, :], ACT.Copy).then_inc(*aT_out.inc)
                act.wait_ge(*aT_out(t))
                act.dma_start(row(c.aT, t), aT[:, b].rearrange("p f n -> p (f n)")).then_inc(*aT_stored.inc(b))

            def run(tiles):
                steps = steps_of(tiles)
                for n in range(len(steps) + 1):
                    if n < len(steps):
                        weights(*steps[n])
                    if n:
                        transposed(*steps[n - 1])
                    if n % HA == 2 and n > HA:
                        output(*tiles[n // HA - 1][:2])
                output(*tiles[-1][:2])
            runs(act, run)

        @block.tensor
        def _(pe):
            pe.wait_ge(c.kv_in, 16 * (NT + 1))

            def scores(t, h, b, nb):
                if h == 0:
                    pe.wait_ge(*qz_in(t, b))
                pe.wait_ge(*s_out(t, h - 1))
                n = min(nb * P, BANK)
                k0 = t * P - (nb - 1) * P
                last = nc.tensor.matmul(s_banks(h)[:, 0:n], qz[:, b, h, :], c.kT[:, h // 2, ds(k0, n)], start=True, stop=True)
                if nb == NKB:
                    last = nc.tensor.matmul(s_banks(h)[:, n:n + P], qz[:, b, h, :], c.kT[:, h // 2, ds(k0 + n, P)], start=True, stop=True)
                last.then_inc(*s_done.inc)

            def transposed(t, h, b, nb):
                pe.wait_ge(*p_ready(t, h + 1))
                pe.wait_ge(*pT_out(t, h))
                for k in range(nb):
                    last = nc.tensor.transpose(pT_banks[:, k * P:(k + 1) * P], Pr[:, h % 2, k * P:(k + 1) * P], c.ident)
                last.then_inc(*pT_done.inc)

            def weighted(t, h, b, nb):
                if h == 0:
                    pe.wait_ge(*a_out(t - 1))
                pe.wait_ge(*pT_out(t, h + 1))
                for k in range(nb):
                    last = nc.tensor.matmul(ps[:, 6, h * HDA:(h + 1) * HDA], pT[:, h % 2, k, :],
                                            c.vA[:, ds(t - (nb - 1) + k, 1), h * HDA:(h + 1) * HDA].rearrange("p a n -> p (a n)"),
                                            start=k == 0, stop=k == nb - 1)
                last.then_inc(*pv_done.inc)

            def output(t):
                pe.wait_ge(*a_out(t))
                pe.wait_ge(*aT_out(t - 1))
                for f in range(FA):
                    last = nc.tensor.transpose(ps[:, 7, f * P:(f + 1) * P], a[:, 2 * f:2 * f + 2, :].rearrange("p h d -> p (h d)"), c.ident)
                last.then_inc(*aT_done.inc)

            def run(tiles):
                steps = steps_of(tiles)
                for n in range(len(steps) + 2):
                    if n < len(steps):
                        scores(*steps[n])
                    if 1 <= n <= len(steps):
                        transposed(*steps[n - 1])
                    if n >= 2:
                        weighted(*steps[n - 2])
                    if n % HA == 2 and n > HA:
                        output(tiles[n // HA - 1][0])
                output(tiles[-1][0])
            runs(pe, run)


def stage_c2(c):
    nc, ps = c.nc, c.psum
    s = Stage(nc, "c2")
    c.stages.append(s)
    k_in, v_in = s.dmas("k_in", "v_in")
    vn_in = s.dmas("vn_in")[0]
    s_done, s_out, max_ready, p_ready, inv_ready, pn_ready, pT_done, pv_done = s.counters(
        "s_done", "s_out", "max_ready", "p_ready", "inv_ready", "pn_ready", "pT_done", "pv_done")
    kT_done, kT_out, pT_out, a_out = s.counters("kT_done", "kT_out", "pT_out", "a_out", per=2)
    q_in, qs_ready, bias_in, stored = (nc.alloc_semaphore(f"c2_{n}") for n in ("q_in", "qs_ready", "bias_in", "stored"))
    NK = PAST + DEC_S
    room = Room(c, R2, KV)
    ck, cv = room.take(2, 2, WA), room.take(2, 3, WA)
    kT, pT = room.take(2, FA, PAST), room.take(2, 3, P)
    S, Pr = room.take(2, NK), room.take(2, NK)
    qz = c.at(WORK, HA, P)
    work = Room(c, WORK + 1024)
    aT, bias = work.take(FA, P), work.take(NK)
    qs = work.take(DEC_B, HA, DEC_S)
    nmax, rsum, rinv = work.take(2), work.take(2), work.take(2)
    with nc.Block() as block:
        @block.sync
        def _(sp):
            sp.dma_start(qz.rearrange("p h n -> p (h n)"), row(c.qz, NT - 1)).then_inc(q_in, 16)
            s.credit(sp)
            def load_keys(n):
                sp.wait_ge(*kT_done(n - 2))
                sp.dma_start(ck[:, n % 2], c.i["cache_k_a"][0, n].rearrange("(k p) h d -> p k (h d)", p=P)).then_inc(*k_in.inc(n % 2))

            def load_values(n):
                b = n % 2
                sp.wait_ge(*pv_done(n - 2))
                sp.dma_start(cv[:, b, 0:2], c.i["cache_v_a"][0, n].rearrange("(k p) h d -> p k (h d)", p=P)).then_inc(*v_in.inc(b))
                sp.dma_start(cv[0:DEC_S, b, 2], c.o["v_all"][NT - 1, n * DEC_S:(n + 1) * DEC_S, :]).then_inc(*vn_in.inc(b))

            load_keys(0)
            load_keys(1)
            for h in range(HA):
                sp.dma_start(bias[h * DEC_S:(h + 1) * DEC_S, :], bass.AP(
                    tensor=c.skew.tensor, offset=h * P * SKEW + (NKB * P - 1) - PAST, ap=[[SKEW - 1, DEC_S], [1, NK]])).then_inc(bias_in, 16)
            for n in range(DEC_B):
                if n >= 1 and n + 1 < DEC_B:
                    load_keys(n + 1)
                load_values(n)
            sp.wait_ge(*a_out(DEC_B - 1))
            sp.dma_start(row(c.aT, NT - 1), aT.rearrange("p f n -> p (f n)")).then_inc(stored, 16)
            sp.wait_ge(stored, 16)

        @block.vector
        def _(dve):
            dve.wait_ge(q_in, 16)
            nc.vector.tensor_copy(qs.rearrange("p b h x -> p h b x"), qz.rearrange("p h (b x) -> p h b x", b=DEC_B)).then_inc(qs_ready, 1)
            dve.wait_ge(bias_in, 16 * HA)

            def outputs(n):
                b = n % 2
                dve.wait_ge(*pv_done(n))
                src = ps[:, 6 + b, 0:FA * 2 * DEC_S].rearrange("p (f two x) -> p f two x", f=FA, two=2)
                for half in range(2):
                    rows = slice(64 * half, 64 * half + 64)
                    nc.vector.tensor_copy(aT[rows, :, n * DEC_S:(n + 1) * DEC_S], src[rows, :, half, :]).then_inc(*a_out.inc)

            def softmax(n):
                b = n % 2
                dve.wait_ge(*s_done(n))
                dve.wait_ge(*p_ready(n - 2))
                nc.vector.scalar_tensor_tensor(S[:, b, :], ps[:, 2 + b, 0:NK], SCALE, bias, ALU.mult, ALU.add).then_inc(*s_out.inc)
                dve.wait_ge(*s_out(n))
                nc.vector.reduce_max(nmax[:, b:b + 1], S[:, b, :], AX.X, negate=True).then_inc(*max_ready.inc)
                dve.wait_ge(*p_ready(n))
                nc.vector.reciprocal(rinv[:, b:b + 1], rsum[:, b:b + 1]).then_inc(*inv_ready.inc)
                dve.wait_ge(*inv_ready(n))
                nc.vector.tensor_scalar(Pr[:, b, :], Pr[:, b, :], rinv[:, b:b + 1], None, ALU.mult).then_inc(*pn_ready.inc)

            softmax(0)
            softmax(1)
            for n in range(DEC_B):
                outputs(n)
                if n + 2 < DEC_B:
                    softmax(n + 2)

        @block.scalar
        def _(act):
            def keys(n):
                b = n % 2
                for h in range(2):
                    act.wait_ge(*kT_done(n, h + 1))
                    act.wait_ge(*s_done(n - 2))
                    nc.scalar.activation(kT[:, b, 2 * h:2 * h + 2].rearrange("p f n -> p (f n)"), ps[:, h, :], ACT.Copy).then_inc(*kT_out.inc)

            def weights(n):
                b = n % 2
                act.wait_ge(*max_ready(n))
                act.wait_ge(*pT_done(n - 2))
                nc.scalar.activation(Pr[:, b, :], S[:, b, :], ACT.Exp, bias=nmax[:, b:b + 1], accum_out=rsum[:, b:b + 1]).then_inc(*p_ready.inc)

            keys(0)
            keys(1)
            weights(0)
            weights(1)
            for n in range(DEC_B):
                b = n % 2
                act.wait_ge(*pT_done(n))
                act.wait_ge(*pv_done(n - 2))
                nc.scalar.activation(pT[:, b, 0:2].rearrange("p k n -> p (k n)"), ps[:, 4 + b, 0:2 * P], ACT.Copy).then_inc(*pT_out.inc)
                nc.scalar.activation(pT[0:DEC_S, b, 2], ps[0:DEC_S, 4 + b, 2 * P:3 * P], ACT.Copy).then_inc(*pT_out.inc)
                if n + 2 < DEC_B:
                    keys(n + 2)
                    weights(n + 2)

        @block.tensor
        def _(pe):
            pe.wait_ge(qs_ready, 1)

            def keys(n):
                b = n % 2
                pe.wait_ge(*k_in(n, b))
                for h in range(2):
                    pe.wait_ge(*kT_out(n - 1, h + 1))
                    for f in range(2 * h, 2 * h + 2):
                        for k in range(2):
                            last = nc.tensor.transpose(ps[:, h, ((f % 2) * 2 + k) * P:((f % 2) * 2 + k + 1) * P],
                                                       ck[:, b, k, f * P:(f + 1) * P], c.ident)
                    last.then_inc(*kT_done.inc)

            def scores(n):
                b = n % 2
                pe.wait_ge(*kT_out(n))
                pe.wait_ge(*s_out(n - 2))
                for f in range(FA):
                    q = qs[:, n, 2 * f:2 * f + 2, :].rearrange("p h x -> p (h x)")
                    out = ps[32 * f:32 * f + 32, 2 + b, :]
                    nc.tensor.matmul(out[:, 0:PAST], q, kT[:, b, f, :], start=True, stop=True)
                    last = nc.tensor.matmul(out[:, PAST:NK], q, c.kT[:, f, SEQ + n * DEC_S:SEQ + (n + 1) * DEC_S], start=True, stop=True)
                last.then_inc(*s_done.inc)

            def transposed(n):
                b = n % 2
                pe.wait_ge(*pn_ready(n))
                pe.wait_ge(*pT_out(n - 2))
                for k in range(2):
                    nc.tensor.transpose(ps[:, 4 + b, k * P:(k + 1) * P], Pr[:, b, k * P:(k + 1) * P], c.ident)
                nc.tensor.transpose(ps[0:DEC_S, 4 + b, 2 * P:3 * P], Pr[:, b, PAST:NK], c.ident).then_inc(*pT_done.inc)

            def outputs(n):
                b = n % 2
                pe.wait_ge(*pT_out(n))
                pe.wait_ge(*v_in(n, b))
                pe.wait_ge(*vn_in(n, b))
                pe.wait_ge(*a_out(n - 2))
                for f in range(FA):
                    for k in range(3):
                        rows = P if k < 2 else DEC_S
                        last = nc.tensor.matmul(ps[:, 6 + b, f * 32:(f + 1) * 32], cv[0:rows, b, k, f * P:(f + 1) * P],
                                                pT[0:rows, b, k, f * 32:(f + 1) * 32], start=k == 0, stop=k == 2)
                last.then_inc(*pv_done.inc)

            keys(0)
            keys(1)
            scores(0)
            scores(1)
            for n in range(DEC_B):
                transposed(n)
                if n + 2 < DEC_B:
                    keys(n + 2)
                outputs(n)
                if n + 2 < DEC_B:
                    scores(n + 2)


NR = NG + NE
LOGITS = ARENA - NT * NR
TOP = 2
IDS = NBLK + NBLK % 2
FAR = -100.0
ROUTE_TABLES = (("before", P), ("ones", P), ("gidx", NG), ("eidx", NE), ("ebase", NE), ("ebase31", NE), ("oidx", OVER),
                ("blocks", NBLK - 1), ("block", IDS), ("slot", P), ("one", NE), ("token", NT))
ROUTE_WORDS = sum(w for _, w in ROUTE_TABLES)
TABLES = LOGITS - ROUTE_WORDS
PIECE = 2048


def expert_slot(c, b):
    off = R1 + b * 12 * 1024
    return c.at(off, KD, DE), c.at(off + 4 * 1024, KD, DE), c.at(off + 8 * 1024, KE, D)


class MergeWeights:

    def __init__(self, c):
        self.c, self.pieces = c, 7
        self.lo = c.at(R1, self.pieces, PIECE)
        self.hi = c.at(R1 + self.pieces * PIECE, self.pieces, PIECE)
        self.arrived = [c.nc.alloc_semaphore(f"merge_piece{n}_in") for n in range(self.pieces)]
        self.of_weight = ((0, 1), (2,), (3, 4), (5, 6))

    def source(self, n, half):
        i, cols = self.c.i, slice(half % 2 * BANK, half % 2 * BANK + BANK)
        if half >= 2:
            w, first = slabs(i["w_out"][0], 0, D), 3 * (half - 2)
        else:
            w, first = ((slabs(i["w_in"][0], CGA, CGT), 0), (slabs(i["w_in"][0], CGA, CGT), 0), (slabs(i["w_proj_a"][0], 0, D), 2),
                        (slabs(i["w_in"][0], CGT, CGT + D), 3), (slabs(i["w_in"][0], CGT, CGT + D), 3),
                        (slabs(i["w_proj_b"][0], 0, D), 5), (slabs(i["w_proj_b"][0], 0, D), 5))[n]
        return w[:, 4 * (n - first):4 * (n - first) + 4, cols]

    def load(self, eng, n, half):
        eng.dma_start(self.lo[:, n, :].rearrange("p (k m) -> p k m", k=4), self.source(n, half)).then_inc(self.arrived[n], 16)

    def slab(self, w, k):
        n = self.of_weight[w][k // 4]
        cols = slice(k % 4 * BANK, (k % 4 + 1) * BANK)
        return self.c.exact(self.hi[:, n, cols]), self.c.exact(self.lo[:, n, cols])


def stage_merge(c):
    nc, ps, W = c.nc, c.psum, c.merge_weights
    reuse_semaphores(c)
    s = Stage(nc, "merge")
    c.stages.append(s)
    hT_in, aT_in, bT_in = s.dmas("hT_in", "aT_in", "bT_in")
    proj_done, = s.counters("proj_done", per=4)
    gate_out, prod_out = s.counters("gate_out", "prod_out", per=2)
    m_ready, mT_done, mT_out = s.counters("m_ready", "mT_done", "mT_out")
    hi_ready, lo_ready = s.counters("hi_ready", "lo_ready", per=3)
    w_hi_ready, w_lo_ready = (nc.alloc_semaphore(f"merge_{n}") for n in ("w_hi_ready", "w_lo_ready"))
    room = Room(c, R1 + 2 * W.pieces * PIECE, IDENT)
    c.mT = room.take(NT, KD, P)
    hT, aT, bT = room.take(2, KD, P), room.take(2, FA, P), room.take(2, FB, P)
    hT_hi, aT_hi = room.take(2, KD, P), room.take(2, FA, P)
    work = Room(c, WORK, LOGITS)
    bT_hi, g, m = work.take(2, FB, P), work.take(2, BANK), work.take(BANK)
    c.after_merge = work.off
    c.rounded("merge_w", *(W.lo[:, n] for n in range(W.pieces)), *(W.hi[:, n] for n in range(W.pieces)))
    c.rounded("merge_x", hT, aT, bT, hT_hi, aT_hi, bT_hi)
    operands = ((hT, hT_hi, 1), (aT, aT_hi, 2), (hT, hT_hi, 1), (bT, bT_hi, 3))
    tensors = ((hT, hT_hi, hT_in), (aT, aT_hi, aT_in), (bT, bT_hi, bT_in))
    early, late = range(5), range(5, W.pieces)
    last = 2 * NT - 1

    def place(t, half):
        return (t % NT, t // NT) if isinstance(t, int) else (t - half * NT, half)

    def turns(eng, turn, between=None):
        turn(0, 0, 0)
        for half in range(2):
            with eng.Fori(0, PT // 2 - 1) as i:
                for b in range(2):
                    t = i * 2 + (half * NT + 1 + b)
                    turn(t, (half + 1 + b) % 2, half)
            first = half * NT + 7
            for t in range(first, first + 2 + (half == 0)):
                turn(t, t % 2, t // NT)
        if between:
            between()
        turn(last + 1, 0, 2)

    def at(t, step):
        return isinstance(t, int) and t == step

    with nc.Block() as block:
        @block.sync
        def _(sp):
            def load(t, b, half):
                if not at(t, 0):
                    sp.wait_ge(*proj_done(t - 2))
                for (dst, _, sig), src in zip(tensors, (c.hT, c.aT, c.bT)):
                    sp.dma_start(dst[:, b].rearrange("p k n -> p (k n)"), row(src, place(t, half)[0])).then_inc(*sig.inc(b))

            def turn(t, b, half):
                if isinstance(t, int) and t >= last:
                    return
                load(t + 1, 1 - b, half)
                if at(t, NT - 1):
                    for w, pieces in enumerate(W.of_weight):
                        sp.wait_ge(*proj_done(t, w + 1))
                        for n in pieces:
                            W.load(sp, n, 1)
            load(0, 0, 0)
            s.credit(sp)
            turns(sp, turn)
            for w in (0, 2):
                sp.wait_ge(*proj_done(last, w + 1))
                for n in W.of_weight[w]:
                    W.load(sp, n, 2 + w // 2)

        @block.scalar
        def _(act):
            def hi(t, b):
                for k, (raw, high, arrived) in enumerate(tensors):
                    act.wait_ge(*arrived(t, b))
                    act.wait_ge(*proj_done(t - 2))
                    nc.scalar.activation(c.exact(high[:, b]), raw[:, b], ACT.Copy).then_inc(*hi_ready.inc)

            def w_hi(pieces, half):
                for n in pieces:
                    act.wait_ge(W.arrived[n], 16 * (half + 1))
                    nc.scalar.activation(c.exact(W.hi[:, n, :]), W.lo[:, n, :], ACT.Copy).then_inc(w_hi_ready, 1)

            def turn(t, b, half):
                def gated(n):
                    act.wait_ge(*proj_done(t, 2 * n + 1))
                    act.wait_ge(*m_ready(t - 1))
                    nc.scalar.activation(g[:, n, :], ps[:, 2 * n, :], ACT.Sigmoid).then_inc(*gate_out.inc)
                if at(t, last + 1):
                    return
                gated(0)
                if at(t, 0) or at(t, NT):
                    w_hi(late, half)
                if not at(t, last):
                    hi(t + 1, 1 - b)
                if at(t, NT - 1):
                    w_hi(early[:2], 1)
                gated(1)
                if at(t, NT - 1):
                    w_hi(early[2:], 1)

            w_hi(early[:1], 0)
            hi(0, 0)
            w_hi(early[1:], 0)
            turns(act, turn)
            w_hi(W.of_weight[0], 2)

        @block.gpsimd
        def _(pool):
            def turn(t, b, half):
                if not at(t, last + 1):
                    pool.wait_ge(*prod_out(t))
                    pool.wait_ge(*mT_done(t - 1))
                    nc.gpsimd.tensor_tensor(m, g[:, 0, :], g[:, 1, :], ALU.add).then_inc(*m_ready.inc)
            turns(pool, turn)

        @block.vector
        def _(dve):
            def lo(t, b):
                for k, (raw, high, _) in enumerate(tensors):
                    dve.wait_ge(*hi_ready(t, k + 1))
                    nc.vector.tensor_tensor(c.exact(raw[:, b]), raw[:, b], c.high(high[:, b]), ALU.subtract).then_inc(*lo_ready.inc)

            def w_lo(pieces, half):
                for n in pieces:
                    dve.wait_ge(w_hi_ready, half * W.pieces + n + 1)
                    nc.vector.tensor_tensor(c.exact(W.lo[:, n, :]), W.lo[:, n, :], c.high(W.hi[:, n, :]), ALU.subtract).then_inc(w_lo_ready, 1)

            def turn(t, b, half):
                def product(n):
                    dve.wait_ge(*proj_done(t, 2 * n + 2))
                    dve.wait_ge(*gate_out(t, n + 1))
                    nc.vector.tensor_tensor(g[:, n, :], g[:, n, :], ps[:, 2 * n + 1, :], ALU.mult).then_inc(*prod_out.inc)
                if not at(t, 0):
                    dve.wait_ge(*mT_done(t - 1))
                    tile, of = place(t - 1, half)
                    kept = c.mT[:, ds(tile, 1), 4 * of:4 * of + 4, :].rearrange("p a k n -> p (a k n)")
                    nc.vector.tensor_scalar(kept, ps[:, 4, :], 1.0, None, ALU.mult).then_inc(*mT_out.inc)
                if at(t, last + 1):
                    return
                product(0)
                if at(t, 0) or at(t, NT):
                    w_lo(late, half)
                if not at(t, last):
                    lo(t + 1, 1 - b)
                if at(t, NT - 1):
                    w_lo(early[:2], 1)
                product(1)
                if at(t, NT - 1):
                    w_lo(early[2:], 1)

            w_lo(early[:1], 0)
            lo(0, 0)
            w_lo(early[1:], 0)
            turns(dve, turn, between=lambda: w_lo(W.of_weight[0], 2))
            dve.wait_ge(w_lo_ready, 2 * W.pieces + 2)

        @block.tensor
        def _(pe):
            def project(t, b, w, half):
                x, x_hi, part = operands[w]
                pe.wait_ge(*lo_ready(t, part))
                pe.wait_ge(*(prod_out if w % 2 else gate_out)(t - 1, w // 2 + 1))
                slab_count = x.shape[2]
                for k in range(slab_count):
                    if k % 4 == 0 and (at(t, 0) or at(t, NT)):
                        pe.wait_ge(w_lo_ready, half * W.pieces + W.of_weight[w][k // 4] + 1)
                    w_hi, w_lo = W.slab(w, k)
                    last_product = split_product(nc, ps[:, w, :], c.exact(x_hi[:, b, k, :]), c.exact(x[:, b, k, :]), w_hi, w_lo,
                                                 k == 0, k == slab_count - 1)
                last_product.then_inc(*proj_done.inc)

            def turn(t, b, half):
                for w in range(4):
                    if not at(t, last + 1):
                        project(t, b, w, half)
                    if w == 0 and not at(t, 0):
                        pe.wait_ge(*m_ready(t - 1))
                        pe.wait_ge(*mT_out(t - 2))
                        for k in range(4):
                            transposed = nc.tensor.transpose(ps[:, 4, k * P:(k + 1) * P], m[:, k * P:(k + 1) * P], c.ident)
                        transposed.then_inc(*mT_done.inc)
            turns(pe, turn)


def stage_d(c):
    nc, ps, W = c.nc, c.psum, c.merge_weights
    s = Stage(nc, "d")
    c.stages.append(s)
    x_in, x1_stored, xn_stored = s.dmas("x_in", "x1_stored", "xn_stored")
    wo_done, x1_ready, h2_done, h2_out = s.counters("wo_done", "x1_ready", "h2_done", "h2_out", per=2)
    hi_ready, lo_ready, ssq_ready, ms_ready, rstd_ready, xn_ready, lg_done, lg_out = s.counters(
        "hi_ready", "lo_ready", "ssq_ready", "ms_ready", "rstd_ready", "xn_ready", "lg_done", "lg_out")
    router_in, w_hi_ready, w_lo_ready = (nc.alloc_semaphore(f"d_{n}") for n in ("router_in", "w_hi_ready", "w_lo_ready"))
    room = Room(c, R1 + 2 * W.pieces * PIECE + NT * D, IDENT)
    x, x1, xn, h2, mT_hi, mT_lo = (room.take(2, D), room.take(D), room.take(D), room.take(KD, P), room.take(2, KD, P),
                                   c.at(WORK, 2, KD, P))
    c.rounded("d_merged", mT_hi, mT_lo)
    work = Room(c, c.after_merge, TABLES)
    wr, br = work.take(KD, NR), work.take(NR)
    ssq, ms, rstd = work.take(1), work.take(1), work.take(1)
    c.logits = c.at(LOGITS, NT, NR)
    c.tables, c.tables_in = c.at(TABLES, ROUTE_WORDS), nc.alloc_semaphore("route_tables_in")
    first_table = c.const_at[ROUTE_TABLES[0][0]][0]
    for k, (name, words) in enumerate(ROUTE_TABLES):
        assert c.const_at[name] == (first_table + sum(w for _, w in ROUTE_TABLES[:k]), words)
    c.expert_in = [[nc.alloc_semaphore(f"expert_{n}_in{b}") for b in range(2)] for n in ("gate", "up", "down")]

    def turns(eng, turn):
        turn(0, 0, True, False)
        with eng.Fori(0, PT // 2) as i:
            for b in range(2):
                turn(i * 2 + (1 + b), 1 - b, True, True)
        turn(NT, 1, False, True)

    with nc.Block() as block:
        @block.sync
        def _(sp):
            s.credit(sp)

            def load(t, b):
                sp.wait_ge(*x1_ready(t - 2))
                sp.dma_start(x[:, b], row(c.i["x_all"], t)).then_inc(*x_in.inc(b))

            def turn(t, b, new, old):
                if new:
                    load(t, b)
                if old:
                    sp.wait_ge(*x1_ready(t - 1))
                    sp.dma_start(row(c.x1, t - 1), x1).then_inc(*x1_stored.inc(1 - b))
                    sp.wait_ge(*xn_ready(t - 1))
                    sp.dma_start(c.xn[ds((t - 1) * P, P), :], xn).then_inc(*xn_stored.inc(1 - b))

            sp.dma_start(wr[:, :, 0:NG], slabs(c.i["w_router_group"][0], 0, NG), allow_slow_non_contiguous=True).then_inc(router_in, 16)
            sp.dma_start(wr[:, :, NG:NR], slabs(c.i["w_router_expert"][0], 0, NE)).then_inc(router_in, 16)
            sp.dma_start(br[:, 0:NG], c.i["b_router_group"].to_broadcast([P, NG])).then_inc(router_in, 16)
            sp.dma_start(br[:, NG:NR], c.i["b_router_expert"].to_broadcast([P, NE])).then_inc(router_in, 16)
            turn(0, 0, True, False)
            sp.dma_start(c.tables, c.i["consts"][:, first_table:first_table + ROUTE_WORDS]).then_inc(c.tables_in, 16)
            with sp.Fori(0, PT // 2) as i:
                for b in range(2):
                    turn(i * 2 + (1 + b), 1 - b, True, True)
            first = [(expert_slot(c, b)[n], c.i[name][0, b], c.expert_in[n][b]) for b in range(2)
                     for n, name in enumerate(("w_gate_e", "w_up_e", "w_down_e"))]
            sp.wait_ge(*wo_done(NT - 1))
            for n, (dst, src, sem) in enumerate(first):
                if n == 1:
                    turn(NT, 1, False, True)
                sp.dma_start(dst, src.rearrange("(k p) n -> p k n", p=P)).then_inc(sem, 16)
            for sig in (x1_stored, xn_stored):
                sp.wait_ge(*sig(8, 0))
                sp.wait_ge(*sig(7, 1))

        @block.scalar
        def _(act):
            def turn(t, b, new, old):
                if old:
                    act.wait_ge(*x1_ready(t - 1))
                    act.wait_ge(*xn_stored(t - 2, b))
                    act.wait_ge(*h2_done(t - 2))
                    nc.scalar.activation(xn, x1, ACT.Square, accum_out=ssq).then_inc(*ssq_ready.inc)
                    act.wait_ge(*rstd_ready(t - 1))
                    nc.scalar.activation(xn, x1, ACT.Copy, scale=rstd).then_inc(*xn_ready.inc)

            for n in range(3, 5):
                act.wait_ge(W.arrived[n], 16 * 3)
                nc.scalar.activation(c.exact(W.hi[:, n, :]), W.lo[:, n, :], ACT.Copy).then_inc(w_hi_ready, 1)
            turns(act, turn)

        @block.gpsimd
        def _(pool):
            def turn(t, b, new, old):
                if old:
                    pool.wait_ge(*ms_ready(t - 1))
                    nc.gpsimd.tensor_tensor(rstd, ms, c.half[:, 0:1], ALU.pow).then_inc(*rstd_ready.inc)
            turns(pool, turn)

        @block.vector
        def _(dve):
            def split(t, b):
                raw = c.mT[:, ds(t, 1)].rearrange("p a k n -> p (a k n)")
                high = mT_hi[:, b].rearrange("p k n -> p (k n)")
                dve.wait_ge(*wo_done(t - 2))
                nc.vector.tensor_scalar(c.exact(high), raw, 1.0, None, ALU.mult).then_inc(*hi_ready.inc)
                dve.wait_ge(*hi_ready(t))
                nc.vector.tensor_tensor(c.exact(mT_lo[:, b]).rearrange("p k n -> p (k n)"), raw, c.high(high), ALU.subtract).then_inc(*lo_ready.inc)

            def residual(t, b, h):
                cols = slice(h * BANK, (h + 1) * BANK)
                dve.wait_ge(*wo_done(t, h + 1))
                dve.wait_ge(*x_in(t, b))
                dve.wait_ge(*x1_stored(t - 1, 1 - b))
                dve.wait_ge(*xn_ready(t - 1))
                nc.vector.tensor_tensor(x1[:, cols], ps[:, h, :], x[:, b, cols], ALU.add).then_inc(*x1_ready.inc)

            def turn(t, b, new, old, ahead=True):
                if old:
                    dve.wait_ge(*ssq_ready(t - 1))
                    nc.vector.tensor_scalar(ms, ssq, 1.0 / D, EPS, ALU.mult, ALU.add).then_inc(*ms_ready.inc)
                if ahead:
                    split(t + 1, 1 - b)
                if new:
                    residual(t, b, 0)
                if old:
                    for h in range(2):
                        dve.wait_ge(*h2_done(t - 1, h + 1))
                        dve.wait_ge(*lg_done(t - 2))
                        nc.vector.tensor_tensor(h2[:, 4 * h:4 * h + 4, :], ps[:, 2 + h, :].rearrange("p (k n) -> p k n", k=4),
                                                gain(c.g_ffn, 4 * h, 4 * h + 4), ALU.mult).then_inc(*h2_out.inc)
                if new:
                    residual(t, b, 1)
                if old:
                    dve.wait_ge(*lg_done(t - 1))
                    nc.vector.tensor_tensor(c.logits[:, ds(t - 1, 1), :].rearrange("p a n -> p (a n)"), ps[:, 4, 0:NR], br, ALU.add).then_inc(*lg_out.inc)

            split(0, 0)
            for n in range(2):
                dve.wait_ge(w_hi_ready, n + 1)
                nc.vector.tensor_tensor(c.exact(W.lo[:, 3 + n, :]), W.lo[:, 3 + n, :], c.high(W.hi[:, 3 + n, :]), ALU.subtract).then_inc(w_lo_ready, 1)
            dve.wait_ge(router_in, 64)
            turn(0, 0, True, False)
            with dve.Fori(0, PT // 2 - 1) as i:
                for b in range(2):
                    turn(i * 2 + (1 + b), 1 - b, True, True)
            turn(NT - 2, 1, True, True)
            turn(NT - 1, 0, True, True, False)
            turn(NT, 1, False, True, False)

        @block.tensor
        def _(pe):
            def projected(t, b, h, first=False):
                pe.wait_ge(*lo_ready(t))
                pe.wait_ge(*x1_ready(t - 1, h + 1))
                for k in range(KD):
                    if first and h and k % 4 == 0:
                        pe.wait_ge(w_lo_ready, k // 4 + 1)
                    w_hi, w_lo = W.slab(2 * h, k)
                    last = split_product(nc, ps[:, h, :], c.exact(mT_hi[:, b, k, :]), c.exact(mT_lo[:, b, k, :]), w_hi, w_lo, k == 0, k == KD - 1)
                last.then_inc(*wo_done.inc)

            def turn(t, b, new, old):
                if new:
                    projected(t, b, 0, isinstance(t, int) and t == 0)
                if old:
                    pe.wait_ge(*xn_ready(t - 1))
                    for h in range(2):
                        pe.wait_ge(*h2_out(t - 2, h + 1))
                        for k in range(4 * h, 4 * h + 4):
                            last = nc.tensor.transpose(ps[:, 2 + h, (k % 4) * P:(k % 4 + 1) * P], xn[:, k * P:(k + 1) * P], c.ident)
                        last.then_inc(*h2_done.inc)
                if new:
                    projected(t, b, 1, isinstance(t, int) and t == 0)
                if old:
                    pe.wait_ge(*h2_out(t - 1))
                    pe.wait_ge(*lg_out(t - 2))
                    for k in range(KD):
                        last = nc.tensor.matmul(ps[:, 4, 0:NR], h2[:, k, :], wr[:, k, :], start=k == 0, stop=k == KD - 1)
                    last.then_inc(*lg_done.inc)
            pe.wait_ge(router_in, 64)
            turns(pe, turn)


def stage_e(c):
    nc, ps = c.nc, c.psum
    s = Stage(nc, "e")
    c.stages.append(s)
    step, placed = s.counters("step", "placed")
    exp_in, chosen, counted, gap_ready, gap_exp, ids_done = s.counters(
        "exp_in", "chosen", "counted", "gap_ready", "gap_exp", "ids_done")
    sel_ready = s.counter("sel_ready", 2)
    keep = Room(c, WORK, TABLES)
    c.weights = keep.take(TOP, NT)
    c.places = keep.take(TOP, NT).bitcast(I32)
    c.block_ids = keep.take(NBLK).bitcast(I32)
    c.over_expert, c.over_count = keep.take(OVER).bitcast(I32), keep.take(1).bitcast(I32)
    c.after_routing = keep.off
    room = Room(c, KV, IDENT)
    T, at = {}, 0
    for n, w in ROUTE_TABLES:
        T[n], at = c.tables[:, at:at + w], at + w
    lg, le = c.logits[:, :, 0:NG], c.logits[:, :, NG:NR]
    gmax, gmin = room.take(NT), room.take(NT)
    g4, gsel, gexp = room.take(NT, NG), room.take(NT, NG), room.take(NT, NG)
    v, t32 = room.take(NT, NE), room.take(NT, NE)
    pick = [room.take(NT, NE) for _ in range(TOP)]
    top, first = [room.take(NT) for _ in range(TOP)], room.take(NT)
    both, rank, base = room.take(NT, NE), room.take(NT, NE), room.take(NT, NE)
    pg, gap = room.take(NT), room.take(NT)
    count, extra, total, diff = room.take(NE), room.take(NE), room.take(NE), room.take(NE)
    over = Room(c, R2, KV)
    at_slot, at_block = over.take(TOP * NT, P), over.take(TOP * NT, IDS)
    grid, place = over.take(NE, 8), over.take(TOP, NT)
    grid2 = over.take(OVER, NE)
    grid3, hi, lo = over.take(TOP * NT, NBLK - 1), over.take(TOP, NT), over.take(TOP, NT)
    over_f = over.take(OVER)
    c.rounded("e_select", at_slot, at_block)

    def wide(ap, *shape):
        return ap.to_broadcast([P, *shape])

    with nc.Block() as block:
        @block.sync
        def _(sp):
            s.credit(sp)

        @block.scalar
        def _(act):
            act.wait_ge(*exp_in(0))
            nc.scalar.activation(gexp, g4, ACT.Exp).then_inc(*gap_exp.inc)
            act.wait_ge(*gap_ready(0))
            nc.scalar.activation(gap, gap, ACT.Exp).then_inc(*gap_exp.inc)

        @block.tensor
        def _(pe):
            pe.wait_ge(*chosen(0))
            rows = both.rearrange("p t e -> p (t e)")
            nc.tensor.matmul(ps[:, 0, 0:NT * NE], T["before"], rows, start=True, stop=True)
            nc.tensor.matmul(ps[:, 1, 0:NT * NE], T["ones"], rows, start=True, stop=True).then_inc(*counted.inc)
            for n in range(TOP * NT):
                if n % NT == 0:
                    pe.wait_ge(*sel_ready(0, n // NT + 1))
                last = nc.tensor.matmul(ps[:, 2, 0:IDS], c.exact(at_slot[:, n, :]), c.exact(at_block[:, n, :]), start=n == 0, stop=n == TOP * NT - 1)
            last.then_inc(*ids_done.inc)

        @block.vector
        def _(dve):
            st = Steps(dve, step)
            st.start(0)
            link, V = st.link, nc.vector
            dve.wait_ge(c.tables_in, 16)
            link(V.tensor_reduce(gmax, lg, AX.X, ALU.max))
            link(V.tensor_tensor(g4, lg, wide(gmax.unsqueeze(2), NT, NG), ALU.is_equal))
            link(V.scalar_tensor_tensor(g4, g4, FAR, wide(T["gidx"].unsqueeze(1), NT, NG), ALU.mult, ALU.add))
            link(V.tensor_reduce(gmin, g4, AX.X, ALU.min))
            link(V.tensor_tensor(gsel, g4, wide(gmin.unsqueeze(2), NT, NG), ALU.is_equal))
            V.tensor_tensor(g4, lg, wide(gmax.unsqueeze(2), NT, NG), ALU.subtract).then_inc(*exp_in.inc)
            link(V.tensor_scalar(gsel, gsel, -NEG, NEG, ALU.mult, ALU.add))
            link(V.tensor_tensor(v.rearrange("p t (g e) -> p t g e", g=NG), le.rearrange("p t (g e) -> p t g e", g=NG),
                                 wide(gsel.unsqueeze(3), NT, NG, EPG), ALU.add))
            for k in range(TOP):
                link(V.tensor_reduce(top[k], v, AX.X, ALU.max))
                link(V.tensor_tensor(t32, v, wide(top[k].unsqueeze(2), NT, NE), ALU.is_equal))
                link(V.scalar_tensor_tensor(t32, t32, FAR, wide(T["eidx"].unsqueeze(1), NT, NE), ALU.mult, ALU.add))
                link(V.tensor_reduce(first, t32, AX.X, ALU.min))
                link(V.tensor_tensor(pick[k], t32, wide(first.unsqueeze(2), NT, NE), ALU.is_equal))
                if k == 0:
                    link(V.scalar_tensor_tensor(v, pick[0], 2 * NEG, v, ALU.mult, ALU.add))
            V.tensor_tensor(both, pick[0], pick[1], ALU.add).then_inc(*chosen.inc)
            V.tensor_tensor(gap, top[1], top[0], ALU.subtract).then_inc(*gap_ready.inc)
            dve.wait_ge(*gap_exp(0))
            link(V.tensor_reduce(pg, gexp, AX.X, ALU.add))
            dve.wait_ge(*gap_exp(1))
            link(V.tensor_scalar(first, gap, 1.0, None, ALU.add))
            link(V.tensor_tensor(pg, pg, first, ALU.mult))
            link(V.reciprocal(c.weights[:, 0, :], pg))
            link(V.tensor_tensor(c.weights[:, 1, :], c.weights[:, 0, :], gap, ALU.mult))
            dve.wait_ge(*counted(0))
            seen = ps[:, 1, 0:NT * NE].rearrange("p (t e) -> p t e", t=NT)
            link(V.memset(base[:, 0, :], 0.0))
            for t in range(1, NT):
                link(V.tensor_tensor(base[:, t, :], base[:, t - 1, :], seen[:, t - 1, :], ALU.add))
            link(V.tensor_tensor(count, base[:, NT - 1, :], seen[:, NT - 1, :], ALU.add))
            link(V.tensor_tensor(rank, base, ps[:, 0, 0:NT * NE].rearrange("p (t e) -> p t e", t=NT), ALU.add))
            link(V.tensor_tensor(grid, wide(count.unsqueeze(2), NE, 8), wide(T["blocks"][:, 0:8].unsqueeze(1), NE, 8), ALU.is_gt))
            link(V.tensor_reduce(extra, grid, AX.X, ALU.add))
            link(V.tensor_tensor_scan(total, T["one"], extra, 0.0, ALU.mult, ALU.add))
            link(V.tensor_tensor(diff, total, extra, ALU.subtract))
            link(V.scalar_tensor_tensor(diff, diff, float(P), T["ebase31"], ALU.mult, ALU.add))
            link(V.scalar_tensor_tensor(t32, rank, float(P), wide(diff.unsqueeze(1), NT, NE), ALU.is_ge, ALU.mult))
            link(V.tensor_tensor(rank, rank, wide(T["ebase"].unsqueeze(1), NT, NE), ALU.add))
            link(V.tensor_tensor(rank, rank, t32, ALU.add))
            for k in range(TOP):
                link(V.tensor_tensor(t32, pick[k], rank, ALU.mult))
                link(V.tensor_reduce(place[:, k, :], t32, AX.X, ALU.add))
            flat = place.rearrange("p k t -> p (k t)")
            link(V.tensor_copy(c.places, place))
            link(V.tensor_tensor(grid3, wide(flat.unsqueeze(2), TOP * NT, NBLK - 1), wide(T["blocks"].unsqueeze(1), TOP * NT, NBLK - 1), ALU.is_ge))
            link(V.tensor_reduce(hi.rearrange("p k t -> p (k t)"), grid3, AX.X, ALU.add))
            link(V.scalar_tensor_tensor(lo, hi, -float(P), place, ALU.mult, ALU.add))
            link(V.tensor_tensor(at_block, wide(hi.rearrange("p k t -> p (k t)").unsqueeze(2), TOP * NT, IDS),
                                 wide(T["block"].unsqueeze(1), TOP * NT, IDS), ALU.is_equal))
            link(V.tensor_tensor(c.exact(at_block).rearrange("p (k t) b -> p k t b", k=TOP), at_block.rearrange("p (k t) b -> p k t b", k=TOP),
                                 wide(T["token"].unsqueeze(1).unsqueeze(3), TOP, NT, IDS), ALU.mult))
            for k in range(TOP):
                V.tensor_tensor(c.exact(at_slot[:, k * NT:(k + 1) * NT, :]), wide(lo[:, k, :].unsqueeze(2), NT, P),
                                wide(T["slot"].unsqueeze(1), NT, P), ALU.is_equal).then_inc(*sel_ready.inc)
            link(V.tensor_tensor(grid2, wide(total.unsqueeze(1), OVER, NE), wide(T["oidx"].unsqueeze(2), OVER, NE), ALU.is_le))
            link(V.tensor_reduce(over_f, grid2, AX.X, ALU.add))
            link(V.tensor_scalar(over_f, over_f, float(NE - 1), None, ALU.min))
            link(V.tensor_copy(c.over_expert, over_f))
            link(V.tensor_copy(c.over_count, total[:, NE - 1:NE]))
            dve.wait_ge(*ids_done(0))
            link(V.tensor_copy(c.block_ids, ps[:, 2, 0:NBLK]))


def stage_f(c):
    nc, ps = c.nc, c.psum
    s = Stage(nc, "f")
    c.stages.append(s)
    (g_in,), (y_stored,) = s.dmas("g_in", credits=0), s.dmas("y_stored")
    idx_ready, silu_out, hh_ready, hhT_done, hhT_hi_ready, hhT_lo_ready = s.counters(
        "idx_ready", "silu_out", "hh_ready", "hhT_done", "hhT_hi_ready", "hhT_lo_ready")
    gate_done, up_done = s.counters("gate_done", "up_done")
    xT_done, xT_out, hg_hi_ready, hg_lo_ready, down_done, y_out = s.counters(
        "xT_done", "xT_out", "hg_hi_ready", "hg_lo_ready", "down_done", "y_out", per=2)
    names = ("gate", "up", "down")
    w_hi_ready = s.counters(*(f"{n}_hi_ready" for n in names), per=2)
    w_lo_ready = s.counters(*(f"{n}_lo_ready" for n in names), per=2)
    w_used = (gate_done, up_done, down_done)
    c.ple_in = nc.alloc_semaphore("ple_in")
    room = Room(c, R2, R2 + 8 * 1024)
    xg, hg, hg_hi, y = room.take(2, D), room.take(KD, P), room.take(KD, P), room.take(2, D)
    sil, hh, hhT, hhT_hi = room.take(DE), room.take(DE), room.take(KE, P), room.take(KE, P)
    his = [c.at(R2 + (8 + 4 * n) * 1024, 2, 2048) for n in range(3)]
    c.idx = c.at(c.after_routing, 2 * TOP).bitcast(I32)
    c.w_pp = c.at(-(-(c.after_routing + 2 * TOP) // 8) * 8, KP, D)
    c.w_ple = c.at(R1, KD, D)
    c.g_final = c.at(KV + 8 * 1024, D)
    slots = [expert_slot(c, b) for b in range(2)]
    halves = [[c.at(R1 + (12 * b + 4 * n) * 1024, 2, 2048) for n in range(3)] for b in range(2)]
    his_by_slab = [his[n].rearrange("p a (k n) -> p (a k) n", n=DE if n < 2 else D) for n in range(3)]
    c.rounded("expert_w", *(x[:, n] for x in his + halves[0] + halves[1] for n in range(2)))
    c.rounded("expert_x", hg, hg_hi, hhT, hhT_hi)

    def turns(eng, turn, last=2):
        turn(0, 0, True, False, True)
        with eng.Fori(0, (NE - last) // 2) as i:
            for b in range(2):
                turn(i * 2 + (1 + b), 1 - b, True, True, True)
        for e in range(NE - last + 1, NE + 1):
            turn(e, e % 2, e < NE, True, e + 1 < NE)

    with nc.Block() as block:
        @block.sync
        def _(sp):
            s.credit(sp)

            def load(n, e, b):
                src = c.i[("w_gate_e", "w_up_e", "w_down_e")[n]]
                sp.dma_start(slots[b][n], src[0, ds(e, 1)].rearrange("a (k p) n -> p (a k) n", p=P)).then_inc(c.expert_in[n][b], 16)

            def turn(e, b, new, old, ahead):
                late = isinstance(e, int) and e >= NE - 2
                if not late:
                    sp.wait_ge(*gate_done(e))
                    load(0, e + 2, b)
                    sp.wait_ge(*up_done(e))
                    load(1, e + 2, b)
                if old:
                    sp.wait_ge(*down_done(e - 1))
                    if ahead:
                        load(2, e + 1, 1 - b)
                    if isinstance(e, int) and e == NE - 2:
                        sp.wait_ge(*up_done(e))
                        for k in range(KD):
                            sp.dma_start(c.w_ple[:, k, :], slabs(c.i["w_ple_gate"][0], 0, D)[:, k, :]).then_inc(c.ple_in, 16)
                        sp.dma_start(c.w_pp, slabs(c.i["w_ple_proj"][0], 0, D)).then_inc(c.ple_in, 16)
                        sp.dma_start(c.g_final, c.i["final_norm_g"].unsqueeze(0).to_broadcast([P, D])).then_inc(c.ple_in, 16)
                    sp.wait_ge(*y_out(e - 1))
                    sp.dma_start(c.y[ds((e - 1) * P, P), :], y[:, 1 - b, :]).then_inc(*y_stored.inc(1 - b))
            turns(sp, turn, last=4)
            sp.wait_ge(*y_stored(NE - 2, 0))
            sp.wait_ge(*y_stored(NE - 1, 1))

        @block.gpsimd
        def _(pool):
            def gather(e, b, ahead):
                pool.wait_ge(*xT_done(e - 2))
                c.hold(pool)
                nc.gpsimd.tensor_copy(c.idx[:, b:b + 1], c.block_ids[:, ds(e, 1)]).then_inc(*idx_ready.inc)
                pool.wait_ge(*idx_ready(e))
                c.hold(pool)
                nc.gpsimd.indirect_dma_start(xg[:, b, :], None, c.xn, bass.IndirectOffsetOnAxis(ap=c.idx[:, b:b + 1], axis=0)).then_inc(
                    *g_in.inc(b))
            in_pairs(pool, NE, gather, peel=2)

        @block.scalar
        def _(act):
            def w_hi(n, e, b, half):
                act.wait_ge(c.expert_in[n][b], e * 8 + (16 - 8 * b))
                act.wait_ge(*w_used[n](e - 1))
                nc.scalar.activation(c.exact(his[n][:, half, :]), halves[b][n][:, half, :], ACT.Copy).then_inc(*w_hi_ready[n].inc)

            def rows_hi(e):
                for h in range(2):
                    act.wait_ge(*xT_out(e, h + 1))
                    nc.scalar.activation(c.exact(hg_hi[:, 4 * h:4 * h + 4, :]), hg[:, 4 * h:4 * h + 4, :], ACT.Copy).then_inc(*hg_hi_ready.inc)

            def turn(e, b, new, old, ahead):
                if old:
                    w_hi(2, e - 1, 1 - b, 0)
                    w_hi(2, e - 1, 1 - b, 1)
                if new:
                    act.wait_ge(*gate_done(e))
                    act.wait_ge(*hh_ready(e - 1))
                    nc.scalar.activation(sil, ps[:, 0, :], ACT.Silu).then_inc(*silu_out.inc)
                if old:
                    act.wait_ge(*hhT_done(e - 1))
                    nc.scalar.activation(c.exact(hhT_hi), ps[:, 4, :].rearrange("p (k n) -> p k n", k=KE), ACT.Copy).then_inc(*hhT_hi_ready.inc)
                if ahead:
                    w_hi(0, e + 1, 1 - b, 0)
                    w_hi(0, e + 1, 1 - b, 1)
                    w_hi(1, e + 1, 1 - b, 0)
                    rows_hi(e + 1)
                    w_hi(1, e + 1, 1 - b, 1)
                if old:
                    for h in range(2):
                        act.wait_ge(*down_done(e - 1, h + 1))
                        act.wait_ge(*y_stored(e - 3, 1 - b))
                        nc.scalar.activation(y[:, 1 - b, h * BANK:(h + 1) * BANK], ps[:, 5 + h, :], ACT.Copy).then_inc(*y_out.inc)

            w_hi(0, 0, 0, 0)
            w_hi(0, 0, 0, 1)
            rows_hi(0)
            w_hi(1, 0, 0, 0)
            w_hi(1, 0, 0, 1)
            turns(act, turn)

        @block.vector
        def _(dve):
            def w_lo(n, e, b, half):
                dve.wait_ge(*w_hi_ready[n](e, half + 1))
                raw = halves[b][n][:, half, :]
                nc.vector.tensor_tensor(c.exact(raw), raw, c.high(his[n][:, half, :]), ALU.subtract).then_inc(*w_lo_ready[n].inc)

            def rows(e):
                for h in range(2):
                    dve.wait_ge(*xT_done(e, h + 1))
                    dve.wait_ge(*up_done(e - 1))
                    nc.vector.tensor_tensor(hg[:, 4 * h:4 * h + 4, :], ps[:, 2 + h, :].rearrange("p (k n) -> p k n", k=4),
                                            gain(c.g_ffn, 4 * h, 4 * h + 4), ALU.mult).then_inc(*xT_out.inc)

            def rows_lo(e):
                for h in range(2):
                    dve.wait_ge(*hg_hi_ready(e, h + 1))
                    raw = hg[:, 4 * h:4 * h + 4, :]
                    nc.vector.tensor_tensor(c.exact(raw), raw, c.high(hg_hi[:, 4 * h:4 * h + 4, :]), ALU.subtract).then_inc(*hg_lo_ready.inc)

            def turn(e, b, new, old, ahead):
                if old:
                    w_lo(2, e - 1, 1 - b, 0)
                    w_lo(2, e - 1, 1 - b, 1)
                    dve.wait_ge(*hhT_hi_ready(e - 1))
                    nc.vector.tensor_tensor(c.exact(hhT), ps[:, 4, :].rearrange("p (k n) -> p k n", k=KE), c.high(hhT_hi), ALU.subtract).then_inc(
                        *hhT_lo_ready.inc)
                if ahead:
                    w_lo(0, e + 1, 1 - b, 0)
                    w_lo(0, e + 1, 1 - b, 1)
                if new:
                    dve.wait_ge(*silu_out(e))
                    dve.wait_ge(*up_done(e))
                    dve.wait_ge(*hhT_done(e - 1))
                    nc.vector.tensor_tensor(hh, sil, ps[:, 1, :], ALU.mult).then_inc(*hh_ready.inc)
                if ahead:
                    rows(e + 1)
                    w_lo(1, e + 1, 1 - b, 0)
                    rows_lo(e + 1)
                    w_lo(1, e + 1, 1 - b, 1)

            w_lo(0, 0, 0, 0)
            rows(0)
            rows_lo(0)
            w_lo(0, 0, 0, 1)
            w_lo(1, 0, 0, 0)
            w_lo(1, 0, 0, 1)
            turns(dve, turn)

        @block.tensor
        def _(pe):
            def rows(e, b):
                pe.wait_ge(*g_in(e, b))
                for h in range(2):
                    pe.wait_ge(*xT_out(e - 1, h + 1))
                    for k in range(4 * h, 4 * h + 4):
                        last = nc.tensor.transpose(ps[:, 2 + h, (k % 4) * P:(k % 4 + 1) * P], xg[:, b, k * P:(k + 1) * P], c.ident)
                    last.then_inc(*xT_done.inc)

            def product(n, e, b, out, x, x_hi, cols, done):
                slab_count = x.shape[1]
                for k in range(slab_count):
                    if k % (slab_count // 2) == 0:
                        pe.wait_ge(*w_lo_ready[n](e, 2 * k // slab_count + 1))
                    last = split_product(nc, out, c.exact(x_hi[:, k, :]), c.exact(x[:, k, :]), c.exact(his_by_slab[n][:, k, cols]),
                                         c.exact(slots[b][n][:, k, cols]), k == 0, k == slab_count - 1)
                last.then_inc(*done.inc)

            def turn(e, b, new, old, ahead):
                if new:
                    pe.wait_ge(*hg_lo_ready(e))
                    pe.wait_ge(*silu_out(e - 1))
                    product(0, e, b, ps[:, 0, :], hg, hg_hi, slice(0, DE), gate_done)
                if old:
                    pe.wait_ge(*hh_ready(e - 1))
                    pe.wait_ge(*hhT_lo_ready(e - 2))
                    for k in range(KE):
                        last = nc.tensor.transpose(ps[:, 4, k * P:(k + 1) * P], hh[:, k * P:(k + 1) * P], c.ident)
                    last.then_inc(*hhT_done.inc)
                if new:
                    pe.wait_ge(*hh_ready(e - 1))
                    product(1, e, b, ps[:, 1, :], hg, hg_hi, slice(0, DE), up_done)
                if ahead:
                    rows(e + 1, 1 - b)
                if old:
                    pe.wait_ge(*hhT_lo_ready(e - 1))
                    for h in range(2):
                        pe.wait_ge(*y_out(e - 2, h + 1))
                        product(2, e - 1, 1 - b, ps[:, 5 + h, :], hhT, hhT_hi, slice(h * BANK, (h + 1) * BANK), down_done)
            rows(0, 0)
            turns(pe, turn)


def stage_g(c):
    nc, ps = c.nc, c.psum
    reuse_semaphores(c)
    names = ("idx_ready", "g_in", "w_in", "xT_done", "xT_out", "gate_done", "up_done", "silu_out", "hh_ready", "hhT_done",
             "hhT_out", "down_done", "y_out", "y_stored")
    idx_ready, g_in, w_in, xT_done, xT_out, gate_done, up_done, silu_out, hh_ready, hhT_done, hhT_out, down_done, y_out, y_stored = (
        nc.alloc_semaphore(f"g_{n}") for n in names)
    room = Room(c, R2, R2 + 8 * 1024)
    xg, hg, y = room.take(D), room.take(KD, P), room.take(D)
    sil, hh, hhT = room.take(DE), room.take(DE), room.take(KE, P)
    w = expert_slot(c, 1)

    def blocks(eng, body):
        count = eng.value_load(c.over_count[0:1, 0:1], min_val=0, max_val=OVER)
        with eng.If(count > 0):
            with eng.Fori(0, OVER) as j:
                with eng.If(count > j):
                    body(j)

    with nc.Block() as block:
        @block.sync
        def _(sp):
            def body(j):
                e = sp.value_load(c.over_expert[0:1, ds(j, 1)], min_val=0, max_val=NE - 1)
                for n, name in enumerate(("w_gate_e", "w_up_e", "w_down_e")):
                    sp.dma_start(w[n], c.i[name][0, ds(e, 1)].rearrange("a (k p) n -> p (a k) n", p=P)).then_inc(w_in, 16)
                sp.wait_ge(y_out, j * 2 + 2)
                sp.dma_start(c.y[ds((j + NE) * P, P), :], y).then_inc(y_stored, 16)
                sp.wait_ge(y_stored, j * 16 + 16)
                c.hold(sp)
            blocks(sp, body)

        @block.gpsimd
        def _(pool):
            def body(j):
                nc.gpsimd.tensor_copy(c.idx[:, 0:1], c.block_ids[:, ds(j + NE, 1)]).then_inc(idx_ready, 1)
                pool.wait_ge(idx_ready, j + 1)
                c.hold(pool)
                nc.gpsimd.indirect_dma_start(xg, None, c.xn, bass.IndirectOffsetOnAxis(ap=c.idx[:, 0:1], axis=0)).then_inc(g_in, 16)
                pool.wait_ge(y_stored, j * 16 + 16)
                c.hold(pool)
            blocks(pool, body)

        @block.scalar
        def _(act):
            def body(j):
                act.wait_ge(gate_done, j + 1)
                nc.scalar.activation(sil, ps[:, 0, :], ACT.Silu).then_inc(silu_out, 1)
                for h in range(2):
                    act.wait_ge(down_done, j * 2 + (h + 1))
                    nc.scalar.activation(y[:, h * BANK:(h + 1) * BANK], ps[:, 5 + h, :], ACT.Copy).then_inc(y_out, 1)
                act.wait_ge(y_stored, j * 16 + 16)
                c.hold(act)
            blocks(act, body)

        @block.vector
        def _(dve):
            def body(j):
                for h in range(2):
                    dve.wait_ge(xT_done, j * 2 + (h + 1))
                    nc.vector.tensor_tensor(hg[:, 4 * h:4 * h + 4, :], ps[:, 2 + h, :].rearrange("p (k n) -> p k n", k=4),
                                            gain(c.g_ffn, 4 * h, 4 * h + 4), ALU.mult).then_inc(xT_out, 1)
                dve.wait_ge(silu_out, j + 1)
                dve.wait_ge(up_done, j + 1)
                nc.vector.tensor_tensor(hh, sil, ps[:, 1, :], ALU.mult).then_inc(hh_ready, 1)
                dve.wait_ge(hhT_done, j + 1)
                nc.vector.tensor_copy(hhT.rearrange("p k n -> p (k n)"), ps[:, 4, :]).then_inc(hhT_out, 1)
                dve.wait_ge(y_stored, j * 16 + 16)
                c.hold(dve)
            blocks(dve, body)

        @block.tensor
        def _(pe):
            def body(j):
                pe.wait_ge(g_in, j * 16 + 16)
                for h in range(2):
                    for k in range(4 * h, 4 * h + 4):
                        last = nc.tensor.transpose(ps[:, 2 + h, (k % 4) * P:(k % 4 + 1) * P], xg[:, k * P:(k + 1) * P], c.ident)
                    last.then_inc(xT_done, 1)
                pe.wait_ge(xT_out, j * 2 + 2)
                pe.wait_ge(w_in, j * 48 + 48)
                for n, done in ((0, gate_done), (1, up_done)):
                    for k in range(KD):
                        last = nc.tensor.matmul(ps[:, n, :], hg[:, k, :], w[n][:, k, :], start=k == 0, stop=k == KD - 1)
                    last.then_inc(done, 1)
                pe.wait_ge(hh_ready, j + 1)
                for k in range(KE):
                    last = nc.tensor.transpose(ps[:, 4, k * P:(k + 1) * P], hh[:, k * P:(k + 1) * P], c.ident)
                last.then_inc(hhT_done, 1)
                pe.wait_ge(hhT_out, j + 1)
                for h in range(2):
                    for k in range(KE):
                        last = nc.tensor.matmul(ps[:, 5 + h, :], hhT[:, k, :], w[2][:, k, h * BANK:(h + 1) * BANK],
                                                start=k == 0, stop=k == KE - 1)
                    last.then_inc(down_done, 1)
                pe.wait_ge(y_stored, j * 16 + 16)
            blocks(pe, body)


def stage_h(c):
    nc, ps = c.nc, c.psum
    s = Stage(nc, "h")
    x_in, p_in, out_stored = s.dmas("x_in", "p_in", "out_stored")
    y1_in, y2_in = s.dmas("y1_in", "y2_in", credits=0)
    idx_ready, pT_done, f_ready = s.counters("idx_ready", "pT_done", "f_ready")
    ssq_ready, ms_ready, rstd_ready, xn_ready, x2_ready, x2a_ready = s.counters(
        "ssq_ready", "ms_ready", "rstd_ready", "xn_ready", "x2_ready", "x2a_ready")
    ssq3_ready, ms3_ready, rstd3_ready, n3_ready = s.counters("ssq3_ready", "ms3_ready", "rstd3_ready", "n3_ready")
    hT_hi_ready, hT_lo_ready = s.counters("hT_hi_ready", "hT_lo_ready", per=2)
    pT_hi_ready, pT_lo_ready = s.counters("pT_hi_ready", "pT_lo_ready")
    xT_done, xT_out, gate_done, gate_out, emb_done, e_ready, x3_ready = s.counters(
        "xT_done", "xT_out", "gate_done", "gate_out", "emb_done", "e_ready", "x3_ready", per=2)
    room = Room(c, R1 + 8 * 1024, KV + 8 * 1024)
    x, p, y1, y2 = room.take(2, D), room.take(2, DP), room.take(2, D), room.take(2, D)
    xn, hT, pT = room.take(D), room.take(2, KD, P), room.take(2, KP, P)
    hT_hi, pT_hi = room.take(2, KD, P), room.take(2, KP, P)
    w_ple_hi, w_pp_hi = room.take(KD, D), room.take(KP, D)
    pieces = [(c.w_ple[:, k:k + 2], w_ple_hi[:, k:k + 2]) for k in range(0, KD, 2)] + [(c.w_pp, w_pp_hi)]
    c.rounded("ple_w", *(x for pair in pieces for x in pair))
    c.rounded("ple_x", hT, pT, hT_hi, pT_hi)
    w_hi_ready, w_lo_ready = (nc.alloc_semaphore(f"h_{n}") for n in ("w_hi_ready", "w_lo_ready"))
    g, e, x3, out = room.take(D), room.take(D), room.take(D), room.take(2, D)
    x2 = room.take(2, D)
    x2a = room.take(D)
    ssq, ms, rstd, ssq3, ms3, rstd3 = (room.take(1) for _ in range(6))

    def turns(eng, turn, after_first=None):
        turn(0, 0, 2, False)
        if after_first:
            after_first()
        with eng.Fori(0, PT // 2 - 1) as i:
            for b in range(2):
                turn(i * 2 + (1 + b), 1 - b, 2, True)
        turn(NT - 2, 1, 2, True)
        turn(NT - 1, 0, 1, True)
        turn(NT, 1, False, True)

    with nc.Block() as block:
        @block.sync
        def _(sp):
            def load(t, b):
                first = isinstance(t, int) and t < 2
                if not first:
                    sp.wait_ge(*x2a_ready(t - 2))
                sp.dma_start(x[:, b], row(c.x1, t)).then_inc(*x_in.inc(b))
                if not first:
                    sp.wait_ge(*pT_done(t - 2))
                sp.dma_start(p[:, b], row(c.i["p_all"], t)).then_inc(*p_in.inc(b))

            load(0, 0)
            s.credit(sp)
            load(1, 1)

            def tile(t, b, ahead):
                if ahead:
                    load(t + 2, b)
                sp.wait_ge(*f_ready(t))
                sp.dma_start(row(c.o["y_all"], t), out[:, b]).then_inc(*out_stored.inc(b))
            in_pairs(sp, NT, tile, peel=3)
            sp.wait_ge(*out_stored(NT - 1, 0))
            sp.wait_ge(*out_stored(NT - 2, 1))

        @block.gpsimd
        def _(pool):
            def gather(t, b):
                pool.wait_ge(*x2_ready(t - 2))
                c.hold(pool)
                nc.gpsimd.tensor_copy(c.idx[:, 2 * b:2 * b + 2], c.places[:, :, ds(t, 1)].rearrange("p k a -> p (k a)")).then_inc(*idx_ready.inc)
                pool.wait_ge(*idx_ready(t))
                c.hold(pool)
                for k, (dst, sig) in enumerate(((y1, y1_in), (y2, y2_in))):
                    nc.gpsimd.indirect_dma_start(dst[:, b, :], None, c.y, bass.IndirectOffsetOnAxis(
                        ap=c.idx[:, 2 * b + k:2 * b + k + 1], axis=0)).then_inc(*sig.inc(b))

            def root(m, ms_, rstd_, ready, t):
                pool.wait_ge(*m(t))
                nc.gpsimd.tensor_tensor(rstd_, ms_, c.half[:, 0:1], ALU.pow).then_inc(*ready.inc)

            def turn(t, b, new, old):
                if new == 2:
                    gather(t + 1, 1 - b)
                if new:
                    root(ms_ready, ms, rstd, rstd_ready, t)
                if old:
                    root(ms3_ready, ms3, rstd3, rstd3_ready, t - 1)
                    pool.wait_ge(*n3_ready(t - 1))
                    pool.wait_ge(*out_stored(t - 3, 1 - b))
                    nc.gpsimd.tensor_tensor(out[:, 1 - b], x3, c.g_final, ALU.mult).then_inc(*f_ready.inc)
            gather(0, 0)
            pool.wait_ge(c.ple_in, 16 * (KD + 2))
            turns(pool, turn)

        @block.vector
        def _(dve):
            def combined(t, b):
                w = c.weights
                dve.wait_ge(*x_in(t, b))
                dve.wait_ge(*y1_in(t, b))
                nc.vector.scalar_tensor_tensor(x2a, y1[:, b], w[:, 0, ds(t, 1)], x[:, b], ALU.mult, ALU.add).then_inc(*x2a_ready.inc)
                dve.wait_ge(*x2a_ready(t))
                dve.wait_ge(*y2_in(t, b))
                dve.wait_ge(*x3_ready(t - 2))
                nc.vector.scalar_tensor_tensor(x2[:, b], y2[:, b], w[:, 1, ds(t, 1)], x2a, ALU.mult, ALU.add).then_inc(*x2_ready.inc)
                dve.wait_ge(*ssq_ready(t))
                nc.vector.tensor_scalar(ms, ssq, 1.0 / D, EPS, ALU.mult, ALU.add).then_inc(*ms_ready.inc)

            def transposed(t, b):
                for h in range(2):
                    dve.wait_ge(*xT_done(t, h + 1))
                    nc.vector.tensor_tensor(hT[:, b, 4 * h:4 * h + 4, :], ps[:, h, :].rearrange("p (k n) -> p k n", k=4),
                                            gain(c.g_ple, 4 * h, 4 * h + 4), ALU.mult).then_inc(*xT_out.inc)
                for h in range(2):
                    dve.wait_ge(*hT_hi_ready(t, h + 1))
                    raw = hT[:, b, 4 * h:4 * h + 4, :]
                    nc.vector.tensor_tensor(c.exact(raw), raw, c.high(hT_hi[:, b, 4 * h:4 * h + 4, :]), ALU.subtract).then_inc(*hT_lo_ready.inc)
                dve.wait_ge(*pT_hi_ready(t))
                nc.vector.tensor_tensor(c.exact(pT[:, b]), ps[:, 2, 0:KP * P].rearrange("p (k n) -> p k n", k=KP), c.high(pT_hi[:, b]),
                                        ALU.subtract).then_inc(*pT_lo_ready.inc)

            def w_lo(ns):
                for n in ns:
                    raw, high = pieces[n]
                    dve.wait_ge(w_hi_ready, n + 1)
                    nc.vector.tensor_tensor(c.exact(raw), raw, c.high(high), ALU.subtract).then_inc(w_lo_ready, 1)

            def embedded(r, b, h):
                cols = slice(h * BANK, (h + 1) * BANK)
                dve.wait_ge(*emb_done(r, h + 1))
                dve.wait_ge(*gate_out(r, h + 1))
                nc.vector.tensor_tensor(e[:, cols], g[:, cols], ps[:, 5 + h, :], ALU.mult).then_inc(*e_ready.inc)
                dve.wait_ge(*e_ready(r, h + 1))
                dve.wait_ge(*f_ready(r - 1))
                nc.vector.tensor_tensor(x3[:, cols], e[:, cols], x2[:, b, cols], ALU.add).then_inc(*x3_ready.inc)

            def turn(t, b, new, old):
                if new:
                    combined(t, b)
                if not old:
                    w_lo(range(3, len(pieces)))
                if old:
                    embedded(t - 1, 1 - b, 0)
                if new:
                    dve.wait_ge(*gate_done(t - 2))
                    dve.wait_ge(*emb_done(t - 2))
                    transposed(t, b)
                if old:
                    embedded(t - 1, 1 - b, 1)
                    dve.wait_ge(*ssq3_ready(t - 1))
                    nc.vector.tensor_scalar(ms3, ssq3, 1.0 / D, EPS, ALU.mult, ALU.add).then_inc(*ms3_ready.inc)
            w_lo(range(3))
            turns(dve, turn)

        @block.scalar
        def _(act):
            def turn(t, b, new, old):
                if new:
                    act.wait_ge(*x2_ready(t))
                    act.wait_ge(*xT_done(t - 1))
                    nc.scalar.activation(xn, x2[:, b], ACT.Square, accum_out=ssq).then_inc(*ssq_ready.inc)
                    act.wait_ge(*rstd_ready(t))
                    nc.scalar.activation(xn, x2[:, b], ACT.Copy, scale=rstd).then_inc(*xn_ready.inc)
                for h in range(2):
                    if old:
                        cols = slice(h * BANK, (h + 1) * BANK)
                        act.wait_ge(*gate_done(t - 1, h + 1))
                        act.wait_ge(*e_ready(t - 2))
                        nc.scalar.activation(g[:, cols], ps[:, 3 + h, :], ACT.Sigmoid).then_inc(*gate_out.inc)
                if new:
                    act.wait_ge(*gate_done(t - 2))
                    act.wait_ge(*emb_done(t - 2))
                    for h in range(2):
                        act.wait_ge(*xT_out(t, h + 1))
                        part = slice(4 * h, 4 * h + 4)
                        nc.scalar.activation(c.exact(hT_hi[:, b, part]), hT[:, b, part], ACT.Copy).then_inc(*hT_hi_ready.inc)
                    act.wait_ge(*pT_done(t))
                    nc.scalar.activation(c.exact(pT_hi[:, b]), ps[:, 2, 0:KP * P].rearrange("p (k n) -> p k n", k=KP), ACT.Copy).then_inc(
                        *pT_hi_ready.inc)
                if old:
                    act.wait_ge(*x3_ready(t - 1))
                    nc.scalar.activation(g, x3, ACT.Square, accum_out=ssq3).then_inc(*ssq3_ready.inc)
                    act.wait_ge(*rstd3_ready(t - 1))
                    nc.scalar.activation(x3, x3, ACT.Copy, scale=rstd3).then_inc(*n3_ready.inc)
            def w_hi(ns):
                for n in ns:
                    raw, high = pieces[n]
                    nc.scalar.activation(c.exact(high), raw, ACT.Copy).then_inc(w_hi_ready, 1)

            act.wait_ge(c.ple_in, 16 * (KD + 2))
            w_hi(range(len(pieces)))
            turns(act, turn)

        @block.tensor
        def _(pe):
            def gate(r, b, h):
                if h == 0:
                    pe.wait_ge(*hT_lo_ready(r))
                pe.wait_ge(*gate_out(r - 1, h + 1))
                cols = slice(h * BANK, (h + 1) * BANK)
                for k in range(KD):
                    last = split_product(nc, ps[:, 3 + h, :], c.exact(hT_hi[:, b, k, :]), c.exact(hT[:, b, k, :]),
                                         c.exact(w_ple_hi[:, k, cols]), c.exact(c.w_ple[:, k, cols]), k == 0, k == KD - 1)
                last.then_inc(*gate_done.inc)

            def embed(r, b, h):
                if h == 0:
                    pe.wait_ge(*pT_lo_ready(r))
                pe.wait_ge(*e_ready(r - 1, h + 1))
                cols = slice(h * BANK, (h + 1) * BANK)
                for k in range(KP):
                    last = split_product(nc, ps[:, 5 + h, :], c.exact(pT_hi[:, b, k, :]), c.exact(pT[:, b, k, :]),
                                         c.exact(w_pp_hi[:, k, cols]), c.exact(c.w_pp[:, k, cols]), k == 0, k == KP - 1)
                last.then_inc(*emb_done.inc)

            def transposes(t, b):
                pe.wait_ge(*xn_ready(t))
                for h in range(2):
                    pe.wait_ge(*xT_out(t - 1, h + 1))
                    for k in range(4 * h, 4 * h + 4):
                        last = nc.tensor.transpose(ps[:, h, (k % 4) * P:(k % 4 + 1) * P], xn[:, k * P:(k + 1) * P], c.ident)
                    last.then_inc(*xT_done.inc)
                pe.wait_ge(*p_in(t, b))
                pe.wait_ge(*pT_lo_ready(t - 1))
                for k in range(KP):
                    last = nc.tensor.transpose(ps[:, 2, k * P:(k + 1) * P], p[:, b, k * P:(k + 1) * P], c.ident)
                last.then_inc(*pT_done.inc)

            def turn(t, b, new, old):
                if old:
                    gate(t - 1, 1 - b, 0)
                    embed(t - 1, 1 - b, 0)
                    gate(t - 1, 1 - b, 1)
                if new:
                    transposes(t, b)
                if old:
                    embed(t - 1, 1 - b, 1)
            pe.wait_ge(c.ple_in, 16 * (KD + 2))
            turns(pe, turn, lambda: pe.wait_ge(w_lo_ready, len(pieces)))


def build(nc, ins, outs, const_at, decay_tile, decay_sample):
    c = Core(nc, ins, outs, const_at, decay_tile, decay_sample)
    stage_a(c)
    stage_b(c)
    stage_b2(c)
    stage_c(c)
    stage_c2(c)
    stage_merge(c)
    stage_d(c)
    stage_e(c)
    stage_f(c)
    stage_g(c)
    stage_h(c)


INPUTS = ("cache_k_a", "cache_v_a", "state_ret", "norm_mix_g", "w_in", "rel_bias", "ret_norm_g", "w_proj_a",
          "w_proj_b", "w_out", "norm_ffn_g", "w_router_group", "b_router_group", "w_router_expert",
          "b_router_expert", "w_gate_e", "w_up_e", "w_down_e", "norm_ple_g", "w_ple_gate", "w_ple_proj",
          "final_norm_g")
OUTPUTS = {"y_all": (NT, P, D), "k_all": (NT, P, WA), "v_all": (NT, P, WA), "state_p": (HB, DK, DV),
           "state_s": (DEC_B, HB, DK, DV)}


def kernel(**inputs):
    import numpy as np
    import concourse.bacc as bacc
    from concourse.bass_utils import run_bass_kernel_spmd

    nc = bacc.Bacc("TRN2", target_bir_lowering=False, num_devices=1)
    consts, const_at, rot, decay_tile, decay_sample = shape_constants()
    arrays = {name: np.ascontiguousarray(inputs[name]) for name in INPUTS}
    tiles = lambda p, s: np.concatenate([np.asarray(p).reshape(PT, P, -1), np.asarray(s).reshape(1, P, -1)])
    arrays["x_all"] = tiles(inputs["x_prompt"], inputs["x_sample"])
    arrays["p_all"] = tiles(inputs["p_prompt"], inputs["p_sample"])
    arrays["rel_reversed"] = np.ascontiguousarray(np.asarray(inputs["rel_bias"])[0, :, ::-1])
    arrays["consts"], arrays["rot"] = consts, rot
    ins = {n: nc.dram_tensor(n, a.shape, mybir.dt.from_np(a.dtype), kind="ExternalInput").ap() for n, a in arrays.items()}
    outs = {n: nc.dram_tensor(n, shape, F32, kind="ExternalOutput").ap() for n, shape in OUTPUTS.items()}
    build(nc, ins, outs, const_at, decay_tile, decay_sample)
    r = run_bass_kernel_spmd(nc, [arrays], core_ids=[0])
    y, k, v, sp, ss = (np.asarray(r.results[0][n]) for n in OUTPUTS)
    band = PT - BAND // P
    return (y[:PT].reshape(1, SEQ, D), y[PT].reshape(DEC_B, DEC_S, D),
            k[band:PT].reshape(1, 1, BAND, HA, HDA), v[band:PT].reshape(1, 1, BAND, HA, HDA),
            sp.reshape(1, 1, HB, DK, DV),
            k[PT].reshape(1, DEC_B, DEC_S, HA, HDA), v[PT].reshape(1, DEC_B, DEC_S, HA, HDA),
            ss.reshape(1, DEC_B, HB, DK, DV))
```
